# Optimizing a Trainium2 kernel written in Bass

```python
import jax, jax.numpy as jnp
from jax import lax
import numpy as np

D_MODEL = 1024
BATCH = 1
SEQ = 256
DEPTH = 1

HEAD_DIM = 64
NSA_HEADS = 8
NSA_KV_GROUPS = 2
NSA_HPG = NSA_HEADS // NSA_KV_GROUPS
NSA_WIDTH = NSA_HEADS * HEAD_DIM
NSA_KV_COLS = NSA_KV_GROUPS * HEAD_DIM
FOX_HEADS = 8
FOX_WIDTH = FOX_HEADS * HEAD_DIM
CMP_BLOCK = 32
CMP_STRIDE = 16
CMP_HIDDEN = 256
SEL_BLOCK = 64
SEL_TOPN = 16
SEL_Q_BLOCK = 32
WINDOW = 512
Q_BLOCK = 128
N_EXPERTS = 32
TOP_K = 4
D_FF = D_MODEL
SWIGLU_LIMIT = 7.0
SWIGLU_ALPHA = 1.702
RMS_EPS = 1e-6
NEG_INF = -1e30
FORCED_SCORE = 1e9
S1 = NSA_WIDTH
S2 = S1 + 6 * NSA_KV_COLS
S3 = S2 + 3 * NSA_HEADS
S4 = S3 + 3 * FOX_WIDTH
S5 = S4 + FOX_HEADS
D_IN = S5 + 2 * D_MODEL

kernel_name = 'hybrid_nsa_fox_moe_block'

def rms_norm(x, g):
    xf = x.astype(jnp.float32)
    y = xf * lax.rsqrt(jnp.mean(xf * xf, axis=-1, keepdims=True) + RMS_EPS)
    return (y * g.astype(jnp.float32)).astype(x.dtype)

def alibi_slopes(n):
    return 2.0 ** (-8.0 * jnp.arange(1, n + 1, dtype=jnp.float32) / n)

def masked_softmax(s, mask):
    p = jax.nn.softmax(jnp.where(mask, s, NEG_INF), axis=-1)
    return jnp.where(mask, p, 0.0)

def compress(kv, pos, w1, b1, w2, b2):
    B, T, G, Dh = kv.shape
    n_cmp = (T - CMP_BLOCK) // CMP_STRIDE + 1
    idx = CMP_STRIDE * jnp.arange(n_cmp)[:, None] + jnp.arange(CMP_BLOCK)[None, :]
    blk = kv[:, idx] + pos[None, None, :, None, :]
    blk = blk.transpose(0, 1, 3, 2, 4).reshape(B, n_cmp, G, CMP_BLOCK * Dh)
    hid = jax.nn.gelu(blk @ w1 + b1)
    return hid @ w2 + b2

def nsa_mixer(q, k_c, v_c, k_s, v_s, k_w, v_w, gates):
    B, T = q.shape[:2]
    G, HPG, Dh = NSA_KV_GROUPS, NSA_HPG, HEAD_DIM
    scale = Dh ** -0.5
    qg = q.reshape(B, T, G, HPG, Dh)
    slopes = alibi_slopes(NSA_HEADS).reshape(G, HPG)
    pos = jnp.arange(T)

    n_cmp = k_c.shape[1]
    c_start = CMP_STRIDE * jnp.arange(n_cmp)
    c_end = c_start + CMP_BLOCK - 1
    dist_c = pos[:, None] - c_end[None, :]
    mask_c = dist_c >= 0
    s_c = jnp.einsum('btghd,bcgd->bghtc', qg, k_c).astype(jnp.float32) * scale \
        - slopes[:, :, None, None] * jnp.abs(dist_c)
    p_c = masked_softmax(s_c, mask_c)
    o_c = jnp.einsum('bghtc,bcgd->btghd', p_c.astype(v_c.dtype), v_c)

    n_sel = T // SEL_BLOCK
    top_n = min(SEL_TOPN, n_sel)
    j = jnp.arange(n_sel)
    lo = c_start // SEL_BLOCK
    hi = c_end // SEL_BLOCK
    overlap = ((j[None, :] == lo[:, None]) | (j[None, :] == hi[:, None])).astype(jnp.float32)
    imp = jnp.einsum('bghtc,cj->bgtj', p_c, overlap)
    t_blk = pos // SEL_BLOCK
    valid = j[None, :] <= t_blk[:, None]
    forced = (j[None, :] == 0) | (j[None, :] == t_blk[:, None]) | (j[None, :] == t_blk[:, None] - 1)
    imp = jnp.where(forced & valid, FORCED_SCORE, imp)
    imp = jnp.where(valid, imp, -1.0)
    _, sel_idx = lax.top_k(imp, top_n)

    k_sb = k_s.reshape(B, n_sel, SEL_BLOCK, G, Dh).transpose(0, 3, 1, 2, 4)
    v_sb = v_s.reshape(B, n_sel, SEL_BLOCK, G, Dh).transpose(0, 3, 1, 2, 4)
    nqs = T // SEL_Q_BLOCK
    q_sblocks = qg.reshape(B, nqs, SEL_Q_BLOCK, G, HPG, Dh).transpose(1, 0, 3, 2, 4, 5)
    idx_blocks = sel_idx.reshape(B, G, nqs, SEL_Q_BLOCK, top_n).transpose(2, 0, 1, 3, 4)
    b_ar = jnp.arange(B)[:, None, None, None]
    g_ar = jnp.arange(G)[None, :, None, None]
    n_keys = top_n * SEL_BLOCK

    def sel_block(args):
        i, q_b, idx_b = args
        kb = k_sb[b_ar, g_ar, idx_b].reshape(B, G, SEL_Q_BLOCK, n_keys, Dh)
        vb = v_sb[b_ar, g_ar, idx_b].reshape(B, G, SEL_Q_BLOCK, n_keys, Dh)
        t = i * SEL_Q_BLOCK + jnp.arange(SEL_Q_BLOCK)
        s_pos = (idx_b[..., None] * SEL_BLOCK + jnp.arange(SEL_BLOCK)).reshape(B, G, SEL_Q_BLOCK, n_keys)
        dist = t[None, None, :, None] - s_pos
        s = jnp.einsum('bgqhd,bgqkd->bghqk', q_b, kb).astype(jnp.float32) * scale \
            - slopes[None, :, :, None, None] * jnp.abs(dist)[:, :, None]
        p = masked_softmax(s, (dist >= 0)[:, :, None])
        return jnp.einsum('bghqk,bgqkd->bgqhd', p.astype(vb.dtype), vb)

    o_s = lax.map(sel_block, (jnp.arange(nqs), q_sblocks, idx_blocks))
    o_s = o_s.transpose(1, 0, 3, 2, 4, 5).reshape(B, T, G, HPG, Dh)

    nwb = T // Q_BLOCK
    span = WINDOW + Q_BLOCK
    k_pad = jnp.pad(k_w, ((0, 0), (WINDOW, 0), (0, 0), (0, 0)))
    v_pad = jnp.pad(v_w, ((0, 0), (WINDOW, 0), (0, 0), (0, 0)))
    q_wblocks = qg.reshape(B, nwb, Q_BLOCK, G, HPG, Dh).transpose(1, 0, 3, 2, 4, 5)

    def win_block(args):
        i, q_b = args
        start = i * Q_BLOCK
        kb = lax.dynamic_slice_in_dim(k_pad, start, span, axis=1)
        vb = lax.dynamic_slice_in_dim(v_pad, start, span, axis=1)
        t = start + jnp.arange(Q_BLOCK)
        s_pos = start - WINDOW + jnp.arange(span)
        dist = t[:, None] - s_pos[None, :]
        mask = (dist >= 0) & (dist < WINDOW) & (s_pos[None, :] >= 0)
        s = jnp.einsum('bgqhd,bkgd->bghqk', q_b, kb).astype(jnp.float32) * scale \
            - slopes[:, :, None, None] * jnp.abs(dist)
        p = masked_softmax(s, mask)
        return jnp.einsum('bghqk,bkgd->bgqhd', p.astype(vb.dtype), vb)

    o_w = lax.map(win_block, (jnp.arange(nwb), q_wblocks))
    o_w = o_w.transpose(1, 0, 3, 2, 4, 5).reshape(B, T, G, HPG, Dh)

    gt = gates.reshape(B, T, 3, G, HPG, 1)
    o = gt[:, :, 0] * o_c + gt[:, :, 1] * o_s + gt[:, :, 2] * o_w
    return o.reshape(B, T, NSA_WIDTH)

def fox_mixer(q, k, v, f_logit, b_forget):
    B, T, H, Dh = q.shape
    scale = Dh ** -0.5
    log_f = jax.nn.log_sigmoid((f_logit + b_forget).astype(jnp.float32))
    c_t = jnp.cumsum(log_f, axis=1).transpose(0, 2, 1)
    nqb = T // Q_BLOCK
    q_blocks = q.reshape(B, nqb, Q_BLOCK, H, Dh).transpose(1, 0, 2, 3, 4)
    c_blocks = c_t.reshape(B, H, nqb, Q_BLOCK).transpose(2, 0, 1, 3)
    s_pos = jnp.arange(T)

    def fox_block(args):
        i, q_b, c_b = args
        t = i * Q_BLOCK + jnp.arange(Q_BLOCK)
        mask = s_pos[None, :] <= t[:, None]
        s = jnp.einsum('bqhd,bkhd->bhqk', q_b, k).astype(jnp.float32) * scale \
            + (c_b[..., None] - c_t[:, :, None, :])
        p = masked_softmax(s, mask)
        return jnp.einsum('bhqk,bkhd->bqhd', p.astype(v.dtype), v)

    o = lax.map(fox_block, (jnp.arange(nqb), q_blocks, c_blocks))
    return o.transpose(1, 0, 2, 3, 4).reshape(B, T, H * Dh)

def moe_ffn(h, w_router, b_router, w_e_gate, b_e_gate, w_e_up, b_e_up, w_e_down, b_e_down):
    B, T, D = h.shape
    xt = h.reshape(B * T, D)
    logits = (xt @ w_router + b_router).astype(jnp.float32)
    top_val, top_idx = lax.top_k(logits, TOP_K)
    top_w = jax.nn.softmax(top_val, axis=-1)
    combine = jnp.sum(jax.nn.one_hot(top_idx, N_EXPERTS, dtype=jnp.float32) * top_w[..., None], axis=1)

    def expert_step(acc, args):
        wg, bg, wu, bu, wd, bd, cw = args
        g = jnp.minimum(xt @ wg + bg, SWIGLU_LIMIT)
        u = jnp.clip(xt @ wu + bu, -SWIGLU_LIMIT, SWIGLU_LIMIT)
        y = ((u + 1.0) * g * jax.nn.sigmoid(SWIGLU_ALPHA * g)) @ wd + bd
        return acc + cw[:, None].astype(y.dtype) * y, None

    acc, _ = lax.scan(expert_step, jnp.zeros_like(xt),
                      (w_e_gate, b_e_gate, w_e_up, b_e_up, w_e_down, b_e_down, combine.T))
    return acc.reshape(B, T, D)

def hybrid_layer(x, g_attn, w_in, qn_nsa, kn_cmp, kn_sel, kn_win,
                 pos_cmp_k, w_ck1, b_ck1, w_ck2, b_ck2,
                 pos_cmp_v, w_cv1, b_cv1, w_cv2, b_cv2,
                 b_nsa_gate, qn_fox, kn_fox, b_forget,
                 w_up_nsa, w_up_fox, b_merge, w_out, g_mlp,
                 w_router, b_router, w_e_gate, b_e_gate, w_e_up, b_e_up, w_e_down, b_e_down):
    B, T, _ = x.shape
    h = rms_norm(x, g_attn)
    proj = h @ w_in
    q_n, kv_n, gate_n, qkv_f, f_logit, merge_logit = jnp.split(proj, [S1, S2, S3, S4, S5], axis=-1)

    q_n = rms_norm(q_n.reshape(B, T, NSA_HEADS, HEAD_DIM), qn_nsa)
    kv_n = kv_n.reshape(B, T, 6, NSA_KV_GROUPS, HEAD_DIM)
    k_c = rms_norm(compress(kv_n[:, :, 0], pos_cmp_k, w_ck1, b_ck1, w_ck2, b_ck2), kn_cmp)
    v_c = compress(kv_n[:, :, 1], pos_cmp_v, w_cv1, b_cv1, w_cv2, b_cv2)
    k_s = rms_norm(kv_n[:, :, 2], kn_sel)
    k_w = rms_norm(kv_n[:, :, 4], kn_win)
    nsa_gates = jax.nn.sigmoid(gate_n + b_nsa_gate)
    o_nsa = nsa_mixer(q_n, k_c, v_c, k_s, kv_n[:, :, 3], k_w, kv_n[:, :, 5], nsa_gates)

    qkv_f = qkv_f.reshape(B, T, 3, FOX_HEADS, HEAD_DIM)
    o_fox = fox_mixer(rms_norm(qkv_f[:, :, 0], qn_fox), rms_norm(qkv_f[:, :, 1], kn_fox),
                      qkv_f[:, :, 2], f_logit, b_forget)

    merge = jax.nn.sigmoid(merge_logit + b_merge).reshape(B, T, 2, D_MODEL)
    y = merge[:, :, 0] * (o_nsa @ w_up_nsa) + merge[:, :, 1] * (o_fox @ w_up_fox)
    x = x + y @ w_out

    x = x + moe_ffn(rms_norm(x, g_mlp), w_router, b_router, w_e_gate, b_e_gate,
                    w_e_up, b_e_up, w_e_down, b_e_down)
    return x

def setup_inputs(seed: int = 0) -> dict:
    key = jax.random.key(seed)
    ks = iter(jax.random.split(key, 40))

    def nrm(shape, scale):
        return scale * jax.random.normal(next(ks), (DEPTH,) + shape, dtype=jnp.float32)

    def gain(n):
        return 1.0 + nrm((n,), 0.02)

    x = jax.random.normal(next(ks), (BATCH, SEQ, D_MODEL), dtype=jnp.float32)
    cmp_in = CMP_BLOCK * HEAD_DIM
    return {
        'x': x,
        'g_attn': gain(D_MODEL),
        'w_in': nrm((D_MODEL, D_IN), D_MODEL ** -0.5),
        'qn_nsa': gain(HEAD_DIM),
        'kn_cmp': gain(HEAD_DIM),
        'kn_sel': gain(HEAD_DIM),
        'kn_win': gain(HEAD_DIM),
        'pos_cmp_k': nrm((CMP_BLOCK, HEAD_DIM), 0.1),
        'w_ck1': nrm((cmp_in, CMP_HIDDEN), cmp_in ** -0.5),
        'b_ck1': nrm((CMP_HIDDEN,), 0.02),
        'w_ck2': nrm((CMP_HIDDEN, HEAD_DIM), CMP_HIDDEN ** -0.5),
        'b_ck2': nrm((HEAD_DIM,), 0.02),
        'pos_cmp_v': nrm((CMP_BLOCK, HEAD_DIM), 0.1),
        'w_cv1': nrm((cmp_in, CMP_HIDDEN), cmp_in ** -0.5),
        'b_cv1': nrm((CMP_HIDDEN,), 0.02),
        'w_cv2': nrm((CMP_HIDDEN, HEAD_DIM), CMP_HIDDEN ** -0.5),
        'b_cv2': nrm((HEAD_DIM,), 0.02),
        'b_nsa_gate': nrm((3 * NSA_HEADS,), 0.1),
        'qn_fox': gain(HEAD_DIM),
        'kn_fox': gain(HEAD_DIM),
        'b_forget': 3.0 + nrm((FOX_HEADS,), 0.5),
        'w_up_nsa': nrm((NSA_WIDTH, D_MODEL), NSA_WIDTH ** -0.5),
        'w_up_fox': nrm((FOX_WIDTH, D_MODEL), FOX_WIDTH ** -0.5),
        'b_merge': nrm((2 * D_MODEL,), 0.1),
        'w_out': nrm((D_MODEL, D_MODEL), D_MODEL ** -0.5),
        'g_mlp': gain(D_MODEL),
        'w_router': nrm((D_MODEL, N_EXPERTS), D_MODEL ** -0.5),
        'b_router': nrm((N_EXPERTS,), 0.01),
        'w_e_gate': nrm((N_EXPERTS, D_MODEL, D_FF), D_MODEL ** -0.5),
        'b_e_gate': nrm((N_EXPERTS, D_FF), 0.02),
        'w_e_up': nrm((N_EXPERTS, D_MODEL, D_FF), D_MODEL ** -0.5),
        'b_e_up': nrm((N_EXPERTS, D_FF), 0.02),
        'w_e_down': nrm((N_EXPERTS, D_FF, D_MODEL), D_FF ** -0.5),
        'b_e_down': nrm((N_EXPERTS, D_MODEL), 0.02),
    }

def reference(x, g_attn, w_in, qn_nsa, kn_cmp, kn_sel, kn_win,
              pos_cmp_k, w_ck1, b_ck1, w_ck2, b_ck2,
              pos_cmp_v, w_cv1, b_cv1, w_cv2, b_cv2,
              b_nsa_gate, qn_fox, kn_fox, b_forget,
              w_up_nsa, w_up_fox, b_merge, w_out, g_mlp,
              w_router, b_router, w_e_gate, b_e_gate, w_e_up, b_e_up, w_e_down, b_e_down):
    for l in range(DEPTH):
        x = hybrid_layer(x, g_attn[l], w_in[l], qn_nsa[l], kn_cmp[l], kn_sel[l], kn_win[l],
                         pos_cmp_k[l], w_ck1[l], b_ck1[l], w_ck2[l], b_ck2[l],
                         pos_cmp_v[l], w_cv1[l], b_cv1[l], w_cv2[l], b_cv2[l],
                         b_nsa_gate[l], qn_fox[l], kn_fox[l], b_forget[l],
                         w_up_nsa[l], w_up_fox[l], b_merge[l], w_out[l], g_mlp[l],
                         w_router[l], b_router[l], w_e_gate[l], b_e_gate[l], w_e_up[l], b_e_up[l],
                         w_e_down[l], b_e_down[l])
    return x


_drawn_inputs = setup_inputs


def setup_inputs(seed=0):
    import zlib

    import numpy as np

    out = dict(_drawn_inputs(seed))
    spreads = {}
    factors = {'qn_nsa': 2.913,
     'kn_cmp': 7.623,
     'kn_sel': 8.0,
     'kn_win': 8.0,
     'pos_cmp_k': 3.123,
     'b_ck1': 8.0,
     'b_ck2': 8.0,
     'b_cv1': 4.861,
     'b_cv2': 2.867,
     'qn_fox': 8.0,
     'kn_fox': 2.852,
     'b_e_gate': 6.345,
     'b_e_up': 8.0,
     'b_e_down': 6.006}
    for name, (base, spread) in spreads.items():
        noise = np.random.default_rng([zlib.crc32(name.encode()), seed]).standard_normal(out[name].shape)
        drawn = base * np.exp(spread * noise) if base else spread * noise
        out[name] = __import__('jax').numpy.asarray(drawn.astype(out[name].dtype))
    for name, factor in factors.items():
        out[name] = (out[name] * factor).astype(out[name].dtype)
    return out
```

```python
from contextlib import ExitStack

import concourse.bass as bass
from concourse import mybir

ALU = mybir.AluOpType
ACT = mybir.ActivationFunctionType
F32 = mybir.dt.float32
I32 = mybir.dt.int32
AX = mybir.AxisListType

P = 128
T = 256
NT = T // P
D = 1024
KD = D // P
DH = 64
DE = DH + 1
HN = 8
G = 2
HF = 8
NC = 16
CMP_BLOCK, CMP_STRIDE = 32, 16
E = 32
C = 64
ROUNDS = T // C
TOPK = 4
EPS = 1e-6
NEG = -1e30
SCALE = DH ** -0.5
LIMIT, SWISH = 7.0, 1.702
SLOTS = 6
SLOPES = [2.0 ** (-8.0 * (h + 1) / HN) for h in range(HN)]

C_Q, C_KV = 0, 512
C_KW, C_GATE = 1024, 1280
C_FQ, C_FK, C_FV, C_FL, C_MERGE = 1304, 1816, 2328, 2840, 2848

R_GA, R_GM, R_PK, R_PV, R_BK1, R_BV1, R_BM = 0, 8, 16, 32, 48, 50, 52
R_QN, R_KC, R_KS, R_KW, R_QF, R_KF, R_ALL = 68, 69, 70, 71, 72, 73, 74
B_GATE, B_CK2, B_CV2, B_ROUTER, B_ALL = 0, 32, 96, 160, 192


def build(nc, a, out):
    with ExitStack() as ctx:
        def sb(name, shape, dt=F32):
            return ctx.enter_context(nc.sbuf_tensor(name, shape, dt))

        def sem(name):
            return ctx.enter_context(nc.semaphore(name))

        banks = [ctx.enter_context(nc.psum_tensor(f"bank{i}", [P, 512], F32)) for i in range(4)]
        bank45 = ctx.enter_context(nc.psum_tensor("bank45", [P, 2, 512], F32))
        bank67 = ctx.enter_context(nc.psum_tensor("bank67", [P, 2, 512], F32))
        PJ = [banks[0], banks[1]]
        S = [banks[2], banks[3]]
        TB = [bank45[:, 0, :], bank45[:, 1, :]]
        OB = [bank67[:, 0, :], bank67[:, 1, :]]

        ring = sb("ring", [P, SLOTS, 4096])
        x = sb("x", [P, NT, D])
        xn = sb("xn", [P, NT, D])
        hT = sb("hT", [P, KD, T])
        rows = sb("rows", [P, 4096])
        heads = sb("heads", [P, 7168])
        late = sb("late", [P, 4096])
        work = sb("work", [P, 2304])
        vrow = sb("vrow", [R_ALL, P])
        vcol = sb("vcol", [P, R_ALL])
        scaled = sb("scaled", [P, 18])
        brow = sb("brow", [1, B_ALL])
        w_c2 = sb("w_c2", [P, 2, 2, DH])
        w_r = sb("w_r", [P, KD, E])
        ident = sb("ident", [P, P])
        causal = sb("causal", [P, T])
        before = sb("before", [P, P])
        upto = sb("upto", [P, P])
        ones = sb("ones", [P, P])
        spread = sb("spread", [NC, P])
        own_head = sb("own_head", [P, HN])
        cmask = sb("cmask", [P, NT, NC])
        cneg = sb("cneg", [P, NT, NC])
        slot_no = sb("slot_no", [P, C])
        t_pos = sb("t_pos", [P, NT])
        small = sb("small", [P, 640])
        route = sb("route", [P, (ROUNDS * E + 2) * 4])
        total_i = sb("total_i", [1, 2], I32)

        def tok(off, n):
            return rows[:, off:off + NT * n * DE].rearrange("p (t h d) -> p t h d", t=NT, h=n)
        o = 0
        q_tok = tok(o, HN); o += NT * HN * DE
        ks_tok = tok(o, G); o += NT * G * DE
        kw_tok = tok(o, G); o += NT * G * DE
        fq_tok = tok(o, HF); o += NT * HF * DE
        fk_tok = tok(o, HF)
        o_nsa = rows[:, 0:1024].rearrange("p (t n) -> p t n", t=NT)
        o_fox = rows[:, 1024:2048].rearrange("p (t n) -> p t n", t=NT)
        oT = [rows[:, 2048 + 1024 * m:3072 + 1024 * m].rearrange("p (k t) -> p k t", t=T) for m in range(2)]
        xflat = xn[:, :, :].rearrange("p t n -> p (t n)")
        vs = xflat[:, 0:256].rearrange("p (t g d) -> p t g d", t=NT, g=G)
        vw = xflat[:, 256:512].rearrange("p (t g d) -> p t g d", t=NT, g=G)
        fv = xflat[:, 512:1536].rearrange("p (t h d) -> p t h d", t=NT, h=HF)
        kc_dup = xflat[:, 1536:2048].rearrange("p (t g u d) -> p t g u d", t=NT, g=G, u=2)
        vc_dup = late[:, 2048:2560].rearrange("p (t g u d) -> p t g u d", t=NT, g=G, u=2)
        e_rows = late[0:E, 0:2048].rearrange("p (m n) -> p m n", m=2)
        v_block = late[:, 2560:3072].rearrange("p (h d) -> p h d", h=HN)
        mergeT = late[:, :].rearrange("p (c t) -> p c t", t=T)
        def feat(off, n):
            return heads[0:DE, off:off + n * T].rearrange("p (h t) -> p h t", t=T)
        qT, ksT, kwT = feat(0, HN), feat(2048, G), feat(2560, G)
        fqT, fkT = feat(3072, HF), feat(5120, HF)
        yT = heads[:, 0:2048].rearrange("p (k t) -> p k t", t=T)

        def hb(off, n=512):
            return heads[:, off:off + n]
        e_x = hb(2048).rearrange("p (k s) -> p k s", s=C)
        e_g, e_sig, e_u, e_h, e_y = (hb(2560 + 512 * i) for i in range(5))
        e_hT = hb(5120).rearrange("p (k h s) -> p k h s", h=2, s=C)
        b_down = heads[0:E, 6144:7168]
        sq = [work[:, 512 * i:512 * i + 512] for i in range(2)]
        blk = [work[:, 1024 + 512 * i:1536 + 512 * i].rearrange("p (m g i) -> p m g i", m=16, g=G) for i in range(2)]
        sm = [work[:, 384 * i:384 * i + 384] for i in range(2)]
        pr = [work[:, 768 + 384 * i:1152 + 384 * i] for i in range(2)]
        prT = [work[:, 1536 + 384 * i:1920 + 384 * i] for i in range(2)]

        cur = [0]
        def sm_(n, shape=None, **kw):
            v = small[:, cur[0]:cur[0] + n]
            cur[0] += n
            assert cur[0] <= 640
            return v.rearrange(shape, **kw) if shape else v
        ss = sm_(2); rr = sm_(2); minus_half = sm_(8)
        ssq = sm_(8); rrq = sm_(8)
        gates = sm_(64, "p (t n) -> p t n", t=NT)
        gate = sm_(48, "p (t n) -> p t n", t=NT)
        fa = sm_(16, "p (t h) -> p t h", t=NT); fb = sm_(16, "p (t h) -> p t h", t=NT)
        mx = sm_(4, "p (b t) -> p b t", t=NT); nmx = sm_(4, "p (b t) -> p b t", t=NT)
        sums = sm_(48, "p (n t) -> p n t", t=NT)
        rg = sm_(16, "p (t h) -> p t h", t=NT)
        csum = sm_(16); ck_ss = sm_(2); ck_r = sm_(2)
        lg = sm_(64, "p (t e) -> p t e", t=NT); top8 = sm_(16, "p (t e) -> p t e", t=NT)
        above = sm_(64, "p (t e) -> p t e", t=NT)
        tot = sm_(8)
        now = sm_(8)
        assert cur[0] <= 640
        hid = late[:, 3072:3200].rearrange("p (v c n) -> p v c n", v=2, c=2)
        hid_a, hid_b = late[:, 3200:3328], late[:, 3328:3456]
        ck65 = late[0:NC, 3456:3456 + G * DE].rearrange("p (g d) -> p g d", g=G)
        ck_sq = late[0:NC, 3600:3728]
        vc16 = late[0:NC, 3728:3856]
        kcT = late[0:DE, 3856:3888].rearrange("p (g c) -> p g c", g=G)
        cp = work[:, 1024:1280]
        cpT = work[:, 1280:1536].rearrange("p (t q) -> p t q", t=NT)
        tmp_br = xflat[:, 1536:2048]
        tmp_up = work[:, 0:T]
        equal = work[:, 256:320].rearrange("p (t e) -> p t e", t=NT)
        count = work[:, 320:384].rearrange("p (t e) -> p t e", t=NT)
        chosen = work[:, 384:448].rearrange("p (t e) -> p t e", t=NT)
        comb = work[:, 448:512].rearrange("p (t e) -> p t e", t=NT)
        hot = work[:, 512:640].rearrange("p (t s) -> p t s", t=NT)
        hotw = work[:, 640:896].rearrange("p (t u s) -> p t u s", t=NT, u=2)
        hotT = work[:, 896:1152].rearrange("p (t q) -> p t q", t=NT)
        combT = work[0:E, 1152:1408].rearrange("p (t q) -> p t q", t=NT)
        e_sel = work[0:E, 1408:1472]
        rv0 = route[:, 0:4]

        x_in, vec_in, small_in, ebias_in, bdown_in, out_sent = map(sem, (
            "x_in", "vec_in", "small_in", "ebias_in", "bdown_in", "out_sent"))
        ring_in = [sem(f"ring_in{i}") for i in range(SLOTS)]
        vrow_set, pool_step, consts_made = map(sem, ("vrow_set", "pool_step", "consts_made"))
        mean_made, inv_made = sem("mean_made"), sem("inv_made")
        v_step, a_step, v_loop_step = sem("vector_step"), sem("scalar_step"), sem("vector_loop_step")
        vec_turned, vec_kept = sem("vec_turned"), sem("vec_kept")
        xn_made, xn_turned, hT_made = sem("xn_made"), sem("xn_turned"), sem("hT_made")
        proj_done, proj_read_a, proj_read_v = sem("proj_done"), sem("proj_read_a"), sem("proj_read_v")
        gates_kept, gates_tanh, f_abs, f_exp, f_ln, f_neg = map(sem, (
            "gates_kept", "gates_tanh", "f_abs", "f_exp", "f_ln", "f_neg"))
        f_summed, f_placed = sem("f_summed"), sem("f_placed")
        kv_turned, blk_made, hid_done, hid_in, hid_tanh, hid_made = map(sem, (
            "kv_turned", "blk_made", "hid_done", "hid_in", "hid_tanh", "hid_made"))
        ck_done, ck_kept, ck_turned, ck_ready = map(sem, ("ck_done", "ck_kept", "ck_turned", "ck_ready"))
        turned, kept_a, kept_v = sem("turned"), sem("kept_a"), sem("kept_v")
        cs_done, cs_max, cs_exp, cp_made, cp_turned, cpT_made, co_done, co_kept = map(sem, (
            "cs_done", "cs_max", "cs_exp", "cp_made", "cp_turned", "cpT_made", "co_done", "co_kept"))
        s_done, s_max, p_made, p_turned, pT_made, o_done, o_kept = map(sem, (
            "s_done", "s_max", "p_made", "p_turned", "pT_made", "o_done", "o_kept"))
        merge_done, merge_made = sem("merge_done"), sem("merge_made")
        o_turned, oT_made, up_done, y_made, out_done, x1_made = map(sem, (
            "o_turned", "oT_made", "up_done", "y_made", "out_done", "x1_made"))
        lg_done, sel_made, pos_done, route_made, comb_turned, combT_made, bd_done, bd_added = map(sem, (
            "lg_done", "sel_made", "pos_done", "route_made", "comb_turned", "combT_made", "bd_done", "bd_added"))
        hot_made, gathered, ex_made = sem("hot_made"), sem("gathered"), sem("ex_made")
        hotw_made, hotw_turned, hotT_made = sem("hotw_made"), sem("hotw_turned"), sem("hotT_made")
        half_done = {m: sem(f"expert_{m}_half_done") for m in ("gate", "up", "down")}
        mat_done = {m: sem(f"expert_{m}_done") for m in ("gate", "up", "down")}
        g_made, sig_made, up_read, eh_made, eh_turned, ehT_made = map(sem, (
            "g_made", "sig_made", "up_read", "eh_made", "eh_turned", "ehT_made"))
        y_kept, spread_done, added, rows_added = map(sem, (
            "y_kept", "spread_done", "added", "rows_added"))

        def gain_of(r):
            return vcol[:, r:r + 1]
        UNITS = [(q_tok, qT, 2 * i, scaled[:, 16:17]) for i in range(4)] \
            + [(ks_tok, ksT, 0, gain_of(R_KS)), (kw_tok, kwT, 0, gain_of(R_KW))] \
            + [(fk_tok, fkT, 2 * i, gain_of(R_KF)) for i in range(4)] \
            + [(fq_tok, fqT, 2 * i, scaled[:, 17:18]) for i in range(4)]
        CHAIN = 3

        block = ctx.enter_context(nc.Block())

        w_in = a["w_in"][0].rearrange("(k p) n -> p k n", p=P)

        def in_cols(c0, n):
            return [(w_in[:, :, c0:c0 + n], 0, n)]
        BLOCKS = [
            ("kv", in_cols(C_KV, 512), 8, 512),
            ("kw", in_cols(C_KW, 280) + [(w_in[:, :, C_FL:C_FL + 8], 280, 8)], 8, 288),
            ("q", in_cols(C_Q, 512), 8, 512),
            ("ck1", [(a["w_ck1"][0].rearrange("(m p) n -> p m n", p=P), 0, 256)], 16, 256),
            ("cv1", [(a["w_cv1"][0].rearrange("(m p) n -> p m n", p=P), 0, 256)], 16, 256),
            ("fk", in_cols(C_FK, 512), 8, 512),
            ("fq", in_cols(C_FQ, 512), 8, 512),
            ("fv", in_cols(C_FV, 512), 8, 512),
        ] + [(f"merge{i}", in_cols(C_MERGE + 512 * i, 512), 8, 512) for i in range(4)] + [
            ("up_nsa", [(a["w_up_nsa"][0].rearrange("(k p) n -> p k n", p=P), 0, 1024)], 4, 1024),
            ("up_fox", [(a["w_up_fox"][0].rearrange("(k p) n -> p k n", p=P), 0, 1024)], 4, 1024),
            ("out0", [(a["w_out"][0].rearrange("(k p) n -> p k n", p=P)[:, 0:4, :], 0, 1024)], 4, 1024),
            ("out1", [(a["w_out"][0].rearrange("(k p) n -> p k n", p=P)[:, 4:8, :], 0, 1024)], 4, 1024),
        ]
        FIRST = (SLOTS - len(BLOCKS) % SLOTS) % SLOTS
        slot_of = {b[0]: (FIRST + i) % SLOTS for i, b in enumerate(BLOCKS)}
        view, arrives, n_in = {}, {}, [0] * SLOTS
        for name, pieces, k, n in BLOCKS:
            s = slot_of[name]
            view[name] = ring[:, s, 0:k * n].rearrange("p (k n) -> p k n", k=k)
            n_in[s] += 16 * len(pieces)
            arrives[name] = (s, n_in[s])
        freed = {"kv": (proj_done, 2), "kw": (proj_done, 4), "q": (proj_done, 6), "ck1": (hid_done, 1),
                 "cv1": (hid_done, 2), "fk": (proj_done, 8), "fq": (proj_done, 10), "fv": (proj_done, 12)}
        for i in range(4):
            freed[f"merge{i}"] = (merge_done, 4 * i + 4)
        freed |= {"up_nsa": (up_done, KD), "up_fox": (up_done, KD), "out0": (out_done, 1), "out1": (out_done, 2)}

        def wait_block(eng, name):
            s, v = arrives[name]
            eng.wait_ge(ring_in[s], v)

        ex_half = {"gate": (0, 1), "up": (2, 3), "down": (4, 5)}
        ex_src = {"gate": "w_e_gate", "up": "w_e_up", "down": "w_e_down"}

        def col(ap, n):
            return ap.unsqueeze(2).to_broadcast([ap.shape[0], ap.shape[1], n])

        @block.sync
        def _(sp):
            sp.dma_start(x[:, :, :], a["x"][0].rearrange("(t p) n -> p t n", p=P)).then_inc(x_in, 16)
            for i, (name, pieces, k, n) in enumerate(BLOCKS):
                if i >= SLOTS:
                    sp.wait_ge(*freed[BLOCKS[i - SLOTS][0]])
                for src, c0, w in pieces:
                    sp.dma_start(view[name][:, :, c0:c0 + w], src).then_inc(ring_in[slot_of[name]], 16)

            def expert_loads(e, free):
                for m in ("gate", "up", "down"):
                    src = a[ex_src[m]][0, bass.ds(e, 1)] if not isinstance(e, int) else a[ex_src[m]][0, e:e + 1]
                    src = src.rearrange("o (k p) n -> p (o k) n", p=P)
                    for h in range(2):
                        s = ex_half[m][h]
                        sp.wait_ge(x_in, 16)
                        sp.wait_ge(*free(m, h))
                        sp.dma_start(ring[:, s, :].rearrange("p (k n) -> p k n", k=4),
                                     src[:, 4 * h:4 * h + 4, :]).then_inc(ring_in[s], 16)
            last = [b[0] for b in BLOCKS[-SLOTS:]]
            expert_loads(0, lambda m, h: freed[last[ex_half[m][h]]])
            with sp.Fori(1, E) as it:
                expert_loads(it, lambda m, h: ((half_done if h == 0 else mat_done)[m], it))
            sp.wait_ge(route_made, 1)
            total = sp.value_load(total_i[0:1, 0:1], min_val=E, max_val=ROUNDS * E)
            with sp.If(total > E):
                with sp.Fori(E, total) as it:
                    expert_loads(it & (E - 1), lambda m, h: ((half_done if h == 0 else mat_done)[m], it))
            sp.wait_ge(rows_added, total)
            sp.dma_start(out[0].rearrange("(t p) n -> p t n", p=P), x[:, :, :]).then_inc(out_sent, 16)
            sp.wait_ge(out_sent, 16)

        @block.gpsimd
        def _(pool):
            n = [0]

            def step(ins):
                n[0] += 1
                ins.then_inc(pool_step, 1)
                pool.wait_ge(pool_step, n[0])
            nc.gpsimd.memset(vrow[:, :], 1.0).then_inc(vrow_set, 1)
            step(nc.gpsimd.memset(minus_half, -0.5))
            step(nc.gpsimd.memset(ident[:, :], 0.0))
            nc.gpsimd.affine_select(out=ident[:, :], in_=ident[:, :], compare_op=ALU.not_equal, fill=1.0,
                                    base=0, pattern=[[-1, P]], channel_multiplier=1).then_inc(consts_made, 1)
            step(nc.gpsimd.memset(ones[:, :], 1.0))
            nc.gpsimd.affine_select(out=upto[:, :], in_=ones[:, :], compare_op=ALU.is_ge, fill=0.0,
                                    base=0, pattern=[[1, P]], channel_multiplier=-1)
            nc.gpsimd.affine_select(out=before[:, :], in_=ones[:, :], compare_op=ALU.is_gt, fill=0.0,
                                    base=0, pattern=[[1, P]], channel_multiplier=-1)
            step(nc.gpsimd.memset(causal[:, :], 0.0))
            nc.gpsimd.affine_select(out=causal[:, :], in_=causal[:, :], compare_op=ALU.is_ge, fill=NEG,
                                    base=P, pattern=[[-1, T]], channel_multiplier=1)
            nc.gpsimd.iota(t_pos[:, :], pattern=[[P, NT]], base=0, channel_multiplier=1,
                           allow_small_or_imprecise_dtypes=True)
            nc.gpsimd.iota(slot_no[:, :], pattern=[[1, C]], base=0, channel_multiplier=0,
                           allow_small_or_imprecise_dtypes=True)
            step(nc.gpsimd.memset(cmask[:, :, :], 1.0))
            step(nc.gpsimd.affine_select(out=cmask[:, :, :], in_=cmask[:, :, :], compare_op=ALU.is_ge, fill=0.0,
                                         base=1 - CMP_BLOCK, pattern=[[P, NT], [-CMP_STRIDE, NC]], channel_multiplier=1))
            nc.gpsimd.tensor_scalar(cneg[:, :, :], cmask[:, :, :], -1.0, -NEG, ALU.add, ALU.mult)
            step(nc.gpsimd.memset(spread[:, :], 0.0))
            nc.gpsimd.affine_select(out=spread[:, :].rearrange("p (h c) -> p h c", h=HN),
                                    in_=spread[:, :].rearrange("p (h c) -> p h c", h=HN),
                                    compare_op=ALU.not_equal, fill=1.0, base=0,
                                    pattern=[[0, HN], [-1, NC]], channel_multiplier=1)
            step(nc.gpsimd.memset(own_head[:, :], 1.0))
            step(nc.gpsimd.affine_select(out=own_head[:, :], in_=own_head[:, :], compare_op=ALU.is_ge, fill=0.0,
                                         base=0, pattern=[[-NC, HN]], channel_multiplier=1))
            nc.gpsimd.affine_select(out=own_head[:, :], in_=own_head[:, :], compare_op=ALU.is_ge, fill=0.0,
                                    base=NC - 1, pattern=[[NC, HN]], channel_multiplier=-1)
            nc.gpsimd.memset(blk[0], 0.0)
            nc.gpsimd.memset(blk[1], 0.0)
            for h in range(HN):
                nc.gpsimd.memset(q_tok[:, :, h, DH:DE], SLOPES[h] / SCALE)
            nc.gpsimd.memset(fq_tok[:, :, :, DH:DE], 1.0 / SCALE)
            for g in range(G):
                nc.gpsimd.iota(ck65[:, g, DH:DE], pattern=[[0, 1]], base=CMP_BLOCK - 1, channel_multiplier=CMP_STRIDE,
                               allow_small_or_imprecise_dtypes=True)
            for g in range(G):
                nc.gpsimd.iota(ks_tok[:, :, g, DH:DE], pattern=[[P, NT], [0, 1]], base=0, channel_multiplier=1,
                               allow_small_or_imprecise_dtypes=True)
                last = nc.gpsimd.iota(kw_tok[:, :, g, DH:DE], pattern=[[P, NT], [0, 1]], base=0, channel_multiplier=1,
                                      allow_small_or_imprecise_dtypes=True)
            last.then_inc(consts_made, 1)
            for i, r in enumerate([rr] + [rrq[:, 0:G]] * 4 + [rrq] * 4 + [ck_r[0:NC, :]] + [rrq] * 2 + [rr]):
                pool.wait_ge(mean_made, i + 1)
                nc.gpsimd.tensor_tensor(r, r, minus_half[0:r.shape[0], 0:r.shape[1]], ALU.pow).then_inc(inv_made, 1)

        @block.scalar
        def _(act):
            n = [0]

            def step(ins):
                n[0] += 1
                ins.then_inc(a_step, 1)
                act.wait_ge(a_step, n[0])
            act.wait_ge(vrow_set, 1)
            for r0, nr, name in ((R_GA, 8, "g_attn"), (R_GM, 8, "g_mlp"), (R_BK1, 2, "b_ck1"), (R_BV1, 2, "b_cv1"),
                                 (R_BM, 16, "b_merge")):
                act.dma_start(vrow[r0:r0 + nr, :], a[name][0].rearrange("(r n) -> r n", r=nr)).then_inc(vec_in, 16)
            for r0, name in ((R_PK, "pos_cmp_k"), (R_PV, "pos_cmp_v")):
                act.dma_start(vrow[r0:r0 + 16, :], a[name][0].rearrange("(r u) d -> r (u d)", u=2)).then_inc(vec_in, 16)
            for r0, name in ((R_QN, "qn_nsa"), (R_KC, "kn_cmp"), (R_KS, "kn_sel"), (R_KW, "kn_win"),
                             (R_QF, "qn_fox"), (R_KF, "kn_fox")):
                act.dma_start(vrow[r0:r0 + 1, 0:DH], a[name]).then_inc(vec_in, 16)
            for c0, w, name in ((B_GATE, 24, "b_nsa_gate"), (B_GATE + 24, 8, "b_forget"), (B_CK2, DH, "b_ck2"),
                                (B_CV2, DH, "b_cv2"), (B_ROUTER, E, "b_router")):
                act.dma_start(brow[:, c0:c0 + w], a[name]).then_inc(small_in, 16)
            act.dma_start(w_c2[:, 0, :, :], a["w_ck2"][0].rearrange("(c p) n -> p c n", p=P)).then_inc(small_in, 16)
            act.dma_start(w_c2[:, 1, :, :], a["w_cv2"][0].rearrange("(c p) n -> p c n", p=P)).then_inc(small_in, 16)
            act.dma_start(w_r[:, :, :], a["w_router"][0].rearrange("(k p) n -> p k n", p=P)).then_inc(small_in, 16)

            def two(ap):
                return ap.unsqueeze(2).to_broadcast([P, G, 2, DH])
            for i in range(12):
                b, t, ps = i // 2, i % 2, PJ[i % 2]
                act.wait_ge(proj_done, i + 1)
                dve_before = i if i < 10 else 10
                if i >= 2 and b < 5:
                    act.wait_ge(proj_read_v, dve_before - 1)
                if b == 0:
                    if t == 0:
                        act.wait_ge(xn_turned, 1)
                    kv = ps[:, :].rearrange("p (j g d) -> p j g d", j=4, g=G)
                    nc.scalar.activation(kc_dup[:, t], two(kv[:, 0]), ACT.Copy)
                    nc.scalar.activation(vc_dup[:, t], two(kv[:, 1]), ACT.Copy)
                    nc.scalar.activation(vs[:, t], kv[:, 3], ACT.Copy)
                    nc.scalar.activation(sq[i % 2][:, 0:P], ps[:, 256:384], ACT.Square).then_inc(proj_read_a, 1)
                elif b == 1:
                    nc.scalar.activation(vw[:, t], ps[:, 128:256].rearrange("p (g d) -> p g d", g=G), ACT.Copy)
                    nc.scalar.activation(gates[:, t], ps[:, 256:288], ACT.Copy).then_inc(gates_kept, 1)
                    nc.scalar.activation(sq[i % 2][:, 0:P], ps[:, 0:128], ACT.Square).then_inc(proj_read_a, 1)
                    if t == 1:
                        act.wait_ge(gates_kept, 2)
                        nc.scalar.activation(gate[:, :, :], gates[:, :, 0:24], ACT.Tanh, scale=0.5).then_inc(gates_tanh, 1)
                        nc.scalar.activation(fa[:, :, :], gates[:, :, 24:32], ACT.Abs).then_inc(f_abs, 1)
                        act.wait_ge(f_abs, 1)
                        nc.scalar.activation(fb[:, :, :], fa[:, :, :], ACT.Exp, scale=-1.0).then_inc(f_exp, 1)
                        act.wait_ge(f_exp, 1)
                        nc.scalar.activation(fa[:, :, :], fb[:, :, :], ACT.Ln, bias=1.0).then_inc(f_ln, 1)
                elif b == 5:
                    nc.scalar.activation(fv[:, t], ps[:, :].rearrange("p (h d) -> p h d", h=HF), ACT.Copy).then_inc(proj_read_a, 1)
                else:
                    nc.scalar.activation(sq[i % 2], ps[:, :], ACT.Square).then_inc(proj_read_a, 1)
                if i == 7:
                    act.wait_ge(hid_in, 1)
                    nc.scalar.activation(hid_b, hid_b, ACT.Tanh, scale=0.7978845608028654).then_inc(hid_tanh, 1)
            for u in range(0, len(UNITS), 2):
                src, dst, h0, gain = UNITS[u]
                act.wait_ge(turned, u + 1)
                nc.scalar.activation(dst[:, h0:h0 + 2, :], TB[0][0:DE, :].rearrange("p (h t) -> p h t", h=2), ACT.Copy,
                                     scale=gain[0:DE, :]).then_inc(kept_a, 1)
                if u == 4:
                    act.wait_ge(cs_max, 1)
                    nc.scalar.activation(cp, cp, ACT.Exp).then_inc(cs_exp, 1)
            for m in range(24):
                act.wait_ge(s_max, m + 1)
                if m >= 2:
                    act.wait_ge(p_turned, m - 1)
                nc.scalar.activation(pr[m % 2][:, 0:P], sm[m % 2][:, 0:P], ACT.Exp, bias=nmx[:, m % 2, 0:1],
                                     accum_out=sums[:, m, 0:1])
                nc.scalar.activation(pr[m % 2][:, P:384], sm[m % 2][:, P:384], ACT.Exp, bias=nmx[:, m % 2, 1:2],
                                     accum_out=sums[:, m, 1:2]).then_inc(p_made, 1)
                if m < 16:
                    act.wait_ge(merge_done, m + 1)
                    nc.scalar.activation(mergeT[:, m, :], PJ[m % 2][:, 0:T], ACT.Tanh, scale=0.5,
                                         bias=scaled[:, m:m + 1]).then_inc(merge_made, 1)
            act.wait_ge(o_done, 3)
            act.dma_start(b_down, a["b_e_down"][0]).then_inc(bdown_in, 16)
            act.wait_ge(y_made, KD)
            act.dma_start(e_rows[:, 0, :], a["b_e_gate"][0]).then_inc(ebias_in, 16)
            act.dma_start(e_rows[:, 1, :], a["b_e_up"][0]).then_inc(ebias_in, 16)
            act.wait_ge(sel_made, 1)
            nc.scalar.activation(lg[:, :, :], lg[:, :, :], ACT.Exp).then_inc(sel_made, 1)

            def keep_y(done):
                act.wait_ge(mat_done["down"], done)
                nc.scalar.activation(e_y, banks[3][:, :], ACT.Copy).then_inc(y_kept, 1)

            def expert(it, first):
                if not first:
                    keep_y(it)
                act.wait_ge(g_made, it + 1)
                nc.scalar.activation(e_sig, e_g, ACT.Sigmoid, scale=SWISH).then_inc(sig_made, 1)
                act.wait_ge(hotw_turned, it + 1)
                nc.scalar.activation(hotT, bank45[:, 1, 0:T].rearrange("p (t q) -> p t q", t=NT), ACT.Copy).then_inc(hotT_made, 1)
            act.wait_ge(route_made, 1)
            total = act.value_load(total_i[0:1, 0:1], min_val=E, max_val=ROUNDS * E)
            expert(0, True)
            with act.Fori(1, total) as it:
                expert(it, False)
            keep_y(total)

        @block.vector
        def _(dve):
            n = [0]

            def step(ins):
                n[0] += 1
                ins.then_inc(v_step, 1)
                dve.wait_ge(v_step, n[0])

            n_inv = [0]

            def inv_rms(dst, src, width):
                nc.vector.tensor_scalar(dst, src, 1.0 / width, EPS, ALU.mult, ALU.add).then_inc(mean_made, 1)
                n_inv[0] += 1
                dve.wait_ge(inv_made, n_inv[0])

            def norm_rows(made):
                for t in range(NT):
                    step(nc.vector.tensor_tensor_reduce(xn[:, t, :], x[:, t, :], x[:, t, :], 1.0, 0.0,
                                                        ALU.mult, ALU.add, ss[:, t:t + 1]))
                inv_rms(rr, ss, D)
                for t in range(NT):
                    nc.vector.tensor_scalar(xn[:, t, :], x[:, t, :], rr[:, t:t + 1], None, ALU.mult).then_inc(made, 1)

            def keep_hT(gain_col, bank_list, turned_sem, base):
                for j in range(4):
                    dve.wait_ge(turned_sem, base + 1)
                    nc.vector.tensor_tensor(hT[:, 2 * j:2 * j + 2, :], bank_list[j][:, :].rearrange("p (k t) -> p k t", k=2),
                                            col(vcol[:, gain_col + 2 * j:gain_col + 2 * j + 2], T), ALU.mult).then_inc(hT_made, 1)

            dve.wait_ge(x_in, 16)
            norm_rows(xn_made)
            dve.wait_ge(vec_turned, 1)
            step(nc.vector.tensor_copy(vcol[:, :], TB[0][:, 0:R_ALL]))
            nc.vector.tensor_scalar(scaled[:, 0:16], vcol[:, R_BM:R_BM + 16], 0.5, None, ALU.mult)
            nc.vector.tensor_scalar(scaled[:, 16:17], vcol[:, R_QN:R_QN + 1], SCALE, None, ALU.mult)
            nc.vector.tensor_scalar(scaled[:, 17:18], vcol[:, R_QF:R_QF + 1], SCALE, None, ALU.mult).then_inc(vec_kept, 1)
            keep_hT(R_GA, [PJ[0], PJ[1], S[0], S[1]], xn_turned, 0)

            def head_norm(i, c0, n_heads, dst):
                ps = PJ[i % 2]
                dve.wait_ge(proj_read_a, i + 1)
                step(nc.vector.tensor_reduce(ssq[:, 0:n_heads], sq[i % 2][:, 0:n_heads * DH].rearrange("p (h d) -> p h d", d=DH),
                                             AX.X, ALU.add))
                inv_rms(rrq[:, 0:n_heads], ssq[:, 0:n_heads], DH)
                nc.vector.tensor_tensor(dst, ps[:, c0:c0 + n_heads * DH].rearrange("p (h d) -> p h d", d=DH),
                                        col(rrq[:, 0:n_heads], DH), ALU.mult).then_inc(proj_read_v, 1)
            for t in range(NT):
                head_norm(t, 256, G, ks_tok[:, t, :, 0:DH])
            for t in range(NT):
                head_norm(2 + t, 0, G, kw_tok[:, t, :, 0:DH])
            dve.wait_ge(gates_kept, 2)
            dve.wait_ge(gates_tanh, 1)
            dve.wait_ge(f_abs, 1)
            step(nc.vector.tensor_scalar(gate[:, :, :], gate[:, :, :], 1.0, 0.5, ALU.add, ALU.mult))
            step(nc.vector.tensor_scalar(gates[:, :, 24:32], gates[:, :, 24:32], 0.0, None, ALU.min))
            dve.wait_ge(f_ln, 1)
            nc.vector.tensor_tensor(fb[:, :, :], fa[:, :, :], gates[:, :, 24:32], ALU.subtract).then_inc(f_neg, 1)
            dve.wait_ge(consts_made, 2)
            for v in range(2):
                dve.wait_ge(kv_turned, v + 1)
                tb = TB[v].rearrange("p (g t) -> p g t", g=G)
                for par in range(2):
                    lo = 64 * par
                    for half in range(2):
                        s0 = CMP_STRIDE * half
                        tv = tb[lo:lo + 64, :, s0:s0 + 240].rearrange("p g (i m u) -> p g i m u", m=8, u=2)[:, :, :, :, par]
                        pcol = vcol[lo:lo + 64, (R_PK, R_PV)[v] + 8 * half:(R_PK, R_PV)[v] + 8 * half + 8]
                        pcol = pcol.unsqueeze(1).unsqueeze(1).to_broadcast([64, G, NC - 1, 8])
                        dst = blk[v][lo:lo + 64, 8 * half:8 * half + 8, :, 0:NC - 1].rearrange("p m g i -> p g i m")
                        for g in range(G):
                            last = nc.vector.tensor_tensor(dst[:, g], tv[:, g], pcol[:, g], ALU.add)
                last.then_inc(blk_made, 1)
            for t in range(NT):
                head_norm(4 + t, 0, HN, q_tok[:, t, :, 0:DH])
            dve.wait_ge(hid_done, 2)
            for v in range(2):
                for c in range(2):
                    r = (R_BK1, R_BV1)[v] + c
                    last = nc.vector.tensor_scalar(hid[:, v, c, :], S[0][:, 64 * v + 32 * c:64 * v + 32 * c + 32],
                                                   vcol[:, r:r + 1], None, ALU.add)
            step(last)
            hflat = late[:, 3072:3200]
            step(nc.vector.tensor_tensor(hid_a, hflat, hflat, ALU.mult))
            step(nc.vector.tensor_scalar(hid_b, hid_a, 0.044715, 1.0, ALU.mult, ALU.add))
            nc.vector.tensor_tensor(hid_b, hid_b, hflat, ALU.mult).then_inc(hid_in, 1)
            step(nc.vector.tensor_scalar(hid_a, hflat, 0.5, None, ALU.mult))
            for t in range(NT):
                head_norm(6 + t, 0, HF, fk_tok[:, t, :, 0:DH])
            dve.wait_ge(hid_tanh, 1)
            nc.vector.scalar_tensor_tensor(out=hflat, in0=hid_b, scalar=1.0, in1=hid_a, op0=ALU.add, op1=ALU.mult).then_inc(hid_made, 1)
            dve.wait_ge(ck_done, 1)
            step(nc.vector.tensor_copy(ck_sq, S[1][0:NC, 0:P]))
            step(nc.vector.tensor_tensor(ck_sq, ck_sq, ck_sq, ALU.mult))
            step(nc.vector.tensor_reduce(ck_ss[0:NC, :], ck_sq.rearrange("p (g d) -> p g d", g=G), AX.X, ALU.add))
            inv_rms(ck_r[0:NC, :], ck_ss[0:NC, :], DH)
            nc.vector.tensor_tensor(ck65[:, :, 0:DH], S[1][0:NC, 0:P].rearrange("p (g d) -> p g d", g=G),
                                    col(ck_r[0:NC, :], DH), ALU.mult)
            nc.vector.tensor_copy(vc16, S[1][0:NC, P:2 * P]).then_inc(ck_kept, 1)
            dve.wait_ge(f_summed, 1)
            nc.vector.tensor_copy(fk_tok[:, :, :, DH], OB[0][:, 0:16].rearrange("p (t h) -> p t h", t=NT)).then_inc(f_placed, 1)
            for t in range(NT):
                head_norm(8 + t, 0, HF, fq_tok[:, t, :, 0:DH])
            dve.wait_ge(ck_turned, 1)
            nc.vector.tensor_scalar(kcT, OB[1][0:DE, 0:32].rearrange("p (g c) -> p g c", g=G),
                                    vcol[0:DE, R_KC:R_KC + 1], None, ALU.mult)
            for g in range(G):
                last = nc.vector.tensor_tensor(
                    v_block[:, 4 * g:4 * g + 4, :],
                    S[1][:, DH * g:DH * g + DH].unsqueeze(1).to_broadcast([P, 4, DH]),
                    col(own_head[:, 4 * g:4 * g + 4], DH), ALU.mult)
            last.then_inc(ck_ready, 1)

            def keep_unit(u):
                src, dst, h0, gain = UNITS[u]
                dve.wait_ge(turned, u + 1)
                nc.vector.tensor_scalar(dst[:, h0:h0 + 2, :], TB[1][0:DE, :].rearrange("p (h t) -> p h t", h=2),
                                        gain[0:DE, :], None, ALU.mult).then_inc(kept_v, 1)
            for u in (1, 3, 5):
                keep_unit(u)
            dve.wait_ge(cs_done, 1)
            c4 = cp.rearrange("p (t h c) -> p t h c", t=NT, h=HN)
            c3 = cp.rearrange("p (n c) -> p n c", c=NC)
            for t in range(NT):
                last = nc.vector.tensor_tensor(c4[:, t], S[0][:, P * t:P * t + P].rearrange("p (h c) -> p h c", h=HN),
                                               cneg[:, t, :].unsqueeze(1).to_broadcast([P, HN, NC]), ALU.add)
            step(last)
            step(nc.vector.tensor_reduce(csum, c3, AX.X, ALU.max))
            nc.vector.tensor_tensor(c3, c3, col(csum, NC), ALU.subtract).then_inc(cs_max, 1)
            dve.wait_ge(cs_exp, 1)
            for t in range(NT):
                last = nc.vector.tensor_tensor(c4[:, t], c4[:, t], cmask[:, t, :].unsqueeze(1).to_broadcast([P, HN, NC]), ALU.mult)
            step(last)
            step(nc.vector.tensor_reduce(csum, c3, AX.X, ALU.add))
            step(nc.vector.tensor_scalar(csum, csum, 1e-30, None, ALU.max))
            step(nc.vector.reciprocal(csum, csum))
            step(nc.vector.tensor_tensor(csum.rearrange("p (t h) -> p t h", t=NT), csum.rearrange("p (t h) -> p t h", t=NT),
                                         gate[:, :, 0:HN], ALU.mult))
            nc.vector.tensor_tensor(c3, c3, col(csum, NC), ALU.mult).then_inc(cp_made, 1)
            for u in (7, 9, 11, 13):
                keep_unit(u)
            dve.wait_ge(cp_turned, 1)
            nc.vector.tensor_copy(cpT, S[1][:, 0:T].rearrange("p (t q) -> p t q", t=NT)).then_inc(cpT_made, 1)
            dve.wait_ge(co_done, 1)
            nc.vector.tensor_copy(o_nsa[:, 0, :], OB[0])
            nc.vector.tensor_copy(o_nsa[:, 1, :], OB[1]).then_inc(co_kept, 1)

            def row_max(m):
                dve.wait_ge(s_done, m + 1)
                if m >= 2:
                    dve.wait_ge(p_made, m - 1)
                b = m % 2
                nc.vector.tensor_tensor_reduce(sm[b][:, 0:P], S[b][:, 0:P], causal[:, P:T], 1.0, NEG * 2,
                                               ALU.add, ALU.max, mx[:, b, 0:1])
                step(nc.vector.tensor_tensor_reduce(sm[b][:, P:384], S[b][:, P:384], causal[:, :], 1.0, NEG * 2,
                                                    ALU.add, ALU.max, mx[:, b, 1:2]))
                nc.vector.tensor_scalar(nmx[:, b, :], mx[:, b, :], -1.0, None, ALU.mult).then_inc(s_max, 1)

            def keep_pT(m):
                dve.wait_ge(p_turned, m + 1)
                nc.vector.tensor_copy(prT[m % 2], TB[m % 2][:, 0:384]).then_inc(pT_made, 1)

            def keep_o(br):
                dve.wait_ge(o_done, br + 1)
                dst = o_fox if br == 2 else o_nsa
                step(nc.vector.reciprocal(rg[:, :, :].rearrange("p t h -> p h t"), sums[:, 8 * br:8 * br + 8, :]))
                if br < 2:
                    g0 = (16, 8)[br]
                    step(nc.vector.tensor_tensor(rg[:, :, :], rg[:, :, :], gate[:, :, g0:g0 + 8], ALU.mult))
                for t in range(NT):
                    ob = OB[t].rearrange("p (h d) -> p h d", d=DH)
                    if br == 2:
                        last = nc.vector.tensor_tensor(dst[:, t, :].rearrange("p (h d) -> p h d", d=DH), ob, col(rg[:, t, :], DH), ALU.mult)
                    else:
                        step(nc.vector.tensor_tensor(tmp_br.rearrange("p (h d) -> p h d", d=DH), ob, col(rg[:, t, :], DH), ALU.mult))
                        last = nc.vector.tensor_tensor(dst[:, t, :], dst[:, t, :], tmp_br, ALU.add)
                        if t == 0:
                            step(last)
                last.then_inc(o_kept, 1)
            for m in range(26):
                if m < 24:
                    row_max(m)
                if 1 <= m <= 24:
                    keep_pT(m - 1)
                if m in (9, 17, 25):
                    keep_o((m - 9) // 8)
            for mix in range(2):
                for t2 in range(2):
                    dve.wait_ge(o_turned, 2 * mix + t2 + 1)
                    nc.vector.tensor_copy(oT[mix][:, 2 * t2:2 * t2 + 2, :],
                                          (S, TB)[mix][t2][:, :].rearrange("p (k t) -> p k t", k=2)).then_inc(oT_made, 1)
            dve.wait_ge(merge_made, 16)
            for c in range(KD):
                dve.wait_ge(up_done, c + 1)
                ps = PJ[c % 2]
                step(nc.vector.scalar_tensor_tensor(out=yT[:, c, :], in0=mergeT[:, c, :], scalar=1.0, in1=ps[:, 0:T],
                                                    op0=ALU.add, op1=ALU.mult))
                step(nc.vector.scalar_tensor_tensor(out=tmp_up, in0=mergeT[:, KD + c, :], scalar=1.0, in1=ps[:, T:2 * T],
                                                    op0=ALU.add, op1=ALU.mult))
                nc.vector.tensor_tensor(yT[:, c, :], yT[:, c, :], tmp_up, ALU.add).then_inc(y_made, 1)
                dve.wait_ge(y_made, c + 1)
            dve.wait_ge(out_done, 2)
            for t in range(NT):
                for h in range(2):
                    step(nc.vector.scalar_tensor_tensor(out=x[:, t, 512 * h:512 * h + 512], in0=(S, TB)[t][h][:, :], scalar=0.5,
                                                        in1=x[:, t, 512 * h:512 * h + 512], op0=ALU.mult, op1=ALU.add))
            norm_rows(x1_made)
            keep_hT(R_GM, [PJ[0], PJ[1], OB[0], OB[1]], xn_turned, 1)

            dve.wait_ge(lg_done, 1)
            step(nc.vector.tensor_copy(lg[:, :, :], TB[0][:, 0:64].rearrange("p (t e) -> p t e", t=NT)))
            for t in range(NT):
                last = nc.vector.max(top8[:, t, :], lg[:, t, :])
            step(last)
            for t in range(NT):
                step(nc.vector.tensor_scalar(above[:, t, :], lg[:, t, :], top8[:, t, 3:4], None, ALU.is_gt))
                step(nc.vector.tensor_reduce(tot[:, t:t + 1], above[:, t, :], AX.X, ALU.add))
                step(nc.vector.tensor_scalar(tot[:, 2 + t:3 + t], tot[:, t:t + 1], -1.0, float(TOPK), ALU.mult, ALU.add))
                step(nc.vector.tensor_scalar(equal[:, t, :], lg[:, t, :], top8[:, t, 3:4], None, ALU.is_equal))
                step(nc.vector.tensor_tensor_scan(count[:, t, :], ones[:, 0:E], equal[:, t, :], 0.0, ALU.mult, ALU.add))
                step(nc.vector.scalar_tensor_tensor(out=count[:, t, :], in0=count[:, t, :], scalar=tot[:, 2 + t:3 + t],
                                                    in1=equal[:, t, :], op0=ALU.is_le, op1=ALU.mult))
                step(nc.vector.tensor_tensor(chosen[:, t, :], above[:, t, :], count[:, t, :], ALU.add))
                last = nc.vector.tensor_scalar(lg[:, t, :], lg[:, t, :], top8[:, t, 0:1], None, ALU.subtract)
            last.then_inc(sel_made, 1)
            dve.wait_ge(sel_made, 2)
            step(nc.vector.tensor_tensor(comb[:, :, :], lg[:, :, :], chosen[:, :, :], ALU.mult))
            step(nc.vector.tensor_reduce(tot[:, 4:6], comb[:, :, :], AX.X, ALU.add))
            step(nc.vector.reciprocal(tot[:, 6:8], tot[:, 4:6]))
            nc.vector.tensor_tensor(comb[:, :, :], comb[:, :, :], col(tot[:, 6:8], E), ALU.mult).then_inc(sel_made, 1)
            dve.wait_ge(sel_made, 3)
            dve.wait_ge(pos_done, 1)
            for t in range(NT):
                last = nc.vector.scalar_tensor_tensor(out=above[:, t, :], in0=TB[1][:, E * t:E * t + E], scalar=1.0,
                                                      in1=chosen[:, t, :], op0=ALU.add, op1=ALU.mult)
            step(last)
            steps = ROUNDS * E
            rt = route[:, 0:steps * 4].rearrange("p (r e j) -> p r e j", r=ROUNDS, e=E)
            nc.vector.memset(route[:, steps * 4:], 0.0)
            for r in range(ROUNDS):
                for t in range(NT):
                    nc.vector.tensor_scalar(rt[:, r, :, t], above[:, t, :], -1.0 - C * r, None, ALU.add)
                    last = nc.vector.tensor_copy(rt[:, r, :, 2 + t], comb[:, t, :])
            step(last)
            step(nc.vector.tensor_reduce(tot[:, 0:1], TB[1][:, 2 * E:3 * E], AX.X, ALU.max))
            step(nc.vector.tensor_scalar(tot[:, 1:2], tot[:, 0:1], float(C), None, ALU.is_gt))
            for r in range(2, ROUNDS):
                step(nc.vector.scalar_tensor_tensor(out=tot[:, 1:2], in0=tot[:, 0:1], scalar=float(C * r), in1=tot[:, 1:2],
                                                    op0=ALU.is_gt, op1=ALU.add))
            step(nc.vector.tensor_scalar(tot[:, 2:3], tot[:, 1:2], float(E), float(E), ALU.mult, ALU.add))
            step(nc.vector.tensor_scalar(tot[:, 3:4], tot[:, 2:3], -1.0, None, ALU.add))
            nc.vector.tensor_copy(total_i[:, :], tot[0:1, 2:4]).then_inc(route_made, 1)
            dve.wait_ge(comb_turned, 1)
            nc.vector.tensor_copy(combT, OB[0][0:E, 0:T].rearrange("p (t q) -> p t q", t=NT)).then_inc(combT_made, 1)
            dve.wait_ge(bd_done, 1)
            for t in range(NT):
                for h in range(2):
                    last = nc.vector.tensor_tensor(x[:, t, 512 * h:512 * h + 512], x[:, t, 512 * h:512 * h + 512],
                                                   banks[2 * t + h][:, :], ALU.add)
            last.then_inc(bd_added, 1)

            def expert(it, first):
                k = [0]

                def chain(ins):
                    k[0] += 1
                    ins.then_inc(v_loop_step, 1)
                    dve.wait_ge(v_loop_step, it * CHAIN + k[0])
                e = it if isinstance(it, int) else it & (E - 1)
                rv = route[:, :].rearrange("p (s j) -> p s j", j=4)
                rcols = rv[:, it:it + 2, :] if isinstance(it, int) else rv[:, bass.ds(it, 2), :]
                chain(nc.vector.tensor_copy(now.rearrange("p (s j) -> p s j", j=4), rcols))
                dve.wait_ge(gathered, it + 1)
                for t in range(NT):
                    last = nc.vector.tensor_scalar(hot[:, t, :], slot_no[:, :], now[:, 4 + t:5 + t], None, ALU.is_equal)
                last.then_inc(hot_made, 1)
                if not first:
                    dve.wait_ge(hotw_turned, it)
                for t in range(NT):
                    last = nc.vector.tensor_scalar(hotw[:, t, :, :], slot_no[:, :].unsqueeze(1).to_broadcast([P, 2, C]),
                                                   now[:, t:t + 1], now[:, 2 + t:3 + t], ALU.is_equal, ALU.mult)
                last.then_inc(hotw_made, 1)
                if not first:
                    add_rows(it - 1)
                dve.wait_ge(mat_done["gate"], it + 1)
                nc.vector.tensor_scalar(e_g, banks[1][:, :], LIMIT, None, ALU.min).then_inc(g_made, 1)
                dve.wait_ge(mat_done["up"], it + 1)
                nc.vector.tensor_scalar(e_u, banks[2][:, :], LIMIT, -LIMIT, ALU.min, ALU.max).then_inc(up_read, 1)
                dve.wait_ge(up_read, it + 1)
                dve.wait_ge(g_made, it + 1)
                chain(nc.vector.scalar_tensor_tensor(out=e_u, in0=e_u, scalar=1.0, in1=e_g, op0=ALU.add, op1=ALU.mult))
                dve.wait_ge(sig_made, it + 1)
                nc.vector.tensor_tensor(e_h, e_u, e_sig, ALU.mult).then_inc(eh_made, 1)
                next_sel(it, chain)
                dve.wait_ge(eh_turned, it + 1)
                nc.vector.tensor_copy(e_hT, bank45[:, 0, :].rearrange("p (k h s) -> p k h s", h=2, s=C)).then_inc(ehT_made, 1)
                keep_x(it + 1)
                assert k[0] == CHAIN

            def next_sel(it, chain):
                e1 = (it + 1) & (E - 1)
                col_e = ident[0:E, e1:e1 + 1] if isinstance(e1, int) else ident[0:E, bass.ds(e1, 1)]
                chain(nc.vector.tensor_copy(e_sel, col_e.to_broadcast([E, C])))

            def keep_x(i):
                dve.wait_ge(gathered, i + 1)
                nc.vector.tensor_tensor(e_x, banks[0][:, :].rearrange("p (k s) -> p k s", s=C), col(vcol[:, R_GM:R_GM + KD], C), ALU.mult).then_inc(ex_made, 1)

            def add_rows(i):
                for j in range(4):
                    t, h = j // 2, j % 2
                    dve.wait_ge(spread_done, i * 4 + j + 1)
                    ins = nc.vector.tensor_tensor(x[:, t, 512 * h:512 * h + 512], x[:, t, 512 * h:512 * h + 512],
                                                  bank67[:, j % 2, :], ALU.add)
                    if j != 2:
                        ins.then_inc(rows_added if j == 3 else added, 1)
            dve.wait_ge(route_made, 1)
            total = dve.value_load(total_i[0:1, 0:1], min_val=E, max_val=ROUNDS * E)
            for t in range(NT):
                last = nc.vector.tensor_scalar(hot[:, t, :], slot_no[:, :], rv0[:, t:t + 1], None, ALU.is_equal)
            last.then_inc(hot_made, 1)
            step(nc.vector.tensor_copy(e_sel, ident[0:E, 0:1].to_broadcast([E, C])))
            keep_x(0)
            expert(0, True)
            with dve.Fori(1, total) as it:
                expert(it, False)
            add_rows(dve.value_load(total_i[0:1, 1:2], min_val=E - 1, max_val=ROUNDS * E - 1))

        @block.tensor
        def _(pe):
            mm = nc.tensor.matmul

            def turn_rows(bank_list):
                for j in range(4):
                    for k in range(2):
                        for t in range(NT):
                            last = nc.tensor.transpose(bank_list[j][:, 256 * k + P * t:256 * k + P * t + P],
                                                       xn[:, t, P * (2 * j + k):P * (2 * j + k) + P], ident[:, :])
                return last
            pe.wait_ge(consts_made, 1)
            pe.wait_ge(vec_in, 16 * 13)
            nc.tensor.transpose(TB[0][:, 0:R_ALL], vrow[:, :], ident[0:R_ALL, 0:R_ALL]).then_inc(vec_turned, 1)
            pe.wait_ge(xn_made, NT)
            turn_rows([PJ[0], PJ[1], S[0], S[1]]).then_inc(xn_turned, 1)
            pe.wait_ge(hT_made, 4)
            pe.wait_ge(consts_made, 2)
            pe.wait_ge(small_in, 16 * 8)

            def project(i, name, n):
                ps, t = PJ[i % 2], i % 2
                if i >= 2:
                    pe.wait_ge(proj_read_a, i - 1)
                    pe.wait_ge(proj_read_v, min(i - 1, 10))
                wait_block(pe, name)
                w = view[name]
                for k in range(KD):
                    last = mm(ps[:, 0:n], hT[:, k, P * t:P * t + P], w[:, k, :], start=(k == 0), stop=(k == KD - 1))
                if name == "kw":
                    last = mm(ps[:, 256:288], ones[0:1, :], brow[:, 0:32], start=False, stop=True, skip_group_check=True)
                last.then_inc(proj_done, 1)

            project(0, "kv", 512)
            project(1, "kv", 512)
            project(2, "kw", 288)
            project(3, "kw", 288)
            pe.wait_ge(vec_kept, 1)
            pe.wait_ge(proj_read_a, 2)
            for v in range(2):
                for g in range(G):
                    for t in range(NT):
                        last = nc.tensor.transpose(TB[v][:, 256 * g + P * t:256 * g + P * t + P],
                                                   (kc_dup, vc_dup)[v][:, t, g].rearrange("p u d -> p (u d)"), ident[:, :])
                last.then_inc(kv_turned, 1)
            project(4, "q", 512)
            project(5, "q", 512)
            for v, name in enumerate(("ck1", "cv1")):
                pe.wait_ge(blk_made, v + 1)
                wait_block(pe, name)
                for c in range(2):
                    for m in range(16):
                        last = mm(S[0][:, 64 * v + 32 * c:64 * v + 32 * c + 32], view[name][:, m, P * c:P * c + P],
                                  blk[v][:, m, :, :].rearrange("p g i -> p (g i)"), start=(m == 0), stop=(m == 15))
                last.then_inc(hid_done, 1)
            project(6, "fk", 512)
            project(7, "fk", 512)
            pe.wait_ge(hid_made, 1)
            for v in range(2):
                for g in range(G):
                    c0 = P * v + DH * g
                    for c in range(2):
                        mm(S[1][0:NC, c0:c0 + DH], hid[:, v, c, NC * g:NC * g + NC], w_c2[:, v, c, :], start=(c == 0), stop=False)
                    b0 = (B_CK2, B_CV2)[v]
                    last = mm(S[1][0:NC, c0:c0 + DH], ones[0:1, 0:NC], brow[:, b0:b0 + DH], start=False, stop=True)
            last.then_inc(ck_done, 1)
            pe.wait_ge(f_neg, 1)
            mm(OB[0][:, 0:8], upto[:, :], fb[:, 0, :], start=True, stop=True)
            mm(OB[0][:, 8:16], ones[:, :], fb[:, 0, :], start=True, stop=False)
            mm(OB[0][:, 8:16], upto[:, :], fb[:, 1, :], start=False, stop=True).then_inc(f_summed, 1)
            project(8, "fq", 512)
            project(9, "fq", 512)
            pe.wait_ge(ck_kept, 1)
            for g in range(G):
                nc.tensor.transpose(OB[1][0:DE, NC * g:NC * g + NC], ck65[:, g, :], ident[0:NC, 0:NC])
            mm(S[1][:, 0:P], spread[:, :], vc16, start=True, stop=True).then_inc(ck_turned, 1)
            project(10, "fv", 512)
            project(11, "fv", 512)

            def turn_heads(u):
                src, dst, h0, gain = UNITS[u]
                if u >= 2:
                    pe.wait_ge((kept_a, kept_v)[u % 2], u // 2)
                for h in range(2):
                    for t in range(NT):
                        last = nc.tensor.transpose(TB[u % 2][0:DE, 256 * h + P * t:256 * h + P * t + P],
                                                   src[:, t, h0 + h, :], ident[:, :])
                last.then_inc(turned, 1)
            pe.wait_ge(blk_made, 2)
            pe.wait_ge(proj_read_v, 10)
            pe.wait_ge(f_placed, 1)
            for u in range(6):
                turn_heads(u)
            pe.wait_ge(ck_ready, 1)
            pe.wait_ge(kept_a, 2)
            pe.wait_ge(kept_v, 2)
            for t in range(NT):
                for h in range(HN):
                    last = mm(S[0][:, P * t + NC * h:P * t + NC * h + NC], qT[:, h, P * t:P * t + P], kcT[:, h // 4, :],
                              start=True, stop=True)
            last.then_inc(cs_done, 1)
            for u in range(6, len(UNITS)):
                turn_heads(u)
            pe.wait_ge(cp_made, 1)
            for t in range(NT):
                last = nc.tensor.transpose(S[1][:, P * t:P * t + P], cp[:, P * t:P * t + P], ident[:, :])
            last.then_inc(cp_turned, 1)
            pe.wait_ge(cpT_made, 1)
            for t in range(NT):
                last = mm(OB[t], cpT[:, t, :], v_block.rearrange("p h d -> p (h d)"), start=True, stop=True)
            last.then_inc(co_done, 1)

            MAPS = [(qT, kwT, vw, h, h // 4) for h in range(HN)] + [(qT, ksT, vs, h, h // 4) for h in range(HN)] \
                + [(fqT, fkT, fv, h, h) for h in range(HF)]

            def scores(m):
                q, k, _, h, g = MAPS[m]
                if m >= 2:
                    pe.wait_ge(s_max, m - 1)
                mm(S[m % 2][:, 0:P], q[:, h, 0:P], k[:, g, 0:P], start=True, stop=True)
                mm(S[m % 2][:, P:384], q[:, h, P:T], k[:, g, :], start=True, stop=True).then_inc(s_done, 1)

            def turn_p(m):
                pe.wait_ge(p_made, m + 1)
                if m >= 2:
                    pe.wait_ge(pT_made, m - 1)
                for j in range(3):
                    last = nc.tensor.transpose(TB[m % 2][:, P * j:P * j + P], pr[m % 2][:, P * j:P * j + P], ident[:, :])
                last.then_inc(p_turned, 1)

            def values(m):
                _, _, v, h, g = MAPS[m]
                pe.wait_ge(pT_made, m + 1)
                if h == 0:
                    if m == 0:
                        pe.wait_ge(co_kept, 1)
                    else:
                        pe.wait_ge(o_kept, m // 8)
                pt, c = prT[m % 2], DH * h
                mm(OB[0][:, c:c + DH], pt[:, 0:P], v[:, 0, g, :], start=True, stop=True)
                mm(OB[1][:, c:c + DH], pt[:, P:2 * P], v[:, 0, g, :], start=True, stop=False)
                last = mm(OB[1][:, c:c + DH], pt[:, 2 * P:384], v[:, 1, g, :], start=False, stop=True)
                if h == 7:
                    last.then_inc(o_done, 1)

            def merge(c):
                name = f"merge{c // 4}"
                if c >= 2:
                    pe.wait_ge(merge_made, c - 1)
                wait_block(pe, name)
                for k in range(KD):
                    last = mm(PJ[c % 2][:, 0:T], view[name][:, k, P * (c % 4):P * (c % 4) + P], hT[:, k, :],
                              start=(k == 0), stop=(k == KD - 1))
                last.then_inc(merge_done, 1)
            pe.wait_ge(kept_a, 7)
            pe.wait_ge(kept_v, 7)
            pe.wait_ge(proj_read_a, 12)
            for m in range(26):
                if m < 24:
                    scores(m)
                if m < 16:
                    merge(m)
                if 1 <= m <= 24:
                    turn_p(m - 1)
                if m >= 2:
                    values(m - 2)
            pe.wait_ge(s_max, 24)
            pe.wait_ge(pT_made, 24)
            for mix in range(2):
                pe.wait_ge(o_kept, (2, 3)[mix])
                for j in range(2):
                    for k in range(2):
                        for t in range(NT):
                            c = P * (2 * j + k)
                            last = nc.tensor.transpose((S, TB)[mix][j][:, 256 * k + P * t:256 * k + P * t + P],
                                                       (o_nsa, o_fox)[mix][:, t, c:c + P], ident[:, :])
                    last.then_inc(o_turned, 1)
            pe.wait_ge(oT_made, 4)
            pe.wait_ge(merge_made, 16)
            for c in range(KD):
                if c >= 2:
                    pe.wait_ge(y_made, c - 1)
                for mix, name in enumerate(("up_nsa", "up_fox")):
                    wait_block(pe, name)
                    for k in range(4):
                        last = mm(PJ[c % 2][:, T * mix:T * mix + T], view[name][:, k, P * c:P * c + P], oT[mix][:, k, :],
                                  start=(k == 0), stop=(k == 3))
                last.then_inc(up_done, 1)
            for half in range(2):
                wait_block(pe, f"out{half}")
                for k in range(4):
                    kk = 4 * half + k
                    pe.wait_ge(y_made, KD)
                    for t in range(NT):
                        for h in range(2):
                            last = mm((S, TB)[t][h][:, :], yT[:, kk, P * t:P * t + P], view[f"out{half}"][:, k, 512 * h:512 * h + 512],
                                      start=(kk == 0), stop=(kk == KD - 1), skip_group_check=True)
                last.then_inc(out_done, 1)
            pe.wait_ge(x1_made, NT)
            turn_rows([PJ[0], PJ[1], OB[0], OB[1]]).then_inc(xn_turned, 1)
            pe.wait_ge(hT_made, 8)
            for t in range(NT):
                for k in range(KD):
                    mm(TB[0][:, E * t:E * t + E], hT[:, k, P * t:P * t + P], w_r[:, k, :], start=(k == 0), stop=False)
                last = mm(TB[0][:, E * t:E * t + E], ones[0:1, :], brow[:, B_ROUTER:B_ROUTER + E], start=False, stop=True)
            last.then_inc(lg_done, 1)
            pe.wait_ge(sel_made, 1)
            mm(TB[1][:, 0:E], before[:, :], chosen[:, 0, :], start=True, stop=True)
            mm(TB[1][:, E:2 * E], ones[:, :], chosen[:, 0, :], start=True, stop=False)
            mm(TB[1][:, E:2 * E], before[:, :], chosen[:, 1, :], start=False, stop=True)
            mm(TB[1][:, 2 * E:3 * E], ones[:, :], chosen[:, 0, :], start=True, stop=False)
            mm(TB[1][:, 2 * E:3 * E], ones[:, :], chosen[:, 1, :], start=False, stop=True).then_inc(pos_done, 1)
            pe.wait_ge(sel_made, 3)
            for t in range(NT):
                last = nc.tensor.transpose(OB[0][0:E, P * t:P * t + P], comb[:, t, :], ident[:, :])
            last.then_inc(comb_turned, 1)
            pe.wait_ge(combT_made, 1)
            pe.wait_ge(bdown_in, 16)
            for t in range(NT):
                for h in range(2):
                    last = mm(banks[2 * t + h][:, :], combT[:, t, :], b_down[:, 512 * h:512 * h + 512], start=True, stop=True)
            last.then_inc(bd_done, 1)

            def gather(i):
                pe.wait_ge(hot_made, i + 1)
                for k in range(KD):
                    for t in range(NT):
                        last = mm(banks[0][:, C * k:C * k + C], xn[:, t, P * k:P * k + P], hot[:, t, :], start=(t == 0), stop=(t == NT - 1))
                last.then_inc(gathered, 1)

            def product(m, bank, lhs, it, halves=(0, 1)):
                biased = m != "down"
                for h in halves:
                    if h == 0 and biased:
                        for half in range(2):
                            mm(bank[C * half:C * half + C, :], e_sel, e_rows[:, (m == "up") * 1, 512 * half:512 * half + 512],
                               start=True, stop=False)
                    s = ex_half[m][h]
                    pe.wait_ge(ring_in[s], n_in[s] + 16 + it * 16)
                    w = ring[:, s, :].rearrange("p (k n) -> p k n", k=4)
                    for k in range(4):
                        kk = 4 * h + k
                        for half in range(2):
                            last = mm(bank[C * half:C * half + C, :], lhs(kk), w[:, k, 512 * half:512 * half + 512],
                                      start=(kk == 0 and not biased), stop=(kk == KD - 1))
                    last.then_inc((half_done, mat_done)[h][m], 1)

            def scatter(i):
                pe.wait_ge(y_kept, i + 1)
                pe.wait_ge(hotT_made, i + 1)
                for j in range(4):
                    t, h = j // 2, j % 2
                    if j >= 2:
                        pe.wait_ge(added, i * 2 + j - 1)
                    mm(bank67[:, j % 2, :], hotT[C * h:C * h + C, t, :], e_y[C * h:C * h + C, :], start=True, stop=True).then_inc(spread_done, 1)

            def x_of(kk):
                return e_x[:, kk, :]

            def h_of(kk):
                return e_hT[:, kk % 4, kk // 4, :]

            def expert(it, first):
                pe.wait_ge(ex_made, it + 1)
                product("gate", banks[1], x_of, it, (0,))
                if not first:
                    scatter(it - 1)
                product("gate", banks[1], x_of, it, (1,))
                product("up", banks[2], x_of, it)
                gather(it + 1)
                pe.wait_ge(hotw_made, it + 1)
                for t in range(NT):
                    last = nc.tensor.transpose(bank45[:, 1, P * t:P * t + P], hotw[:, t, :, :].rearrange("p u s -> p (u s)"), ident[:, :])
                last.then_inc(hotw_turned, 1)
                pe.wait_ge(eh_made, it + 1)
                for k in range(4):
                    last = nc.tensor.transpose(bank45[:, 0, P * k:P * k + P], e_h[:, P * k:P * k + P], ident[:, :])
                last.then_inc(eh_turned, 1)
                pe.wait_ge(ehT_made, it + 1)
                product("down", banks[3], h_of, it)
            pe.wait_ge(bd_added, 1)
            pe.wait_ge(ebias_in, 32)
            pe.wait_ge(route_made, 1)
            total = pe.value_load(total_i[0:1, 0:1], min_val=E, max_val=ROUNDS * E)
            last_step = pe.value_load(total_i[0:1, 1:2], min_val=E - 1, max_val=ROUNDS * E - 1)
            gather(0)
            expert(0, True)
            with pe.Fori(1, total) as it:
                expert(it, False)
            scatter(last_step)


_INS = ['x', 'g_attn', 'w_in', 'qn_nsa', 'kn_cmp', 'kn_sel', 'kn_win', 'pos_cmp_k', 'w_ck1', 'b_ck1', 'w_ck2', 'b_ck2',
        'pos_cmp_v', 'w_cv1', 'b_cv1', 'w_cv2', 'b_cv2', 'b_nsa_gate', 'qn_fox', 'kn_fox', 'b_forget', 'w_up_nsa',
        'w_up_fox', 'b_merge', 'w_out', 'g_mlp', 'w_router', 'b_router', 'w_e_gate', 'b_e_gate', 'w_e_up', 'b_e_up',
        'w_e_down', 'b_e_down']


def kernel(**inputs):
    import numpy as _np
    import concourse.bacc as _bacc
    from concourse import mybir as _mybir
    from concourse.bass_utils import run_bass_kernel_spmd as _run

    nc = _bacc.Bacc("TRN2", target_bir_lowering=False, num_devices=1)
    arrays, args = {}, {}
    for name in _INS:
        v = _np.ascontiguousarray(inputs[name])
        arrays[f"in_{name}_dram"] = v
        args[name] = nc.dram_tensor(f"in_{name}_dram", v.shape, _mybir.dt.from_np(v.dtype), kind="ExternalInput").ap()
    out = nc.dram_tensor("out_0_dram", inputs["x"].shape, _mybir.dt.float32, kind="ExternalOutput").ap()
    build(nc, args, out)
    r = _run(nc, [arrays], core_ids=[0])
    return r.results[0]["out_0_dram"]
```

```python
from contextlib import ExitStack

import concourse.bass as bass
from concourse import mybir

ALU = mybir.AluOpType
ACT = mybir.ActivationFunctionType
F32 = mybir.dt.float32
I32 = mybir.dt.int32
AX = mybir.AxisListType

P = 128
T = 256
NT = T // P
D = 1024
KD = D // P
DH = 64
DE = DH + 1
HN = 8
G = 2
HF = 8
NC = 16
CMP_BLOCK, CMP_STRIDE = 32, 16
E = 32
C = 64
ROUNDS = T // C
TOPK = 4
EPS = 1e-6
NEG = -1e30
SCALE = DH ** -0.5
LIMIT, SWISH = 7.0, 1.702
SLOTS = 6
EX_SLOTS = 8
STEPS = 4
SLOPES = [2.0 ** (-8.0 * (h + 1) / HN) for h in range(HN)]

C_Q, C_KV = 0, 512
C_KW, C_GATE = 1024, 1280
C_FQ, C_FK, C_FV, C_FL, C_MERGE = 1304, 1816, 2328, 2840, 2848

R_GA, R_GM, R_PK, R_PV, R_BK1, R_BV1, R_BM = 0, 8, 16, 32, 48, 50, 52
R_QN, R_KC, R_KS, R_KW, R_QF, R_KF, R_ALL = 68, 69, 70, 71, 72, 73, 74
B_GATE, B_CK2, B_CV2, B_ROUTER, B_ALL = 0, 32, 96, 160, 192


def build(nc, a, out):
    with ExitStack() as ctx:
        def sb(name, shape, dt=F32):
            return ctx.enter_context(nc.sbuf_tensor(name, shape, dt))

        def sem(name):
            return ctx.enter_context(nc.semaphore(name))

        banks = [ctx.enter_context(nc.psum_tensor(f"bank{i}", [P, 512], F32)) for i in range(4)]
        bank45 = ctx.enter_context(nc.psum_tensor("bank45", [P, 2, 512], F32))
        bank67 = ctx.enter_context(nc.psum_tensor("bank67", [P, 2, 512], F32))
        PJ = [banks[0], banks[1]]
        S = [banks[2], banks[3]]
        TB = [bank45[:, 0, :], bank45[:, 1, :]]
        OB = [bank67[:, 0, :], bank67[:, 1, :]]

        ring = sb("ring", [P, EX_SLOTS, 4096])
        x = sb("x", [P, NT, D])
        xn = sb("xn", [P, NT, D])
        hT = sb("hT", [P, KD, T])
        rows = ring[:, 7, :]
        heads = sb("heads", [P, 7168])
        late = ring[:, 6, :]
        work = sb("work", [P, 2304])
        vrow = sb("vrow", [R_ALL, P])
        vcol = sb("vcol", [P, R_ALL])
        scaled = sb("scaled", [P, 18])
        brow = sb("brow", [1, B_ALL])
        w_c2 = sb("w_c2", [P, 2, 2, DH])
        w_r = sb("w_r", [P, KD, E])
        ident = sb("ident", [P, P])
        causal = sb("causal", [P, T])
        before = sb("before", [P, P])
        upto = sb("upto", [P, P])
        ones = sb("ones", [P, P])
        spread = sb("spread", [NC, P])
        own_head = sb("own_head", [P, HN])
        cmask = sb("cmask", [P, NT, NC])
        cneg = sb("cneg", [P, NT, NC])
        slot_no = sb("slot_no", [P, C])
        t_pos = sb("t_pos", [P, NT])
        small = sb("small", [P, 760])
        route = sb("route", [P, (ROUNDS * E + 1 + STEPS) * 4])
        in_tile = sb("in_tile", [P, NT * E])
        round_off = sb("round_off", [P, ROUNDS])
        total_i = sb("total_i", [1, 2], I32)

        def tok(off, n):
            return rows[:, off:off + NT * n * DE].rearrange("p (t h d) -> p t h d", t=NT, h=n)
        o = 0
        q_tok = tok(o, HN); o += NT * HN * DE
        ks_tok = tok(o, G); o += NT * G * DE
        kw_tok = tok(o, G); o += NT * G * DE
        fq_tok = tok(o, HF); o += NT * HF * DE
        fk_tok = tok(o, HF)
        o_nsa = rows[:, 0:1024].rearrange("p (t n) -> p t n", t=NT)
        o_fox = rows[:, 1024:2048].rearrange("p (t n) -> p t n", t=NT)
        oT = [rows[:, 2048 + 1024 * m:3072 + 1024 * m].rearrange("p (k t) -> p k t", t=T) for m in range(2)]
        xflat = xn[:, :, :].rearrange("p t n -> p (t n)")
        vs = xflat[:, 0:256].rearrange("p (t g d) -> p t g d", t=NT, g=G)
        vw = xflat[:, 256:512].rearrange("p (t g d) -> p t g d", t=NT, g=G)
        fv = xflat[:, 512:1536].rearrange("p (t h d) -> p t h d", t=NT, h=HF)
        kc_dup = xflat[:, 1536:2048].rearrange("p (t g u d) -> p t g u d", t=NT, g=G, u=2)
        vc_dup = late[:, 2048:2560].rearrange("p (t g u d) -> p t g u d", t=NT, g=G, u=2)
        e_rows = hT[0:E, :, :].rearrange("p k t -> p (k t)").rearrange("p (m n) -> p m n", m=2)
        v_block = late[:, 2560:3072].rearrange("p (h d) -> p h d", h=HN)
        mergeT = late[:, :].rearrange("p (c t) -> p c t", t=T)
        def feat(off, n):
            return heads[0:DE, off:off + n * T].rearrange("p (h t) -> p h t", t=T)
        qT, ksT, kwT = feat(0, HN), feat(2048, G), feat(2560, G)
        fqT, fkT = feat(3072, HF), feat(5120, HF)
        yT = heads[:, 0:2048].rearrange("p (k t) -> p k t", t=T)

        def hb(off, n=512):
            return heads[:, off:off + n]
        e_x = hb(2048).rearrange("p (k s) -> p k s", s=C)
        e_g, e_sig, e_u, e_h, e_y = (hb(2560 + 512 * i) for i in range(5))
        e_hT = hb(5120).rearrange("p (k h s) -> p k h s", h=2, s=C)
        b_down = heads[0:E, 6144:7168]
        sq = [work[:, 512 * i:512 * i + 512] for i in range(2)]
        blk = [work[:, 1024 + 512 * i:1536 + 512 * i].rearrange("p (m g i) -> p m g i", m=16, g=G) for i in range(2)]
        sm = [work[:, 384 * i:384 * i + 384] for i in range(2)]
        pr = [work[:, 768 + 384 * i:1152 + 384 * i] for i in range(2)]
        prT = [work[:, 1536 + 384 * i:1920 + 384 * i] for i in range(2)]

        cur = [0]
        def sm_(n, shape=None, **kw):
            v = small[:, cur[0]:cur[0] + n]
            cur[0] += n
            assert cur[0] <= 760
            return v.rearrange(shape, **kw) if shape else v
        ss = sm_(2); rr = sm_(2); minus_half = sm_(8)
        ssq = sm_(8); rrq = sm_(8)
        gates = sm_(64, "p (t n) -> p t n", t=NT)
        gate = sm_(48, "p (t n) -> p t n", t=NT)
        fa = sm_(16, "p (t h) -> p t h", t=NT); fb = sm_(16, "p (t h) -> p t h", t=NT)
        mx = sm_(4, "p (b t) -> p b t", t=NT); nmx = sm_(4, "p (b t) -> p b t", t=NT)
        sums = sm_(48, "p (n t) -> p n t", t=NT)
        rg = sm_(16, "p (t h) -> p t h", t=NT)
        csum = sm_(16); ck_ss = sm_(2); ck_r = sm_(2)
        lg = sm_(64, "p (t e) -> p t e", t=NT); top8 = sm_(16, "p (t e) -> p t e", t=NT)
        above = sm_(64, "p (t e) -> p t e", t=NT)
        tot = sm_(8)
        b_router = sm_(E)
        now = sm_(8)
        assert cur[0] <= 760
        hid = late[:, 3072:3200].rearrange("p (v c n) -> p v c n", v=2, c=2)
        hid_a, hid_b = late[:, 3200:3328], late[:, 3328:3456]
        ck65 = late[0:NC, 3456:3456 + G * DE].rearrange("p (g d) -> p g d", g=G)
        ck_sq = late[0:NC, 3600:3728]
        vc16 = late[0:NC, 3728:3856]
        kcT = late[0:DE, 3856:3888].rearrange("p (g c) -> p g c", g=G)
        cp = work[:, 1024:1280]
        cpT = work[:, 1280:1536].rearrange("p (t q) -> p t q", t=NT)
        tmp_br = xflat[:, 1536:2048]
        tmp_up = work[:, 0:T]
        equal = work[:, 256:320].rearrange("p (t e) -> p t e", t=NT)
        count = work[:, 320:384].rearrange("p (t e) -> p t e", t=NT)
        chosen = work[:, 384:448].rearrange("p (t e) -> p t e", t=NT)
        comb = work[:, 448:512].rearrange("p (t e) -> p t e", t=NT)
        hot = work[:, 512:640].rearrange("p (t s) -> p t s", t=NT)
        hotw = work[:, 640:896].rearrange("p (t u s) -> p t u s", t=NT, u=2)
        hotT = work[:, 896:1152].rearrange("p (t q) -> p t q", t=NT)
        combT = work[0:E, 1152:1408].rearrange("p (t q) -> p t q", t=NT)
        e_sel = work[0:E, 1408:1472]
        rv0 = route[:, 0:4]
        logits = work[:, 1472:1536].rearrange("p (t e) -> p t e", t=NT)

        x_in = [sem(f"x_in{t}") for t in range(NT)]
        vec_in, small_in, ebias_in, bdown_in, out_sent = map(sem, (
            "vec_in", "small_in", "ebias_in", "bdown_in", "out_sent"))
        ring_in = [sem(f"ring_in{i}") for i in range(EX_SLOTS)]
        vrow_set, pool_step, consts_made = map(sem, ("vrow_set", "pool_step", "consts_made"))
        mean_made, inv_made = sem("mean_made"), sem("inv_made")
        v_step, a_step, v_loop_step = sem("vector_step"), sem("scalar_step"), sem("vector_loop_step")
        vec_turned, vec_kept = sem("vec_turned"), sem("vec_kept")
        xn_made, xn_turned, hT_made = sem("xn_made"), sem("xn_turned"), sem("hT_made")
        proj_done, proj_read_a, proj_read_v = sem("proj_done"), sem("proj_read_a"), sem("proj_read_v")
        gates_kept, gates_tanh, f_abs, f_exp, f_ln, f_neg = map(sem, (
            "gates_kept", "gates_tanh", "f_abs", "f_exp", "f_ln", "f_neg"))
        f_summed, f_placed = sem("f_summed"), sem("f_placed")
        kv_turned, blk_made, hid_done, hid_in, hid_tanh, hid_made, hid_rows, hid_turned = map(sem, (
            "kv_turned", "blk_made", "hid_done", "hid_in", "hid_tanh", "hid_made", "hid_rows", "hid_turned"))
        ck_done, ck_kept, ck_turned, ck_ready = map(sem, ("ck_done", "ck_kept", "ck_turned", "ck_ready"))
        turned, kept_a, kept_v = sem("turned"), sem("kept_a"), sem("kept_v")
        cs_done, cs_max, cs_exp, cp_made, cp_turned, cpT_made, co_done, co_kept = map(sem, (
            "cs_done", "cs_max", "cs_exp", "cp_made", "cp_turned", "cpT_made", "co_done", "co_kept"))
        s_done, s_max, p_made, p_turned, pT_made, o_done, o_kept = map(sem, (
            "s_done", "s_max", "p_made", "p_turned", "pT_made", "o_done", "o_kept"))
        merge_done, merge_made = sem("merge_done"), sem("merge_made")
        o_turned, oT_made, up_done, y_made, out_done, x1_made = map(sem, (
            "o_turned", "oT_made", "up_done", "y_made", "out_done", "x1_made"))
        squared, xn_ready, summed, lg_moved, lg_exp, comb_made = map(sem, ("squared", "xn_ready", "summed", "lg_moved", "lg_exp", "comb_made"))
        lg_done, sel_made, pos_done, route_made, comb_turned, combT_made, bd_done, bd_added = map(sem, (
            "lg_done", "sel_made", "pos_done", "route_made", "comb_turned", "combT_made", "bd_done", "bd_added"))
        hot_made, gathered, ex_made = sem("hot_made"), sem("gathered"), sem("ex_made")
        hotw_made, hotw_turned, hotT_made = sem("hotw_made"), sem("hotw_turned"), sem("hotT_made")
        half_done = {m: sem(f"expert_{m}_half_done") for m in ("gate", "up", "down")}
        mat_done = {m: sem(f"expert_{m}_done") for m in ("gate", "up", "down")}
        g_made, sig_made, up_read, eh_made, eh_turned, ehT_made = map(sem, (
            "g_made", "sig_made", "up_read", "eh_made", "eh_turned", "ehT_made"))
        y_kept, spread_done, added, rows_added = map(sem, (
            "y_kept", "spread_done", "added", "rows_added"))

        def gain_of(r):
            return vcol[:, r:r + 1]
        UNITS = [(q_tok, qT, 2 * i, scaled[:, 16:17]) for i in range(4)] \
            + [(ks_tok, ksT, 0, gain_of(R_KS)), (kw_tok, kwT, 0, gain_of(R_KW))] \
            + [(fk_tok, fkT, 2 * i, gain_of(R_KF)) for i in range(4)] \
            + [(fq_tok, fqT, 2 * i, scaled[:, 17:18]) for i in range(4)]
        MERGE_AT = {m: i for i, m in enumerate(m for m in range(24) if m % 3 != 2)}
        INVERTED = [rr[:, 0:1], rr[:, 1:2]] + [rrq[:, 0:G]] * 4 + [rrq] * 4 + [ck_r[0:NC, :]] + [rrq] * 2 \
            + [rr[:, 0:1], rr[:, 1:2]]
        N_INV = len(INVERTED)
        CHAIN = 3

        block = ctx.enter_context(nc.Block())

        w_in = a["w_in"][0].rearrange("(k p) n -> p k n", p=P)

        def in_cols(c0, n):
            return [(w_in[:, :, c0:c0 + n], 0, n)]
        BLOCKS = [
            ("kv", in_cols(C_KV, 512), 8, 512),
            ("kw", in_cols(C_KW, 280) + [(w_in[:, :, C_FL:C_FL + 8], 280, 8)], 8, 288),
            ("q", in_cols(C_Q, 512), 8, 512),
            ("ck1", [(a["w_ck1"][0].rearrange("(m p) n -> p m n", p=P), 0, 256)], 16, 256),
            ("cv1", [(a["w_cv1"][0].rearrange("(m p) n -> p m n", p=P), 0, 256)], 16, 256),
            ("fk", in_cols(C_FK, 512), 8, 512),
            ("fq", in_cols(C_FQ, 512), 8, 512),
            ("fv", in_cols(C_FV, 512), 8, 512),
        ] + [(f"merge{i}", in_cols(C_MERGE + 512 * i, 512), 8, 512) for i in range(4)] + [
            ("up_nsa", [(a["w_up_nsa"][0].rearrange("(k p) n -> p k n", p=P), 0, 1024)], 4, 1024),
            ("up_fox", [(a["w_up_fox"][0].rearrange("(k p) n -> p k n", p=P), 0, 1024)], 4, 1024),
            ("out0", [(a["w_out"][0].rearrange("(k p) n -> p k n", p=P)[:, 0:4, :], 0, 1024)], 4, 1024),
            ("out1", [(a["w_out"][0].rearrange("(k p) n -> p k n", p=P)[:, 4:8, :], 0, 1024)], 4, 1024),
        ]
        FIRST = (SLOTS - len(BLOCKS) % SLOTS) % SLOTS
        slot_of = {b[0]: (FIRST + i) % SLOTS for i, b in enumerate(BLOCKS)}
        view, arrives, n_in = {}, {}, [0] * EX_SLOTS
        for name, pieces, k, n in BLOCKS:
            s = slot_of[name]
            view[name] = ring[:, s, 0:k * n].rearrange("p (k n) -> p k n", k=k)
            n_in[s] += 16 * len(pieces)
            arrives[name] = (s, n_in[s])
        freed = {"kv": (proj_done, 2), "kw": (proj_done, 4), "q": (proj_done, 6), "ck1": (hid_done, 1),
                 "cv1": (hid_done, 1), "fk": (proj_done, 8), "fq": (proj_done, 10), "fv": (proj_done, 12)}
        for i in range(4):
            freed[f"merge{i}"] = (merge_done, 4 * i + 4)
        freed |= {"up_nsa": (up_done, KD), "up_fox": (up_done, KD), "out0": (out_done, 2), "out1": (out_done, 4)}

        def wait_block(eng, name):
            s, v = arrives[name]
            eng.wait_ge(ring_in[s], v)

        EX_BLOCKS = [(m, h) for m in ("gate", "up", "down") for h in range(2)]

        def ex_slot(u, m, h):
            j = len(EX_BLOCKS) * u + EX_BLOCKS.index((m, h))
            return j % EX_SLOTS, j // EX_SLOTS + 1
        fills = len(EX_BLOCKS) * STEPS // EX_SLOTS
        ex_src = {"gate": "w_e_gate", "up": "w_e_up", "down": "w_e_down"}

        def col(ap, n):
            return ap.unsqueeze(2).to_broadcast([ap.shape[0], ap.shape[1], n])

        @block.sync
        def _(sp):
            for t in range(NT):
                sp.dma_start(x[:, t, :], a["x"][0, P * t:P * t + P, :]).then_inc(x_in[t], 16)
            sp.wait_ge(vrow_set, 1)
            for r0, nr, name in ((R_GA, 8, "g_attn"), (R_GM, 8, "g_mlp"), (R_BK1, 2, "b_ck1"), (R_BV1, 2, "b_cv1"),
                                 (R_BM, 16, "b_merge")):
                sp.dma_start(vrow[r0:r0 + nr, :], a[name][0].rearrange("(r n) -> r n", r=nr)).then_inc(vec_in, 16)
            for r0, name in ((R_QN, "qn_nsa"), (R_KC, "kn_cmp"), (R_KS, "kn_sel"), (R_KW, "kn_win"),
                             (R_QF, "qn_fox"), (R_KF, "kn_fox")):
                sp.dma_start(vrow[r0:r0 + 1, 0:DH], a[name]).then_inc(vec_in, 16)
            for r0, name in ((R_PK, "pos_cmp_k"), (R_PV, "pos_cmp_v")):
                sp.dma_start(vrow[r0:r0 + 16, :], a[name][0].rearrange("(r u) d -> r (u d)", u=2)).then_inc(vec_in, 16)
            for i, (name, pieces, k, n) in enumerate(BLOCKS):
                if i >= SLOTS:
                    sp.wait_ge(*freed[BLOCKS[i - SLOTS][0]])
                for src, c0, w in pieces:
                    sp.dma_start(view[name][:, :, c0:c0 + w], src).then_inc(ring_in[slot_of[name]], 16)

            last = [b[0] for b in BLOCKS[-SLOTS:]]

            def expert_loads(base, u):
                it = base + u
                if isinstance(it, int):
                    e, now, prev = it, it, it - 1
                else:
                    e = sp.snap(sp.to_reg(it & (E - 1)), min_val=0, max_val=E - 1)
                    now, prev = sp.to_reg(it), sp.to_reg(it - 1)
                for b, (m, h) in enumerate(EX_BLOCKS):
                    src = a[ex_src[m]][0, bass.ds(e, 1)] if not isinstance(e, int) else a[ex_src[m]][0, e:e + 1]
                    src = src.rearrange("o (k p) n -> p (o k) n", p=P)
                    s = ex_slot(u, m, h)[0]
                    sp.wait_ge(vrow_set, 1)
                    if isinstance(it, int) and it == 0:
                        sp.wait_ge(*freed[last[b]])
                    elif isinstance(it, int) and it == 1 and b < 2:
                        sp.wait_ge(*((y_made, KD), (up_done, KD))[b])
                    else:
                        pm, ph = EX_BLOCKS[(b - EX_SLOTS) % len(EX_BLOCKS)]
                        sp.wait_ge((half_done, mat_done)[ph][pm], prev if b < 2 else now)
                    sp.dma_start(ring[:, s, :].rearrange("p (k n) -> p k n", k=4),
                                 src[:, 4 * h:4 * h + 4, :]).then_inc(ring_in[s], 16)
            for u in range(STEPS):
                expert_loads(0, u)
            with sp.Fori(STEPS, E, STEPS) as base:
                for u in range(STEPS):
                    expert_loads(base, u)
            sp.wait_ge(route_made, 1)
            total = sp.value_load(total_i[0:1, 0:1], min_val=E, max_val=ROUNDS * E)
            with sp.If(total > E):
                with sp.Fori(E, total, STEPS) as base:
                    for u in range(STEPS):
                        expert_loads(base, u)
            sp.wait_ge(rows_added, total)
            sp.dma_start(out[0].rearrange("(t p) n -> p t n", p=P), x[:, :, :]).then_inc(out_sent, 16)
            sp.wait_ge(out_sent, 16)

        @block.gpsimd
        def _(pool):
            n = [0]

            def step(ins):
                n[0] += 1
                ins.then_inc(pool_step, 1)
                pool.wait_ge(pool_step, n[0])
            nc.gpsimd.memset(vrow[:, :], 1.0).then_inc(vrow_set, 1)
            step(nc.gpsimd.memset(minus_half, -0.5))
            step(nc.gpsimd.memset(ident[:, :], 0.0))
            nc.gpsimd.affine_select(out=ident[:, :], in_=ident[:, :], compare_op=ALU.not_equal, fill=1.0,
                                    base=0, pattern=[[-1, P]], channel_multiplier=1).then_inc(consts_made, 1)
            step(nc.gpsimd.memset(ones[:, :], 1.0))
            nc.gpsimd.affine_select(out=upto[:, :], in_=ones[:, :], compare_op=ALU.is_ge, fill=0.0,
                                    base=0, pattern=[[1, P]], channel_multiplier=-1)
            nc.gpsimd.affine_select(out=before[:, :], in_=ones[:, :], compare_op=ALU.is_gt, fill=0.0,
                                    base=0, pattern=[[1, P]], channel_multiplier=-1)
            step(nc.gpsimd.memset(causal[:, :], 0.0))
            nc.gpsimd.affine_select(out=causal[:, :], in_=causal[:, :], compare_op=ALU.is_ge, fill=NEG,
                                    base=P, pattern=[[-1, T]], channel_multiplier=1)
            nc.gpsimd.iota(t_pos[:, :], pattern=[[P, NT]], base=0, channel_multiplier=1,
                           allow_small_or_imprecise_dtypes=True)
            nc.gpsimd.iota(slot_no[:, :], pattern=[[1, C]], base=0, channel_multiplier=0,
                           allow_small_or_imprecise_dtypes=True)
            nc.gpsimd.iota(round_off[:, :], pattern=[[-C, ROUNDS]], base=-1, channel_multiplier=0,
                           allow_small_or_imprecise_dtypes=True)
            nc.gpsimd.memset(route[:, ROUNDS * E * 4:], 0.0)
            step(nc.gpsimd.memset(in_tile[:, :], 1.0))
            nc.gpsimd.memset(in_tile[:, E:E + 1], 0.0)
            step(nc.gpsimd.memset(cmask[:, :, :], 1.0))
            step(nc.gpsimd.affine_select(out=cmask[:, :, :], in_=cmask[:, :, :], compare_op=ALU.is_ge, fill=0.0,
                                         base=1 - CMP_BLOCK, pattern=[[P, NT], [-CMP_STRIDE, NC]], channel_multiplier=1))
            nc.gpsimd.tensor_scalar(cneg[:, :, :], cmask[:, :, :], -1.0, -NEG, ALU.add, ALU.mult)
            step(nc.gpsimd.memset(spread[:, :], 0.0))
            nc.gpsimd.affine_select(out=spread[:, :].rearrange("p (h c) -> p h c", h=HN),
                                    in_=spread[:, :].rearrange("p (h c) -> p h c", h=HN),
                                    compare_op=ALU.not_equal, fill=1.0, base=0,
                                    pattern=[[0, HN], [-1, NC]], channel_multiplier=1)
            step(nc.gpsimd.memset(own_head[:, :], 1.0))
            step(nc.gpsimd.affine_select(out=own_head[:, :], in_=own_head[:, :], compare_op=ALU.is_ge, fill=0.0,
                                         base=0, pattern=[[-NC, HN]], channel_multiplier=1))
            nc.gpsimd.affine_select(out=own_head[:, :], in_=own_head[:, :], compare_op=ALU.is_ge, fill=0.0,
                                    base=NC - 1, pattern=[[NC, HN]], channel_multiplier=-1)
            nc.gpsimd.memset(blk[0], 0.0)
            nc.gpsimd.memset(blk[1], 0.0)
            for h in range(HN):
                nc.gpsimd.memset(q_tok[:, :, h, DH:DE], SLOPES[h] / SCALE)
            nc.gpsimd.memset(fq_tok[:, :, :, DH:DE], 1.0 / SCALE)
            for g in range(G):
                nc.gpsimd.iota(ck65[:, g, DH:DE], pattern=[[0, 1]], base=CMP_BLOCK - 1, channel_multiplier=CMP_STRIDE,
                               allow_small_or_imprecise_dtypes=True)
            for g in range(G):
                nc.gpsimd.iota(ks_tok[:, :, g, DH:DE], pattern=[[P, NT], [0, 1]], base=0, channel_multiplier=1,
                               allow_small_or_imprecise_dtypes=True)
                last = nc.gpsimd.iota(kw_tok[:, :, g, DH:DE], pattern=[[P, NT], [0, 1]], base=0, channel_multiplier=1,
                                      allow_small_or_imprecise_dtypes=True)
            last.then_inc(consts_made, 1)
            for i, r in enumerate(INVERTED):
                pool.wait_ge(mean_made, i + 1)
                nc.gpsimd.tensor_tensor(r, r, minus_half[0:r.shape[0], 0:r.shape[1]], ALU.pow).then_inc(inv_made, 1)

        @block.scalar
        def _(act):
            n = [0]

            def step(ins):
                n[0] += 1
                ins.then_inc(a_step, 1)
                act.wait_ge(a_step, n[0])
            for c0, w, name in ((B_GATE, 24, "b_nsa_gate"), (B_GATE + 24, 8, "b_forget"), (B_CK2, DH, "b_ck2"),
                                (B_CV2, DH, "b_cv2"), (B_ROUTER, E, "b_router")):
                act.dma_start(brow[:, c0:c0 + w], a[name]).then_inc(small_in, 16)
            act.dma_start(w_c2[:, 0, :, :], a["w_ck2"][0].rearrange("(c p) n -> p c n", p=P)).then_inc(small_in, 16)
            act.dma_start(w_c2[:, 1, :, :], a["w_cv2"][0].rearrange("(c p) n -> p c n", p=P)).then_inc(small_in, 16)
            act.dma_start(w_r[:, :, :], a["w_router"][0].rearrange("(k p) n -> p k n", p=P)).then_inc(small_in, 16)

            def square_out(t):
                return heads[:, 2048 + D * t:2048 + D * t + D]

            def square_rows(t):
                nc.scalar.activation(square_out(t), x[:, t, :],
                                     ACT.Square, accum_out=ss[:, t:t + 1]).then_inc(squared, 1)
            for t in range(NT):
                act.wait_ge(x_in[t], 16)
                square_rows(t)

            def two(ap):
                return ap.unsqueeze(2).to_broadcast([P, G, 2, DH])
            for i in range(12):
                b, t, ps = i // 2, i % 2, PJ[i % 2]
                act.wait_ge(proj_done, i + 1)
                dve_before = i if i < 10 else 10
                if i >= 2 and b < 5:
                    act.wait_ge(proj_read_v, dve_before - 1)
                if b == 0:
                    if t == 0:
                        act.wait_ge(xn_turned, 4)
                    kv = ps[:, :].rearrange("p (j g d) -> p j g d", j=4, g=G)
                    nc.scalar.activation(kc_dup[:, t], two(kv[:, 0]), ACT.Copy)
                    nc.scalar.activation(vc_dup[:, t], two(kv[:, 1]), ACT.Copy)
                    nc.scalar.activation(vs[:, t], kv[:, 3], ACT.Copy)
                    nc.scalar.activation(sq[i % 2][:, 0:P], ps[:, 256:384], ACT.Square).then_inc(proj_read_a, 1)
                elif b == 1:
                    nc.scalar.activation(vw[:, t], ps[:, 128:256].rearrange("p (g d) -> p g d", g=G), ACT.Copy)
                    nc.scalar.activation(gates[:, t], ps[:, 256:288], ACT.Copy).then_inc(gates_kept, 1)
                    nc.scalar.activation(sq[i % 2][:, 0:P], ps[:, 0:128], ACT.Square).then_inc(proj_read_a, 1)
                    if t == 1:
                        act.wait_ge(gates_kept, 2)
                        nc.scalar.activation(gate[:, :, :], gates[:, :, 0:24], ACT.Tanh, scale=0.5).then_inc(gates_tanh, 1)
                        nc.scalar.activation(fa[:, :, :], gates[:, :, 24:32], ACT.Abs).then_inc(f_abs, 1)
                        act.wait_ge(f_abs, 1)
                        nc.scalar.activation(fb[:, :, :], fa[:, :, :], ACT.Exp, scale=-1.0).then_inc(f_exp, 1)
                        act.wait_ge(f_exp, 1)
                        nc.scalar.activation(fa[:, :, :], fb[:, :, :], ACT.Ln, bias=1.0).then_inc(f_ln, 1)
                elif b == 5:
                    nc.scalar.activation(fv[:, t], ps[:, :].rearrange("p (h d) -> p h d", h=HF), ACT.Copy).then_inc(proj_read_a, 1)
                else:
                    nc.scalar.activation(sq[i % 2], ps[:, :], ACT.Square).then_inc(proj_read_a, 1)
                if i == 7:
                    act.wait_ge(hid_in, 1)
                    nc.scalar.activation(hid_b, hid_b, ACT.Tanh, scale=0.7978845608028654).then_inc(hid_tanh, 1)
            for u in range(0, len(UNITS), 2):
                src, dst, h0, gain = UNITS[u]
                act.wait_ge(turned, u + 1)
                nc.scalar.activation(dst[:, h0:h0 + 2, :], TB[0][0:DE, :].rearrange("p (h t) -> p h t", h=2), ACT.Copy,
                                     scale=gain[0:DE, :]).then_inc(kept_a, 1)
                if u == 4:
                    act.wait_ge(cs_max, 1)
                    nc.scalar.activation(cp, cp, ACT.Exp).then_inc(cs_exp, 1)
            for m in range(24):
                act.wait_ge(s_max, m + 1)
                if m >= 2:
                    act.wait_ge(p_turned, m - 1)
                nc.scalar.activation(pr[m % 2][:, 0:P], sm[m % 2][:, 0:P], ACT.Exp, bias=nmx[:, m % 2, 0:1],
                                     accum_out=sums[:, m, 0:1])
                nc.scalar.activation(pr[m % 2][:, P:384], sm[m % 2][:, P:384], ACT.Exp, bias=nmx[:, m % 2, 1:2],
                                     accum_out=sums[:, m, 1:2]).then_inc(p_made, 1)
                if m in MERGE_AT:
                    c = MERGE_AT[m]
                    act.wait_ge(merge_done, c + 1)
                    nc.scalar.activation(mergeT[:, c, :], PJ[c % 2][:, 0:T], ACT.Tanh, scale=0.5,
                                         bias=scaled[:, c:c + 1]).then_inc(merge_made, 1)
            act.wait_ge(o_done, 3)
            act.dma_start(b_down, a["b_e_down"][0]).then_inc(bdown_in, 16)
            for t in range(NT):
                act.wait_ge(summed, t + 1)
                square_rows(t)
            for t in range(NT):
                act.wait_ge(inv_made, N_INV - NT + t + 1)
                last = nc.scalar.activation(xn[:, t, :], x[:, t, :], ACT.Copy, scale=rr[:, t:t + 1])
            last.then_inc(xn_ready, 1)
            act.wait_ge(lg_done, 2)
            act.dma_start(e_rows[:, 0, :], a["b_e_gate"][0]).then_inc(ebias_in, 16)
            act.dma_start(e_rows[:, 1, :], a["b_e_up"][0]).then_inc(ebias_in, 16)
            act.wait_ge(lg_moved, 1)
            nc.scalar.activation(lg[:, :, :], lg[:, :, :], ACT.Exp).then_inc(lg_exp, 1)

            def keep_y(done):
                act.wait_ge(mat_done["down"], done)
                nc.scalar.activation(e_y, banks[3][:, :], ACT.Copy).then_inc(y_kept, 1)

            def expert(it, first):
                if not first:
                    keep_y(it)
                act.wait_ge(g_made, it + 1)
                nc.scalar.activation(e_sig, e_g, ACT.Sigmoid, scale=SWISH).then_inc(sig_made, 1)
                act.wait_ge(hotw_turned, it + 1)
                nc.scalar.activation(hotT, bank45[:, 1, 0:T].rearrange("p (t q) -> p t q", t=NT), ACT.Copy).then_inc(hotT_made, 1)
            expert(0, True)
            act.wait_ge(route_made, 1)
            total = act.value_load(total_i[0:1, 0:1], min_val=E, max_val=ROUNDS * E)
            for u in range(1, STEPS):
                expert(u, False)
            with act.Fori(STEPS, total, STEPS) as base:
                for u in range(STEPS):
                    expert(base + u, False)
            keep_y(total)

        @block.vector
        def _(dve):
            n = [0]

            def step(ins):
                n[0] += 1
                ins.then_inc(v_step, 1)
                dve.wait_ge(v_step, n[0])

            n_inv = [0]

            def inv_rms(dst, src, width):
                nc.vector.tensor_scalar(dst, src, 1.0 / width, EPS, ALU.mult, ALU.add).then_inc(mean_made, 1)
                n_inv[0] += 1
                dve.wait_ge(inv_made, n_inv[0])

            def norm_row_tile(t, made):
                inv_rms(rr[:, t:t + 1], ss[:, t:t + 1], D)
                nc.vector.tensor_scalar(xn[:, t, :], x[:, t, :], rr[:, t:t + 1], None, ALU.mult).then_inc(made, 1)

            def keep_hT_tile(gain_col, bank_list, base, t):
                for j in range(2):
                    dve.wait_ge(xn_turned, base + 2 * t + j + 1)
                    nc.vector.tensor_tensor(hT[:, 4 * j:4 * j + 4, P * t:P * t + P],
                                            bank_list[2 * t + j][:, :].rearrange("p (k q) -> p k q", k=4),
                                            col(vcol[:, gain_col + 4 * j:gain_col + 4 * j + 4], P), ALU.mult).then_inc(hT_made, 1)

            for t in range(NT):
                dve.wait_ge(squared, t + 1)
                norm_row_tile(t, xn_made)
            dve.wait_ge(vec_turned, 1)
            step(nc.vector.tensor_copy(vcol[:, :], TB[0][:, 0:R_ALL]))
            nc.vector.tensor_scalar(scaled[:, 0:16], vcol[:, R_BM:R_BM + 16], 0.5, None, ALU.mult)
            nc.vector.tensor_scalar(scaled[:, 16:17], vcol[:, R_QN:R_QN + 1], SCALE, None, ALU.mult)
            nc.vector.tensor_scalar(scaled[:, 17:18], vcol[:, R_QF:R_QF + 1], SCALE, None, ALU.mult).then_inc(vec_kept, 1)
            for t in range(NT):
                keep_hT_tile(R_GA, [PJ[0], PJ[1], S[0], S[1]], 0, t)

            def head_norm(i, c0, n_heads, dst):
                ps = PJ[i % 2]
                dve.wait_ge(proj_read_a, i + 1)
                step(nc.vector.tensor_reduce(ssq[:, 0:n_heads], sq[i % 2][:, 0:n_heads * DH].rearrange("p (h d) -> p h d", d=DH),
                                             AX.X, ALU.add))
                inv_rms(rrq[:, 0:n_heads], ssq[:, 0:n_heads], DH)
                nc.vector.tensor_tensor(dst, ps[:, c0:c0 + n_heads * DH].rearrange("p (h d) -> p h d", d=DH),
                                        col(rrq[:, 0:n_heads], DH), ALU.mult).then_inc(proj_read_v, 1)
            for t in range(NT):
                head_norm(t, 256, G, ks_tok[:, t, :, 0:DH])
            for t in range(NT):
                head_norm(2 + t, 0, G, kw_tok[:, t, :, 0:DH])
            dve.wait_ge(gates_kept, 2)
            dve.wait_ge(gates_tanh, 1)
            dve.wait_ge(f_abs, 1)
            step(nc.vector.tensor_scalar(gate[:, :, :], gate[:, :, :], 1.0, 0.5, ALU.add, ALU.mult))
            step(nc.vector.tensor_scalar(gates[:, :, 24:32], gates[:, :, 24:32], 0.0, None, ALU.min))
            dve.wait_ge(f_ln, 1)
            nc.vector.tensor_tensor(fb[:, :, :], fa[:, :, :], gates[:, :, 24:32], ALU.subtract).then_inc(f_neg, 1)
            dve.wait_ge(consts_made, 2)
            for v in range(2):
                dve.wait_ge(kv_turned, v + 1)
                tb = TB[v].rearrange("p (g t) -> p g t", g=G)
                for par in range(2):
                    lo = 64 * par
                    for half in range(2):
                        s0 = CMP_STRIDE * half
                        tv = tb[lo:lo + 64, :, s0:s0 + 240].rearrange("p g (i m u) -> p g i m u", m=8, u=2)[:, :, :, :, par]
                        pcol = vcol[lo:lo + 64, (R_PK, R_PV)[v] + 8 * half:(R_PK, R_PV)[v] + 8 * half + 8]
                        pcol = pcol.unsqueeze(1).unsqueeze(1).to_broadcast([64, G, NC - 1, 8])
                        dst = blk[v][lo:lo + 64, 8 * half:8 * half + 8, :, 0:NC - 1].rearrange("p m g i -> p g i m")
                        for g in range(G):
                            last = nc.vector.tensor_tensor(dst[:, g], tv[:, g], pcol[:, g], ALU.add)
                last.then_inc(blk_made, 1)
            for t in range(NT):
                head_norm(4 + t, 0, HN, q_tok[:, t, :, 0:DH])
            dve.wait_ge(hid_done, 1)
            nc.vector.tensor_copy(hid_a, S[0][:, 0:P]).then_inc(hid_rows, 1)
            head_norm(6, 0, HF, fk_tok[:, 0, :, 0:DH])
            dve.wait_ge(hid_turned, 1)
            for v in range(2):
                for c in range(2):
                    r = (R_BK1, R_BV1)[v] + c
                    last = nc.vector.tensor_scalar(hid[:, v, c, :], S[0][:, P + 64 * v + 32 * c:P + 64 * v + 32 * c + 32],
                                                   vcol[:, r:r + 1], None, ALU.add)
            step(last)
            hflat = late[:, 3072:3200]
            step(nc.vector.tensor_tensor(hid_a, hflat, hflat, ALU.mult))
            step(nc.vector.tensor_scalar(hid_b, hid_a, 0.044715, 1.0, ALU.mult, ALU.add))
            nc.vector.tensor_tensor(hid_b, hid_b, hflat, ALU.mult).then_inc(hid_in, 1)
            step(nc.vector.tensor_scalar(hid_a, hflat, 0.5, None, ALU.mult))
            head_norm(7, 0, HF, fk_tok[:, 1, :, 0:DH])
            dve.wait_ge(hid_tanh, 1)
            nc.vector.scalar_tensor_tensor(out=hflat, in0=hid_b, scalar=1.0, in1=hid_a, op0=ALU.add, op1=ALU.mult).then_inc(hid_made, 1)
            dve.wait_ge(ck_done, 1)
            step(nc.vector.tensor_copy(ck_sq, S[1][0:NC, 0:P]))
            step(nc.vector.tensor_tensor(ck_sq, ck_sq, ck_sq, ALU.mult))
            step(nc.vector.tensor_reduce(ck_ss[0:NC, :], ck_sq.rearrange("p (g d) -> p g d", g=G), AX.X, ALU.add))
            inv_rms(ck_r[0:NC, :], ck_ss[0:NC, :], DH)
            nc.vector.tensor_tensor(ck65[:, :, 0:DH], S[1][0:NC, 0:P].rearrange("p (g d) -> p g d", g=G),
                                    col(ck_r[0:NC, :], DH), ALU.mult)
            nc.vector.tensor_copy(vc16, S[1][0:NC, P:2 * P]).then_inc(ck_kept, 1)
            dve.wait_ge(f_summed, 1)
            nc.vector.tensor_copy(b_router, OB[0][:, 32:64])
            nc.vector.tensor_copy(fk_tok[:, :, :, DH], OB[0][:, 0:16].rearrange("p (t h) -> p t h", t=NT)).then_inc(f_placed, 1)
            for t in range(NT):
                head_norm(8 + t, 0, HF, fq_tok[:, t, :, 0:DH])
            dve.wait_ge(ck_turned, 1)
            nc.vector.tensor_scalar(kcT, OB[1][0:DE, 0:32].rearrange("p (g c) -> p g c", g=G),
                                    vcol[0:DE, R_KC:R_KC + 1], None, ALU.mult)
            for g in range(G):
                last = nc.vector.tensor_tensor(
                    v_block[:, 4 * g:4 * g + 4, :],
                    S[1][:, DH * g:DH * g + DH].unsqueeze(1).to_broadcast([P, 4, DH]),
                    col(own_head[:, 4 * g:4 * g + 4], DH), ALU.mult)
            last.then_inc(ck_ready, 1)

            def keep_unit(u):
                src, dst, h0, gain = UNITS[u]
                dve.wait_ge(turned, u + 1)
                nc.vector.tensor_scalar(dst[:, h0:h0 + 2, :], TB[1][0:DE, :].rearrange("p (h t) -> p h t", h=2),
                                        gain[0:DE, :], None, ALU.mult).then_inc(kept_v, 1)
            for u in (1, 3, 5):
                keep_unit(u)
            dve.wait_ge(cs_done, 1)
            c4 = cp.rearrange("p (t h c) -> p t h c", t=NT, h=HN)
            c3 = cp.rearrange("p (n c) -> p n c", c=NC)
            for t in range(NT):
                last = nc.vector.tensor_tensor(c4[:, t], S[0][:, P * t:P * t + P].rearrange("p (h c) -> p h c", h=HN),
                                               cneg[:, t, :].unsqueeze(1).to_broadcast([P, HN, NC]), ALU.add)
            step(last)
            step(nc.vector.tensor_reduce(csum, c3, AX.X, ALU.max))
            nc.vector.tensor_tensor(c3, c3, col(csum, NC), ALU.subtract).then_inc(cs_max, 1)
            dve.wait_ge(cs_exp, 1)
            for t in range(NT):
                last = nc.vector.tensor_tensor(c4[:, t], c4[:, t], cmask[:, t, :].unsqueeze(1).to_broadcast([P, HN, NC]), ALU.mult)
            step(last)
            step(nc.vector.tensor_reduce(csum, c3, AX.X, ALU.add))
            step(nc.vector.tensor_scalar(csum, csum, 1e-30, None, ALU.max))
            step(nc.vector.reciprocal(csum, csum))
            step(nc.vector.tensor_tensor(csum.rearrange("p (t h) -> p t h", t=NT), csum.rearrange("p (t h) -> p t h", t=NT),
                                         gate[:, :, 0:HN], ALU.mult))
            nc.vector.tensor_tensor(c3, c3, col(csum, NC), ALU.mult).then_inc(cp_made, 1)
            for u in (7, 9, 11, 13):
                keep_unit(u)
            dve.wait_ge(cp_turned, 1)
            nc.vector.tensor_copy(cpT, S[1][:, 0:T].rearrange("p (t q) -> p t q", t=NT)).then_inc(cpT_made, 1)
            dve.wait_ge(co_done, 1)
            nc.vector.tensor_copy(o_nsa[:, 0, :], OB[0])
            nc.vector.tensor_copy(o_nsa[:, 1, :], OB[1]).then_inc(co_kept, 1)

            def row_max(m):
                dve.wait_ge(s_done, m + 1)
                if m >= 2:
                    dve.wait_ge(p_made, m - 1)
                b = m % 2
                nc.vector.tensor_tensor_reduce(sm[b][:, 0:P], S[b][:, 0:P], causal[:, P:T], 1.0, NEG * 2,
                                               ALU.add, ALU.max, mx[:, b, 0:1])
                step(nc.vector.tensor_tensor_reduce(sm[b][:, P:384], S[b][:, P:384], causal[:, :], 1.0, NEG * 2,
                                                    ALU.add, ALU.max, mx[:, b, 1:2]))
                nc.vector.tensor_scalar(nmx[:, b, :], mx[:, b, :], -1.0, None, ALU.mult).then_inc(s_max, 1)

            def keep_pT(m):
                dve.wait_ge(p_turned, m + 1)
                nc.vector.tensor_copy(prT[m % 2], TB[m % 2][:, 0:384]).then_inc(pT_made, 1)

            def keep_o(br):
                dve.wait_ge(o_done, br + 1)
                dst = o_fox if br == 2 else o_nsa
                step(nc.vector.reciprocal(rg[:, :, :].rearrange("p t h -> p h t"), sums[:, 8 * br:8 * br + 8, :]))
                if br < 2:
                    g0 = (16, 8)[br]
                    step(nc.vector.tensor_tensor(rg[:, :, :], rg[:, :, :], gate[:, :, g0:g0 + 8], ALU.mult))
                for t in range(NT):
                    ob = OB[t].rearrange("p (h d) -> p h d", d=DH)
                    if br == 2:
                        last = nc.vector.tensor_tensor(dst[:, t, :].rearrange("p (h d) -> p h d", d=DH), ob, col(rg[:, t, :], DH), ALU.mult)
                    else:
                        step(nc.vector.tensor_tensor(tmp_br.rearrange("p (h d) -> p h d", d=DH), ob, col(rg[:, t, :], DH), ALU.mult))
                        last = nc.vector.tensor_tensor(dst[:, t, :], dst[:, t, :], tmp_br, ALU.add)
                        if t == 0:
                            step(last)
                last.then_inc(o_kept, 1)
            for m in range(26):
                if m < 24:
                    row_max(m)
                if 1 <= m <= 24:
                    keep_pT(m - 1)
                if m in (9, 17, 25):
                    keep_o((m - 9) // 8)
            for mix in range(2):
                for t2 in range(2):
                    dve.wait_ge(o_turned, 2 * mix + t2 + 1)
                    nc.vector.tensor_copy(oT[mix][:, 2 * t2:2 * t2 + 2, :],
                                          (S, TB)[mix][t2][:, :].rearrange("p (k t) -> p k t", k=2)).then_inc(oT_made, 1)
            dve.wait_ge(merge_made, 16)
            for c in range(KD):
                dve.wait_ge(up_done, c + 1)
                ps = PJ[c % 2]
                step(nc.vector.scalar_tensor_tensor(out=yT[:, c, :], in0=mergeT[:, c, :], scalar=1.0, in1=ps[:, 0:T],
                                                    op0=ALU.add, op1=ALU.mult))
                step(nc.vector.scalar_tensor_tensor(out=tmp_up, in0=mergeT[:, KD + c, :], scalar=1.0, in1=ps[:, T:2 * T],
                                                    op0=ALU.add, op1=ALU.mult))
                nc.vector.tensor_tensor(yT[:, c, :], yT[:, c, :], tmp_up, ALU.add).then_inc(y_made, 1)
                dve.wait_ge(y_made, c + 1)
            for t in range(NT):
                dve.wait_ge(out_done, 3 + t)
                for h in range(2):
                    last = nc.vector.scalar_tensor_tensor(out=x[:, t, 512 * h:512 * h + 512], in0=(S, TB)[t][h][:, :], scalar=0.5,
                                                          in1=x[:, t, 512 * h:512 * h + 512], op0=ALU.mult, op1=ALU.add)
                last.then_inc(summed, 1)
                keep_hT_tile(R_GM, [PJ[0], PJ[1], OB[0], OB[1]], 4, t)
            for t in range(NT):
                dve.wait_ge(squared, NT + t + 1)
                inv_rms(rr[:, t:t + 1], ss[:, t:t + 1], D)

            dve.wait_ge(lg_done, 2)
            for t in range(NT):
                last = nc.vector.scalar_tensor_tensor(out=logits[:, t, :], in0=PJ[0][:, E * t:E * t + E], scalar=rr[:, t:t + 1],
                                                      in1=b_router, op0=ALU.mult, op1=ALU.add)
            step(last)
            for t in range(NT):
                last = nc.vector.max(top8[:, t, :], logits[:, t, :])
            step(last)
            fourth = top8[:, :, TOPK - 1:TOPK].to_broadcast([P, NT, E])
            nc.vector.tensor_tensor(equal, logits, fourth, ALU.is_equal)
            step(nc.vector.tensor_tensor(above[:, :, :], logits, fourth, ALU.is_gt))
            nc.vector.tensor_tensor(lg[:, :, :], logits, top8[:, :, 0:1].to_broadcast([P, NT, E]), ALU.subtract).then_inc(lg_moved, 1)
            step(nc.vector.tensor_reduce(tot[:, 0:2], above[:, :, :], AX.X, ALU.add))
            nc.vector.tensor_scalar(tot[:, 2:4], tot[:, 0:2], -1.0, float(TOPK), ALU.mult, ALU.add)
            step(nc.vector.tensor_tensor_scan(work[:, 320:384], in_tile[:, :], work[:, 256:320], 0.0, ALU.mult, ALU.add))
            step(nc.vector.tensor_tensor(count, count, col(tot[:, 2:4], E), ALU.is_le))
            step(nc.vector.tensor_tensor(count, count, equal, ALU.mult))
            nc.vector.tensor_tensor(chosen, above[:, :, :], count, ALU.add).then_inc(sel_made, 1)
            dve.wait_ge(sel_made, 1)
            dve.wait_ge(lg_exp, 1)
            step(nc.vector.tensor_tensor(comb, lg[:, :, :], chosen, ALU.mult))
            step(nc.vector.tensor_reduce(tot[:, 4:6], comb, AX.X, ALU.add))
            step(nc.vector.reciprocal(tot[:, 6:8], tot[:, 4:6]))
            nc.vector.tensor_tensor(comb, comb, col(tot[:, 6:8], E), ALU.mult).then_inc(comb_made, 1)
            dve.wait_ge(comb_made, 1)
            dve.wait_ge(pos_done, 1)
            for t in range(NT):
                last = nc.vector.scalar_tensor_tensor(out=above[:, t, :], in0=TB[1][:, E * t:E * t + E], scalar=1.0,
                                                      in1=chosen[:, t, :], op0=ALU.add, op1=ALU.mult)
            step(last)
            steps = ROUNDS * E
            rt = route[:, 0:steps * 4].rearrange("p (r e j) -> p r e j", r=ROUNDS, e=E)
            for t in range(NT):
                last = nc.vector.tensor_tensor(rt[:, :, :, t], above[:, t, :].unsqueeze(1).to_broadcast([P, ROUNDS, E]),
                                               col(round_off[:, :], E), ALU.add)
            step(last)
            for t in range(NT):
                last = nc.vector.tensor_scalar(hot[:, t, :], slot_no[:, :], rv0[:, t:t + 1], None, ALU.is_equal)
            last.then_inc(hot_made, 1)
            for t in range(NT):
                last = nc.vector.tensor_copy(rt[:, :, :, 2 + t], comb[:, t, :].unsqueeze(1).to_broadcast([P, ROUNDS, E]))
            step(last)
            step(nc.vector.tensor_reduce(tot[:, 0:1], TB[1][:, 2 * E:3 * E], AX.X, ALU.max))
            step(nc.vector.tensor_scalar(tot[:, 1:2], tot[:, 0:1], float(C), None, ALU.is_gt))
            for r in range(2, ROUNDS):
                step(nc.vector.scalar_tensor_tensor(out=tot[:, 1:2], in0=tot[:, 0:1], scalar=float(C * r), in1=tot[:, 1:2],
                                                    op0=ALU.is_gt, op1=ALU.add))
            step(nc.vector.tensor_scalar(tot[:, 2:3], tot[:, 1:2], float(E), float(E), ALU.mult, ALU.add))
            step(nc.vector.tensor_scalar(tot[:, 3:4], tot[:, 2:3], -1.0, None, ALU.add))
            nc.vector.tensor_copy(total_i[:, :], tot[0:1, 2:4]).then_inc(route_made, 1)
            step(nc.vector.tensor_copy(e_sel, ident[0:E, 0:1].to_broadcast([E, C])))
            def expert(it, first):
                k = [0]

                def chain(ins):
                    k[0] += 1
                    ins.then_inc(v_loop_step, 1)
                    dve.wait_ge(v_loop_step, it * CHAIN + k[0])
                e = it if isinstance(it, int) else it & (E - 1)
                rv = route[:, :].rearrange("p (s j) -> p s j", j=4)
                rcols = rv[:, it:it + 2, :] if isinstance(it, int) else rv[:, bass.ds(it, 2), :]
                chain(nc.vector.tensor_copy(now.rearrange("p (s j) -> p s j", j=4), rcols))
                dve.wait_ge(gathered, it + 1)
                for t in range(NT):
                    last = nc.vector.tensor_scalar(hot[:, t, :], slot_no[:, :], now[:, 4 + t:5 + t], None, ALU.is_equal)
                last.then_inc(hot_made, 1)
                if not first:
                    dve.wait_ge(hotw_turned, it)
                for t in range(NT):
                    last = nc.vector.tensor_scalar(hotw[:, t, :, :], slot_no[:, :].unsqueeze(1).to_broadcast([P, 2, C]),
                                                   now[:, t:t + 1], now[:, 2 + t:3 + t], ALU.is_equal, ALU.mult)
                last.then_inc(hotw_made, 1)
                if not first:
                    add_rows(it - 1)
                dve.wait_ge(mat_done["gate"], it + 1)
                nc.vector.tensor_scalar(e_g, banks[1][:, :], LIMIT, None, ALU.min).then_inc(g_made, 1)
                dve.wait_ge(mat_done["up"], it + 1)
                nc.vector.tensor_scalar(e_u, banks[2][:, :], LIMIT, -LIMIT, ALU.min, ALU.max).then_inc(up_read, 1)
                dve.wait_ge(up_read, it + 1)
                dve.wait_ge(g_made, it + 1)
                chain(nc.vector.scalar_tensor_tensor(out=e_u, in0=e_u, scalar=1.0, in1=e_g, op0=ALU.add, op1=ALU.mult))
                dve.wait_ge(sig_made, it + 1)
                nc.vector.tensor_tensor(e_h, e_u, e_sig, ALU.mult).then_inc(eh_made, 1)
                next_sel(it, chain)
                dve.wait_ge(eh_turned, it + 1)
                nc.vector.tensor_copy(e_hT, bank45[:, 0, :].rearrange("p (k h s) -> p k h s", h=2, s=C)).then_inc(ehT_made, 1)
                keep_x(it + 1)
                if first:
                    add_biases()
                assert k[0] == CHAIN

            def next_sel(it, chain):
                e1 = (it + 1) & (E - 1)
                col_e = ident[0:E, e1:e1 + 1] if isinstance(e1, int) else ident[0:E, bass.ds(e1, 1)]
                chain(nc.vector.tensor_copy(e_sel, col_e.to_broadcast([E, C])))

            def keep_x(i):
                dve.wait_ge(gathered, i + 1)
                nc.vector.tensor_tensor(e_x, banks[0][:, :].rearrange("p (k s) -> p k s", s=C), col(vcol[:, R_GM:R_GM + KD], C), ALU.mult).then_inc(ex_made, 1)

            def add_biases():
                for t in range(NT):
                    dve.wait_ge(bd_done, t + 1)
                    for h in range(2):
                        last = nc.vector.tensor_tensor(x[:, t, 512 * h:512 * h + 512], x[:, t, 512 * h:512 * h + 512],
                                                       bank67[:, h, :], ALU.add)
                    last.then_inc(bd_added, 1)

            def add_rows(i):
                for j in range(4):
                    t, h = j // 2, j % 2
                    dve.wait_ge(spread_done, i * 4 + j + 1)
                    ins = nc.vector.tensor_tensor(x[:, t, 512 * h:512 * h + 512], x[:, t, 512 * h:512 * h + 512],
                                                  bank67[:, j % 2, :], ALU.add)
                    if j != 2:
                        ins.then_inc(rows_added if j == 3 else added, 1)
            dve.wait_ge(route_made, 1)
            total = dve.value_load(total_i[0:1, 0:1], min_val=E, max_val=ROUNDS * E)
            keep_x(0)
            dve.wait_ge(comb_turned, 1)
            nc.vector.tensor_copy(combT, bank45[0:E, 1, T:2 * T].rearrange("p (t q) -> p t q", t=NT)).then_inc(combT_made, 1)
            expert(0, True)
            for u in range(1, STEPS):
                expert(u, False)
            with dve.Fori(STEPS, total, STEPS) as base:
                for u in range(STEPS):
                    expert(base + u, False)
            add_rows(dve.value_load(total_i[0:1, 1:2], min_val=E - 1, max_val=ROUNDS * E - 1))

        @block.tensor
        def _(pe):
            mm = nc.tensor.matmul

            def turn_rows(src, t, bank_list):
                for j in range(2):
                    for k in range(4):
                        c = P * (4 * j + k)
                        last = nc.tensor.transpose(bank_list[2 * t + j][:, P * k:P * k + P], src[:, t, c:c + P], ident[:, :])
                    last.then_inc(xn_turned, 1)
            pe.wait_ge(consts_made, 1)
            pe.wait_ge(vec_in, 16 * 13)
            nc.tensor.transpose(TB[0][:, 0:R_ALL], vrow[:, :], ident[0:R_ALL, 0:R_ALL]).then_inc(vec_turned, 1)
            for t in range(NT):
                pe.wait_ge(xn_made, t + 1)
                turn_rows(xn, t, [PJ[0], PJ[1], S[0], S[1]])
            pe.wait_ge(hT_made, 4)
            pe.wait_ge(consts_made, 2)
            def project(i, name, n):
                ps, t = PJ[i % 2], i % 2
                if i >= 2:
                    pe.wait_ge(proj_read_a, i - 1)
                    pe.wait_ge(proj_read_v, min(i - 1, 10))
                wait_block(pe, name)
                w = view[name]
                for k in range(KD):
                    last = mm(ps[:, 0:n], hT[:, k, P * t:P * t + P], w[:, k, :], start=(k == 0), stop=(k == KD - 1))
                if name == "kw":
                    pe.wait_ge(small_in, 16 * 8)
                    last = mm(ps[:, 256:288], ones[0:1, :], brow[:, 0:32], start=False, stop=True, skip_group_check=True)
                last.then_inc(proj_done, 1)

            project(0, "kv", 512)
            project(1, "kv", 512)
            project(2, "kw", 288)
            project(3, "kw", 288)
            pe.wait_ge(vec_kept, 1)
            pe.wait_ge(proj_read_a, 2)
            for v in range(2):
                for g in range(G):
                    for t in range(NT):
                        last = nc.tensor.transpose(TB[v][:, 256 * g + P * t:256 * g + P * t + P],
                                                   (kc_dup, vc_dup)[v][:, t, g].rearrange("p u d -> p (u d)"), ident[:, :])
                last.then_inc(kv_turned, 1)
            project(4, "q", 512)
            project(5, "q", 512)
            pe.wait_ge(blk_made, 2)
            wait_block(pe, "ck1")
            wait_block(pe, "cv1")
            for m in range(16):
                for v, name in enumerate(("ck1", "cv1")):
                    for c in range(2):
                        lo = 64 * v + 32 * c
                        last = mm(S[0][lo:lo + 32, 0:P], blk[v][:, m, :, :].rearrange("p g i -> p (g i)"),
                                  view[name][:, m, P * c:P * c + P], start=(m == 0), stop=(m == 15))
            last.then_inc(hid_done, 1)
            project(6, "fk", 512)
            pe.wait_ge(hid_rows, 1)
            nc.tensor.transpose(S[0][:, P:2 * P], hid_a, ident[:, :]).then_inc(hid_turned, 1)
            project(7, "fk", 512)
            pe.wait_ge(hid_made, 1)
            for v in range(2):
                for g in range(G):
                    c0 = P * v + DH * g
                    for c in range(2):
                        mm(S[1][0:NC, c0:c0 + DH], hid[:, v, c, NC * g:NC * g + NC], w_c2[:, v, c, :], start=(c == 0), stop=False)
                    b0 = (B_CK2, B_CV2)[v]
                    last = mm(S[1][0:NC, c0:c0 + DH], ones[0:1, 0:NC], brow[:, b0:b0 + DH], start=False, stop=True)
            last.then_inc(ck_done, 1)
            pe.wait_ge(f_neg, 1)
            mm(OB[0][:, 32:64], ones[0:1, :], brow[:, B_ROUTER:B_ROUTER + E], start=True, stop=True)
            mm(OB[0][:, 0:8], upto[:, :], fb[:, 0, :], start=True, stop=True)
            mm(OB[0][:, 8:16], ones[:, :], fb[:, 0, :], start=True, stop=False)
            mm(OB[0][:, 8:16], upto[:, :], fb[:, 1, :], start=False, stop=True).then_inc(f_summed, 1)
            project(8, "fq", 512)
            project(9, "fq", 512)
            pe.wait_ge(ck_kept, 1)
            for g in range(G):
                nc.tensor.transpose(OB[1][0:DE, NC * g:NC * g + NC], ck65[:, g, :], ident[0:NC, 0:NC])
            mm(S[1][:, 0:P], spread[:, :], vc16, start=True, stop=True).then_inc(ck_turned, 1)
            project(10, "fv", 512)
            project(11, "fv", 512)

            def turn_heads(u):
                src, dst, h0, gain = UNITS[u]
                if u >= 2:
                    pe.wait_ge((kept_a, kept_v)[u % 2], u // 2)
                for h in range(2):
                    for t in range(NT):
                        last = nc.tensor.transpose(TB[u % 2][0:DE, 256 * h + P * t:256 * h + P * t + P],
                                                   src[:, t, h0 + h, :], ident[:, :])
                last.then_inc(turned, 1)
            pe.wait_ge(blk_made, 2)
            pe.wait_ge(proj_read_v, 10)
            pe.wait_ge(f_placed, 1)
            for u in range(6):
                turn_heads(u)
            pe.wait_ge(ck_ready, 1)
            pe.wait_ge(kept_a, 2)
            pe.wait_ge(kept_v, 2)
            for t in range(NT):
                for h in range(HN):
                    last = mm(S[0][:, P * t + NC * h:P * t + NC * h + NC], qT[:, h, P * t:P * t + P], kcT[:, h // 4, :],
                              start=True, stop=True)
            last.then_inc(cs_done, 1)
            for u in range(6, len(UNITS)):
                turn_heads(u)
            pe.wait_ge(cp_made, 1)
            for t in range(NT):
                last = nc.tensor.transpose(S[1][:, P * t:P * t + P], cp[:, P * t:P * t + P], ident[:, :])
            last.then_inc(cp_turned, 1)
            pe.wait_ge(cpT_made, 1)
            for t in range(NT):
                last = mm(OB[t], cpT[:, t, :], v_block.rearrange("p h d -> p (h d)"), start=True, stop=True)
            last.then_inc(co_done, 1)

            MAPS = [(qT, kwT, vw, h, h // 4) for h in range(HN)] + [(qT, ksT, vs, h, h // 4) for h in range(HN)] \
                + [(fqT, fkT, fv, h, h) for h in range(HF)]

            def scores(m):
                q, k, _, h, g = MAPS[m]
                if m >= 2:
                    pe.wait_ge(s_max, m - 1)
                mm(S[m % 2][:, 0:P], q[:, h, 0:P], k[:, g, 0:P], start=True, stop=True)
                mm(S[m % 2][:, P:384], q[:, h, P:T], k[:, g, :], start=True, stop=True).then_inc(s_done, 1)

            def turn_p(m):
                pe.wait_ge(p_made, m + 1)
                if m >= 2:
                    pe.wait_ge(pT_made, m - 1)
                for j in range(3):
                    last = nc.tensor.transpose(TB[m % 2][:, P * j:P * j + P], pr[m % 2][:, P * j:P * j + P], ident[:, :])
                last.then_inc(p_turned, 1)

            def values(m):
                _, _, v, h, g = MAPS[m]
                pe.wait_ge(pT_made, m + 1)
                if h == 0:
                    if m == 0:
                        pe.wait_ge(co_kept, 1)
                    else:
                        pe.wait_ge(o_kept, m // 8)
                pt, c = prT[m % 2], DH * h
                mm(OB[0][:, c:c + DH], pt[:, 0:P], v[:, 0, g, :], start=True, stop=True)
                mm(OB[1][:, c:c + DH], pt[:, P:2 * P], v[:, 0, g, :], start=True, stop=False)
                last = mm(OB[1][:, c:c + DH], pt[:, 2 * P:384], v[:, 1, g, :], start=False, stop=True)
                if h == 7:
                    last.then_inc(o_done, 1)

            def merge(c):
                name = f"merge{c // 4}"
                if c >= 2:
                    pe.wait_ge(merge_made, c - 1)
                wait_block(pe, name)
                for k in range(KD):
                    last = mm(PJ[c % 2][:, 0:T], view[name][:, k, P * (c % 4):P * (c % 4) + P], hT[:, k, :],
                              start=(k == 0), stop=(k == KD - 1))
                last.then_inc(merge_done, 1)
            pe.wait_ge(kept_a, 7)
            pe.wait_ge(kept_v, 7)
            pe.wait_ge(proj_read_a, 12)
            for m in range(26):
                if m < 24:
                    scores(m)
                if m in MERGE_AT:
                    merge(MERGE_AT[m])
                if 1 <= m <= 24:
                    turn_p(m - 1)
                if m >= 2:
                    values(m - 2)
            pe.wait_ge(s_max, 24)
            pe.wait_ge(pT_made, 24)
            for mix in range(2):
                pe.wait_ge(o_kept, (2, 3)[mix])
                for j in range(2):
                    for k in range(2):
                        for t in range(NT):
                            c = P * (2 * j + k)
                            last = nc.tensor.transpose((S, TB)[mix][j][:, 256 * k + P * t:256 * k + P * t + P],
                                                       (o_nsa, o_fox)[mix][:, t, c:c + P], ident[:, :])
                    last.then_inc(o_turned, 1)
            pe.wait_ge(oT_made, 4)
            pe.wait_ge(merge_made, 16)
            for c in range(KD):
                if c >= 2:
                    pe.wait_ge(y_made, c - 1)
                for mix, name in enumerate(("up_nsa", "up_fox")):
                    wait_block(pe, name)
                    for k in range(4):
                        last = mm(PJ[c % 2][:, T * mix:T * mix + T], view[name][:, k, P * c:P * c + P], oT[mix][:, k, :],
                                  start=(k == 0), stop=(k == 3))
                last.then_inc(up_done, 1)
            pe.wait_ge(y_made, KD)
            turned_banks = [PJ[0], PJ[1], OB[0], OB[1]]
            for half in range(2):
                wait_block(pe, f"out{half}")
                for t in range(NT):
                    for h in range(2):
                        for k in range(4):
                            kk = 4 * half + k
                            last = mm((S, TB)[t][h][:, :], yT[:, kk, P * t:P * t + P], view[f"out{half}"][:, k, 512 * h:512 * h + 512],
                                      start=(kk == 0), stop=(kk == KD - 1))
                        if half == 1 and t == 1 and h == 0:
                            pe.wait_ge(summed, 1)
                            turn_rows(x, 0, turned_banks)
                    last.then_inc(out_done, 1)

            def router(t):
                for k in range(KD):
                    last = mm(PJ[0][:, E * t:E * t + E], hT[:, k, P * t:P * t + P], w_r[:, k, :], start=(k == 0), stop=(k == KD - 1))
                last.then_inc(lg_done, 1)
            pe.wait_ge(hT_made, 6)
            router(0)
            pe.wait_ge(summed, 2)
            turn_rows(x, 1, turned_banks)
            pe.wait_ge(hT_made, 8)
            router(1)
            pe.wait_ge(sel_made, 1)
            mm(TB[1][:, 0:E], before[:, :], chosen[:, 0, :], start=True, stop=True)
            mm(TB[1][:, E:2 * E], ones[:, :], chosen[:, 0, :], start=True, stop=False)
            mm(TB[1][:, E:2 * E], before[:, :], chosen[:, 1, :], start=False, stop=True)
            mm(TB[1][:, 2 * E:3 * E], ones[:, :], chosen[:, 0, :], start=True, stop=False)
            mm(TB[1][:, 2 * E:3 * E], ones[:, :], chosen[:, 1, :], start=False, stop=True).then_inc(pos_done, 1)

            def gather(i):
                pe.wait_ge(hot_made, i + 1)
                for k in range(KD):
                    for t in range(NT):
                        last = mm(banks[0][:, C * k:C * k + C], xn[:, t, P * k:P * k + P], hot[:, t, :], start=(t == 0), stop=(t == NT - 1))
                last.then_inc(gathered, 1)

            def product(m, bank, lhs, base, u, halves=(0, 1)):
                biased = m != "down"
                for h in halves:
                    if h == 0 and biased:
                        for half in range(2):
                            mm(bank[C * half:C * half + C, :], e_sel, e_rows[:, (m == "up") * 1, 512 * half:512 * half + 512],
                               start=True, stop=False)
                    s, nth = ex_slot(u, m, h)
                    pe.wait_ge(ring_in[s], n_in[s] + 16 * nth + base * (16 * fills // STEPS))
                    w = ring[:, s, :].rearrange("p (k n) -> p k n", k=4)
                    for k in range(4):
                        kk = 4 * h + k
                        for half in range(2):
                            last = mm(bank[C * half:C * half + C, :], lhs(kk), w[:, k, 512 * half:512 * half + 512],
                                      start=(kk == 0 and not biased), stop=(kk == KD - 1))
                    last.then_inc((half_done, mat_done)[h][m], 1)

            def scatter(i):
                pe.wait_ge(y_kept, i + 1)
                pe.wait_ge(hotT_made, i + 1)
                for j in range(4):
                    t, h = j // 2, j % 2
                    if j >= 2:
                        pe.wait_ge(added, i * 2 + j - 1)
                    mm(bank67[:, j % 2, :], hotT[C * h:C * h + C, t, :], e_y[C * h:C * h + C, :], start=True, stop=True).then_inc(spread_done, 1)

            def x_of(kk):
                return e_x[:, kk, :]

            def h_of(kk):
                return e_hT[:, kk % 4, kk // 4, :]

            def expert(base, u, first=False):
                it = base + u
                pe.wait_ge(ex_made, it + 1)
                product("gate", banks[1], x_of, base, u, (0,))
                if not first:
                    if isinstance(it, int) and it == 1:
                        pe.wait_ge(bd_added, NT)
                    scatter(it - 1)
                product("gate", banks[1], x_of, base, u, (1,))
                product("up", banks[2], x_of, base, u)
                gather(it + 1)
                pe.wait_ge(hotw_made, it + 1)
                for t in range(NT):
                    last = nc.tensor.transpose(bank45[:, 1, P * t:P * t + P], hotw[:, t, :, :].rearrange("p u s -> p (u s)"), ident[:, :])
                last.then_inc(hotw_turned, 1)
                pe.wait_ge(eh_made, it + 1)
                for k in range(4):
                    last = nc.tensor.transpose(bank45[:, 0, P * k:P * k + P], e_h[:, P * k:P * k + P], ident[:, :])
                last.then_inc(eh_turned, 1)
                if first:
                    bias_rows()
                pe.wait_ge(ehT_made, it + 1)
                product("down", banks[3], h_of, base, u)

            def bias_rows():
                pe.wait_ge(combT_made, 1)
                pe.wait_ge(bdown_in, 16)
                for t in range(NT):
                    if t:
                        pe.wait_ge(bd_added, t)
                    for h in range(2):
                        last = mm(bank67[:, h, :], combT[:, t, :], b_down[:, 512 * h:512 * h + 512], start=True, stop=True)
                    last.then_inc(bd_done, 1)
            pe.wait_ge(xn_ready, 1)
            gather(0)
            pe.wait_ge(comb_made, 1)
            pe.wait_ge(route_made, 1)
            for t in range(NT):
                last = nc.tensor.transpose(bank45[0:E, 1, T + P * t:T + P * t + P], comb[:, t, :], ident[:, :])
            last.then_inc(comb_turned, 1)
            pe.wait_ge(ebias_in, 32)
            expert(0, 0, True)
            total = pe.value_load(total_i[0:1, 0:1], min_val=E, max_val=ROUNDS * E)
            last_step = pe.value_load(total_i[0:1, 1:2], min_val=E - 1, max_val=ROUNDS * E - 1)
            for u in range(1, STEPS):
                expert(0, u)
            with pe.Fori(STEPS, total, STEPS) as base:
                for u in range(STEPS):
                    expert(base, u)
            scatter(last_step)


_INS = ['x', 'g_attn', 'w_in', 'qn_nsa', 'kn_cmp', 'kn_sel', 'kn_win', 'pos_cmp_k', 'w_ck1', 'b_ck1', 'w_ck2', 'b_ck2',
        'pos_cmp_v', 'w_cv1', 'b_cv1', 'w_cv2', 'b_cv2', 'b_nsa_gate', 'qn_fox', 'kn_fox', 'b_forget', 'w_up_nsa',
        'w_up_fox', 'b_merge', 'w_out', 'g_mlp', 'w_router', 'b_router', 'w_e_gate', 'b_e_gate', 'w_e_up', 'b_e_up',
        'w_e_down', 'b_e_down']


def kernel(**inputs):
    import numpy as _np
    import concourse.bacc as _bacc
    from concourse import mybir as _mybir
    from concourse.bass_utils import run_bass_kernel_spmd as _run

    nc = _bacc.Bacc("TRN2", target_bir_lowering=False, num_devices=1)
    arrays, args = {}, {}
    for name in _INS:
        v = _np.ascontiguousarray(inputs[name])
        arrays[f"in_{name}_dram"] = v
        args[name] = nc.dram_tensor(f"in_{name}_dram", v.shape, _mybir.dt.from_np(v.dtype), kind="ExternalInput").ap()
    out = nc.dram_tensor("out_0_dram", inputs["x"].shape, _mybir.dt.float32, kind="ExternalOutput").ap()
    build(nc, args, out)
    r = _run(nc, [arrays], core_ids=[0])
    return r.results[0]["out_0_dram"]
```

```python
from contextlib import ExitStack

import concourse.bass as bass
from concourse import mybir

ALU = mybir.AluOpType
ACT = mybir.ActivationFunctionType
F32 = mybir.dt.float32
F32R = mybir.dt.float32r
I32 = mybir.dt.int32
AX = mybir.AxisListType

P = 128
T = 256
NT = T // P
D = 1024
KD = D // P
DH = 64
DE = DH + 1
HN = 8
G = 2
HF = 8
NC = 16
CMP_BLOCK, CMP_STRIDE = 32, 16
E = 32
C = 64
ROUNDS = T // C
TOPK = 4
EPS = 1e-6
NEG = -1e30
SCALE = DH ** -0.5
LIMIT, SWISH = 7.0, 1.702
RING = (3, 4, 5)
EX_ORDER = (7, 3, 6, 4, 5, 0, 1, 2)
EX_SLOTS = len(EX_ORDER)
IN_HEADS = EX_SLOTS
STEPS = 4
SLOPES = [2.0 ** (-8.0 * (h + 1) / HN) for h in range(HN)]

C_Q, C_KV = 0, 512
C_KW, C_GATE = 1024, 1280
C_FQ, C_FK, C_FV, C_FL, C_MERGE = 1304, 1816, 2328, 2840, 2848

R_GA, R_GM, R_PK, R_PV, R_BK1, R_BV1, R_BM = 0, 8, 16, 32, 48, 50, 52
R_QN, R_KC, R_KS, R_KW, R_QF, R_KF, R_ALL = 68, 69, 70, 71, 72, 73, 74
B_GATE, B_CK2, B_CV2, B_ROUTER, B_ALL = 0, 32, 96, 160, 192


def build(nc, a, out):
    with ExitStack() as ctx:
        def sb(name, shape, dt=F32):
            return ctx.enter_context(nc.sbuf_tensor(name, shape, dt))

        def sem(name):
            return ctx.enter_context(nc.semaphore(name))

        banks = [ctx.enter_context(nc.psum_tensor(f"bank{i}", [P, 512], F32)) for i in range(4)]
        bank45 = ctx.enter_context(nc.psum_tensor("bank45", [P, 2, 512], F32))
        bank67 = ctx.enter_context(nc.psum_tensor("bank67", [P, 2, 512], F32))
        PJ = [banks[0], banks[1]]
        S = [banks[2], banks[3]]
        TB = [bank45[:, 0, :], bank45[:, 1, :]]
        OB = [bank67[:, 0, :], bank67[:, 1, :]]

        with ExitStack() as parts:
            w_hi, w_lo = (parts.enter_context(nc.sbuf_tensor(n, [P, KD, 512], F32R)) for n in ("w_hi", "w_lo"))
            hT_hi, hT_lo = (parts.enter_context(nc.sbuf_tensor(n, [P, KD, T], F32R)) for n in ("hT_hi", "hT_lo"))
        ring = sb("ring", [P, EX_SLOTS, 4096])
        x = sb("x", [P, NT, D])
        with ExitStack() as parts:
            oT_hi = parts.enter_context(nc.sbuf_tensor("oT_hi", [P, 4, 2, T], F32R))
        xn = sb("xn", [P, NT, D])
        hT = sb("hT", [P, KD, T])
        rows = ring[:, 7, :]
        with ExitStack() as parts:
            oT_lo = parts.enter_context(nc.sbuf_tensor("oT_lo", [P, 4, 2, T], F32R))
        OT_PLACE = (0, 3, 1, 2)
        heads = sb("heads", [P, 7168])
        late = ring[:, 6, :]
        work = sb("work", [P, 2304])
        vrow = sb("vrow", [R_ALL, P])
        vcol = sb("vcol", [P, R_ALL])
        scaled = sb("scaled", [P, 18])
        brow = sb("brow", [1, B_ALL])
        w_c2 = sb("w_c2", [P, 2, 2, DH])
        w_r = sb("w_r", [P, KD, E])
        ident = sb("ident", [P, P])
        causal = sb("causal", [P, T])
        before = sb("before", [P, P])
        upto = sb("upto", [P, P])
        ones = sb("ones", [P, P])
        spread = sb("spread", [NC, P])
        own_head = sb("own_head", [P, HN])
        cmask = sb("cmask", [P, NT, NC])
        cneg = sb("cneg", [P, NT, NC])
        slot_no = sb("slot_no", [P, C])
        t_pos = sb("t_pos", [P, NT])
        small = sb("small", [P, 760])
        route = sb("route", [P, (ROUNDS * E + 1 + STEPS) * 4])
        in_tile = sb("in_tile", [P, NT * E])
        round_off = sb("round_off", [P, ROUNDS])
        total_i = sb("total_i", [1, 2], I32)

        def tok(off, n):
            return rows[:, off:off + NT * n * DE].rearrange("p (t h d) -> p t h d", t=NT, h=n)
        o = 0
        q_tok = tok(o, HN); o += NT * HN * DE
        ks_tok = tok(o, G); o += NT * G * DE
        kw_tok = tok(o, G); o += NT * G * DE
        fq_tok = tok(o, HF); o += NT * HF * DE
        fk_tok = tok(o, HF)
        o_nsa = rows[:, 0:1024].rearrange("p (t n) -> p t n", t=NT)
        o_fox = rows[:, 1024:2048].rearrange("p (t n) -> p t n", t=NT)
        xflat = xn[:, :, :].rearrange("p t n -> p (t n)")
        vs = xflat[:, 0:256].rearrange("p (t g d) -> p t g d", t=NT, g=G)
        vw = xflat[:, 256:512].rearrange("p (t g d) -> p t g d", t=NT, g=G)
        fv = xflat[:, 512:1536].rearrange("p (t h d) -> p t h d", t=NT, h=HF)
        kc_dup = xflat[:, 1536:2048].rearrange("p (t g u d) -> p t g u d", t=NT, g=G, u=2)
        vc_dup = late[:, 2048:2560].rearrange("p (t g u d) -> p t g u d", t=NT, g=G, u=2)
        v_block = late[:, 2560:3072].rearrange("p (h d) -> p h d", h=HN)
        mergeT = late[:, :].rearrange("p (c t) -> p c t", t=T)
        def feat(off, n):
            return heads[0:DE, off:off + n * T].rearrange("p (h t) -> p h t", t=T)
        qT, ksT, kwT = feat(0, HN), feat(2048, G), feat(2560, G)
        fqT, fkT = feat(3072, HF), feat(5120, HF)
        yT = heads[:, 4096:6144].rearrange("p (k t) -> p k t", t=T)
        yT_hi, yT_lo = hT_hi, hT_lo

        def hb(off, n=512):
            return heads[:, off:off + n]
        e_x = hb(2048).rearrange("p (k s) -> p k s", s=C)
        e_g, e_sig, e_u, e_h, e_y = (hb(2560 + 512 * i) for i in range(5))
        e_hT = hb(5120).rearrange("p (k h s) -> p k h s", h=2, s=C)
        b_down = heads[0:E, 6144:7168]
        e_rows = heads[0:E, 0:2048].rearrange("p (m n) -> p m n", m=2)
        sq = [work[:, 512 * i:512 * i + 512] for i in range(2)]
        blk = [work[:, 1024 + 512 * i:1536 + 512 * i].rearrange("p (m g i) -> p m g i", m=16, g=G) for i in range(2)]
        sm = [work[:, 384 * i:384 * i + 384] for i in range(2)]
        pr = [work[:, 768 + 384 * i:1152 + 384 * i] for i in range(2)]
        prT = [work[:, 1536 + 384 * i:1920 + 384 * i] for i in range(2)]

        cur = [0]
        def sm_(n, shape=None, **kw):
            v = small[:, cur[0]:cur[0] + n]
            cur[0] += n
            assert cur[0] <= 760
            return v.rearrange(shape, **kw) if shape else v
        ss = sm_(2); rr = sm_(2); minus_half = sm_(8)
        ssq = sm_(8); rrq = sm_(8)
        gates = sm_(64, "p (t n) -> p t n", t=NT)
        gate = sm_(48, "p (t n) -> p t n", t=NT)
        fa = sm_(16, "p (t h) -> p t h", t=NT); fb = sm_(16, "p (t h) -> p t h", t=NT)
        mx = sm_(4, "p (b t) -> p b t", t=NT); nmx = sm_(4, "p (b t) -> p b t", t=NT)
        sums = sm_(48, "p (n t) -> p n t", t=NT)
        rg = sm_(16, "p (t h) -> p t h", t=NT)
        csum = sm_(16); ck_ss = sm_(2); ck_r = sm_(2)
        lg = sm_(64, "p (t e) -> p t e", t=NT); top8 = sm_(16, "p (t e) -> p t e", t=NT)
        above = sm_(64, "p (t e) -> p t e", t=NT)
        tot = sm_(8)
        b_router = sm_(E)
        now = sm_(8)
        assert cur[0] <= 760
        hid = late[:, 3072:3200].rearrange("p (v c n) -> p v c n", v=2, c=2)
        hid_a, hid_b = late[:, 3200:3328], late[:, 3328:3456]
        ck65 = late[0:NC, 3456:3456 + G * DE].rearrange("p (g d) -> p g d", g=G)
        ck_sq = late[0:NC, 3600:3728]
        vc16 = late[0:NC, 3728:3856]
        kcT = late[0:DE, 3856:3888].rearrange("p (g c) -> p g c", g=G)
        cp = work[:, 1024:1280]
        cpT = work[:, 1280:1536].rearrange("p (t q) -> p t q", t=NT)
        tmp_br = xflat[:, 1536:2048]
        tmp_up = work[:, 0:T]
        equal = work[:, 256:320].rearrange("p (t e) -> p t e", t=NT)
        count = work[:, 320:384].rearrange("p (t e) -> p t e", t=NT)
        chosen = work[:, 384:448].rearrange("p (t e) -> p t e", t=NT)
        comb = work[:, 448:512].rearrange("p (t e) -> p t e", t=NT)
        hot = work[:, 512:640].rearrange("p (t s) -> p t s", t=NT)
        hotw = work[:, 640:896].rearrange("p (t u s) -> p t u s", t=NT, u=2)
        hotT = work[:, 896:1152].rearrange("p (t q) -> p t q", t=NT)
        combT = work[0:E, 1152:1408].rearrange("p (t q) -> p t q", t=NT)
        e_sel = work[0:E, 1408:1472]
        rv0 = route[:, 0:4]
        logits = work[:, 1472:1536].rearrange("p (t e) -> p t e", t=NT)

        x_in = [sem(f"x_in{t}") for t in range(NT)]
        vec_in, small_in, ebias_in, bdown_in, out_sent = map(sem, (
            "vec_in", "small_in", "ebias_in", "bdown_in", "out_sent"))
        ring_in = [sem(f"ring_in{i}") for i in range(EX_SLOTS)] + [sem("in_heads")]
        vrow_set, pool_step, consts_made = map(sem, ("vrow_set", "pool_step", "consts_made"))
        mean_made, inv_made = sem("mean_made"), sem("inv_made")
        v_step, a_step, v_loop_step = sem("vector_step"), sem("scalar_step"), sem("vector_loop_step")
        vec_turned, vec_kept = sem("vec_turned"), sem("vec_kept")
        xn_made, xn_turned, hT_made = sem("xn_made"), sem("xn_turned"), sem("hT_made")
        hT_hi_made, hT_lo_made = sem("hT_hi_made"), sem("hT_lo_made")
        hi_made, chunk_used = sem("hi_made"), sem("chunk_used")
        lo_made, lo_made_v = sem("low_made_by_gpsimd"), sem("low_made_by_vector")
        proj_done, proj_read_a, proj_read_v = sem("proj_done"), sem("proj_read_a"), sem("proj_read_v")
        gates_kept, gates_tanh, f_abs, f_exp, f_ln, f_neg = map(sem, (
            "gates_kept", "gates_tanh", "f_abs", "f_exp", "f_ln", "f_neg"))
        f_summed, f_placed = sem("f_summed"), sem("f_placed")
        kv_turned, blk_made, hid_done, hid_in, hid_tanh, hid_made, hid_rows, hid_turned = map(sem, (
            "kv_turned", "blk_made", "hid_done", "hid_in", "hid_tanh", "hid_made", "hid_rows", "hid_turned"))
        ck_done, ck_kept, ck_turned, ck_ready = map(sem, ("ck_done", "ck_kept", "ck_turned", "ck_ready"))
        turned, kept_a, kept_v = sem("turned"), sem("kept_a"), sem("kept_v")
        cs_done, cs_max, cs_exp, cp_made, cp_turned, cpT_made, co_done, co_kept = map(sem, (
            "cs_done", "cs_max", "cs_exp", "cp_made", "cp_turned", "cpT_made", "co_done", "co_kept"))
        s_done, s_max, p_made, p_turned, pT_made, o_done, o_kept = map(sem, (
            "s_done", "s_max", "p_made", "p_turned", "pT_made", "o_done", "o_kept"))
        merge_done, merge_made = sem("merge_done"), sem("merge_made")
        o_turned, oT_hi_made, oT_lo_made, up_done, y_made, yT_hi_made, yT_lo_made, out_used, out_done = map(sem, (
            "o_turned", "oT_hi_made", "oT_lo_made", "up_done", "y_made", "yT_hi_made", "yT_lo_made", "out_used",
            "out_done"))
        squared, xn_ready, summed, lg_moved, lg_exp, comb_made = map(sem, ("squared", "xn_ready", "summed", "lg_moved", "lg_exp", "comb_made"))
        lg_done, sel_made, pos_done, route_made, comb_turned, combT_made, bd_done, bd_added = map(sem, (
            "lg_done", "sel_made", "pos_done", "route_made", "comb_turned", "combT_made", "bd_done", "bd_added"))
        hot_made, gathered, ex_made = sem("hot_made"), sem("gathered"), sem("ex_made")
        hotw_made, hotw_turned, hotT_made = sem("hotw_made"), sem("hotw_turned"), sem("hotT_made")
        half_done = {m: sem(f"expert_{m}_half_done") for m in ("gate", "up", "down")}
        mat_done = {m: sem(f"expert_{m}_done") for m in ("gate", "up", "down")}
        g_made, sig_made, up_read, eh_made, eh_turned, ehT_made = map(sem, (
            "g_made", "sig_made", "up_read", "eh_made", "eh_turned", "ehT_made"))
        y_kept, spread_done, added, rows_added = map(sem, (
            "y_kept", "spread_done", "added", "rows_added"))

        def gain_of(r):
            return vcol[:, r:r + 1]
        UNITS = [(q_tok, qT, 2 * i, scaled[:, 16:17]) for i in range(4)] \
            + [(ks_tok, ksT, 0, gain_of(R_KS)), (kw_tok, kwT, 0, gain_of(R_KW))] \
            + [(fk_tok, fkT, 2 * i, gain_of(R_KF)) for i in range(4)] \
            + [(fq_tok, fqT, 2 * i, scaled[:, 17:18]) for i in range(4)]
        MERGE_AT = {m: i for i, m in enumerate(m for m in range(24) if m % 3 != 2)}
        INVERTED = [rr[:, 0:1], rr[:, 1:2]] + [rrq[:, 0:G]] * 4 + [rrq] * 5 + [ck_r[0:NC, :], rrq] \
            + [rr[:, 0:1], rr[:, 1:2]]
        N_INV = len(INVERTED)
        CHAIN = 3

        block = ctx.enter_context(nc.Block())

        w_in = a["w_in"][0].rearrange("(k p) n -> p k n", p=P)

        def in_cols(c0, n):
            return [(w_in[:, :, c0:c0 + n], 0, n)]
        BLOCKS = [
            ("kv", [(w_in[:, :, C_KV + c:C_KV + c + 256], c, 256) for c in (0, 256)], 8, 512),
            ("kw", in_cols(C_KW, 280) + [(w_in[:, :, C_FL:C_FL + 8], 280, 8)], 8, 288),
            ("q", in_cols(C_Q, 512), 8, 512),
            ("ck1", [(a["w_ck1"][0].rearrange("(m p) n -> p m n", p=P), 0, 256)], 16, 256),
            ("cv1", [(a["w_cv1"][0].rearrange("(m p) n -> p m n", p=P), 0, 256)], 16, 256),
            ("fk", in_cols(C_FK, 512), 8, 512),
            ("fq", in_cols(C_FQ, 512), 8, 512),
            ("fv", in_cols(C_FV, 512), 8, 512),
        ] + [(f"merge{i}", in_cols(C_MERGE + 512 * i, 512), 8, 512) for i in range(4)] + [
            ("up_nsa", [(a["w_up_nsa"][0].rearrange("(k p) n -> p k n", p=P), 0, 1024)], 4, 1024),
            ("up_fox", [(a["w_up_fox"][0].rearrange("(k p) n -> p k n", p=P), 0, 1024)], 4, 1024),
            ("out0", [(a["w_out"][0].rearrange("(k p) n -> p k n", p=P)[:, 0:4, :], 0, 1024)], 4, 1024),
            ("out1", [(a["w_out"][0].rearrange("(k p) n -> p k n", p=P)[:, 4:8, :], 0, 1024)], 4, 1024),
        ]
        in_ring = [b[0] for b in BLOCKS if b[0] != "cv1"]
        slot_of = {name: RING[i % len(RING)] for i, name in enumerate(in_ring)}
        slot_of["cv1"] = IN_HEADS
        view, arrives, n_in = {}, {}, [0] * (EX_SLOTS + 1)
        for name, pieces, k, n in BLOCKS:
            s = slot_of[name]
            place = heads if s == IN_HEADS else ring[:, s, :]
            view[name] = place[:, 0:k * n].rearrange("p (k n) -> p k n", k=k)
            n_in[s] += 16 * len(pieces)
            arrives[name] = (s, n_in[s])
        SPLIT = ["kv", "kw", "q", "fk", "fq", "fv"]
        N_SPLIT = KD * len(SPLIT)
        MERGE, UP, OUT, N_PIECES = N_SPLIT, N_SPLIT + 16, N_SPLIT + 16 + KD, N_SPLIT + 16 + 2 * KD

        def low_done(j):
            return (lo_made, j - N_SPLIT // 2)
        freed = {name: [(lo_made, KD // 2 * (b + 1)), (lo_made_v, KD // 2 * (b + 1))] for b, name in enumerate(SPLIT)}
        freed["ck1"] = [(hid_done, 1)]
        freed |= {f"merge{i}": [low_done(MERGE + 4 * i + 4)] for i in range(4)}
        freed |= {"up_nsa": [low_done(OUT)], "up_fox": [low_done(OUT)]}
        ex_freed = [(o_turned, 4), low_done(OUT), (y_made, KD), low_done(OUT + 4), low_done(OUT + KD)] + [(out_done, 2)] * 3

        def quarter(j):
            q = (j - N_SPLIT) % 4
            return slice(P * q, P * q + P)

        def split_piece(j):
            if j < MERGE:
                name, k = SPLIT[j // KD], j % KD
                n = view[name].shape[2]
                return [(view[name][:, k, :], (k, slice(0, n)))], [name]
            q = quarter(j)
            if j < UP:
                name, c = f"merge{(j - MERGE) // 4}", (j - MERGE) % 4
                return [(view[name][:, :, P * c:P * c + P], (slice(0, KD), q))], [name]
            if j < OUT:
                c = j - UP
                return [(view[name][:, :, P * c:P * c + P], (slice(4 * m, 4 * m + 4), q))
                        for m, name in enumerate(("up_nsa", "up_fox"))], ["up_nsa", "up_fox"]
            kk = j - OUT
            name = f"out{kk // 4}"
            return [(view[name][:, kk % 4, :].rearrange("p (a b) -> p a b", b=P), (slice(0, KD), q))], [name]

        def keep_low(eng, vec, j, made):
            eng.wait_ge(hi_made, j + 1)
            for w, (k, n) in split_piece(j)[0]:
                last = vec.tensor_tensor(w_lo[:, k, n], w, w_hi[:, k, n], ALU.subtract)
            last.then_inc(made, 1)

        def wait_block(eng, name):
            s, v = arrives[name]
            eng.wait_ge(ring_in[s], v)

        EX_BLOCKS = [(m, h) for m in ("gate", "up", "down") for h in range(2)]

        def ex_slot(u, m, h):
            j = len(EX_BLOCKS) * u + EX_BLOCKS.index((m, h))
            return EX_ORDER[j % EX_SLOTS], j // EX_SLOTS + 1
        fills = len(EX_BLOCKS) * STEPS // EX_SLOTS
        ex_src = {"gate": "w_e_gate", "up": "w_e_up", "down": "w_e_down"}

        def col(ap, n):
            return ap.unsqueeze(2).to_broadcast([ap.shape[0], ap.shape[1], n])

        @block.sync
        def _(sp):
            for t in range(NT):
                sp.dma_start(x[:, t, :], a["x"][0, P * t:P * t + P, :]).then_inc(x_in[t], 16)

            def load(name, pieces):
                for src, c0, w in pieces:
                    sp.dma_start(view[name][:, :, c0:c0 + w], src).then_inc(ring_in[slot_of[name]], 16)
            load("kv", BLOCKS[0][1][:1])
            sp.wait_ge(vrow_set, 1)
            for r0, nr, name in ((R_GA, 8, "g_attn"), (R_GM, 8, "g_mlp"), (R_BK1, 2, "b_ck1"), (R_BV1, 2, "b_cv1"),
                                 (R_BM, 16, "b_merge")):
                sp.dma_start(vrow[r0:r0 + nr, :], a[name][0].rearrange("(r n) -> r n", r=nr)).then_inc(vec_in, 16)
            load("kv", BLOCKS[0][1][1:])
            for r0, name in ((R_QN, "qn_nsa"), (R_KC, "kn_cmp"), (R_KS, "kn_sel"), (R_KW, "kn_win"),
                             (R_QF, "qn_fox"), (R_KF, "kn_fox")):
                sp.dma_start(vrow[r0:r0 + 1, 0:DH], a[name]).then_inc(vec_in, 16)
            for r0, name in ((R_PK, "pos_cmp_k"), (R_PV, "pos_cmp_v")):
                sp.dma_start(vrow[r0:r0 + 16, :], a[name][0].rearrange("(r u) d -> r (u d)", u=2)).then_inc(vec_in, 16)
            def expert_loads(base, u, first=0, end=len(EX_BLOCKS)):
                it = base + u
                if isinstance(it, int):
                    e, now, prev = it, it, it - 1
                else:
                    e = sp.snap(sp.to_reg(it & (E - 1)), min_val=0, max_val=E - 1)
                    now, prev = sp.to_reg(it), sp.to_reg(it - 1)
                for b in range(first, end):
                    m, h = EX_BLOCKS[b]
                    src = a[ex_src[m]][0, bass.ds(e, 1)] if not isinstance(e, int) else a[ex_src[m]][0, e:e + 1]
                    src = src.rearrange("o (k p) n -> p (o k) n", p=P)
                    s = ex_slot(u, m, h)[0]
                    sp.wait_ge(vrow_set, 1)
                    nth = len(EX_BLOCKS) * it + b if isinstance(it, int) else EX_SLOTS
                    if nth < EX_SLOTS:
                        sp.wait_ge(*ex_freed[nth])
                    else:
                        pm, ph = EX_BLOCKS[(b - EX_SLOTS) % len(EX_BLOCKS)]
                        sp.wait_ge((half_done, mat_done)[ph][pm], prev if b < 2 else now)
                    sp.dma_start(ring[:, s, :].rearrange("p (k n) -> p k n", k=4),
                                 src[:, 4 * h:4 * h + 4, :]).then_inc(ring_in[s], 16)
            for i, (name, pieces, k, n) in enumerate(BLOCKS):
                if name == "out1":
                    expert_loads(0, 0, 0, 1)
                if name == "cv1":
                    sp.wait_ge(squared, NT)
                elif in_ring.index(name) >= len(RING):
                    for user in freed[in_ring[in_ring.index(name) - len(RING)]]:
                        sp.wait_ge(*user)
                if i:
                    load(name, pieces)

            for u in range(STEPS):
                expert_loads(0, u, int(u == 0))
            with sp.Fori(STEPS, E, STEPS) as base:
                for u in range(STEPS):
                    expert_loads(base, u)
            sp.wait_ge(route_made, 1)
            total = sp.value_load(total_i[0:1, 0:1], min_val=E, max_val=ROUNDS * E)
            with sp.If(total > E):
                with sp.Fori(E, total, STEPS) as base:
                    for u in range(STEPS):
                        expert_loads(base, u)
            for t in range(NT):
                if t == 0:
                    sp.wait_ge(added, total + total)
                else:
                    sp.wait_ge(rows_added, total)
                sp.dma_start(out[0, P * t:P * t + P, :], x[:, t, :]).then_inc(out_sent, 16)
            sp.wait_ge(out_sent, 32)

        @block.gpsimd
        def _(pool):
            n = [0]

            def step(ins):
                n[0] += 1
                ins.then_inc(pool_step, 1)
                pool.wait_ge(pool_step, n[0])
            nc.gpsimd.memset(vrow[:, :], 1.0).then_inc(vrow_set, 1)
            step(nc.gpsimd.memset(minus_half, -0.5))
            step(nc.gpsimd.memset(ident[:, :], 0.0))
            nc.gpsimd.affine_select(out=ident[:, :], in_=ident[:, :], compare_op=ALU.not_equal, fill=1.0,
                                    base=0, pattern=[[-1, P]], channel_multiplier=1).then_inc(consts_made, 1)
            step(nc.gpsimd.memset(ones[:, :], 1.0))
            nc.gpsimd.affine_select(out=upto[:, :], in_=ones[:, :], compare_op=ALU.is_ge, fill=0.0,
                                    base=0, pattern=[[1, P]], channel_multiplier=-1)
            nc.gpsimd.affine_select(out=before[:, :], in_=ones[:, :], compare_op=ALU.is_gt, fill=0.0,
                                    base=0, pattern=[[1, P]], channel_multiplier=-1)
            step(nc.gpsimd.memset(causal[:, :], 0.0))
            nc.gpsimd.affine_select(out=causal[:, :], in_=causal[:, :], compare_op=ALU.is_ge, fill=NEG,
                                    base=P, pattern=[[-1, T]], channel_multiplier=1)
            nc.gpsimd.iota(t_pos[:, :], pattern=[[P, NT]], base=0, channel_multiplier=1,
                           allow_small_or_imprecise_dtypes=True)
            nc.gpsimd.iota(slot_no[:, :], pattern=[[1, C]], base=0, channel_multiplier=0,
                           allow_small_or_imprecise_dtypes=True)
            nc.gpsimd.iota(round_off[:, :], pattern=[[-C, ROUNDS]], base=-1, channel_multiplier=0,
                           allow_small_or_imprecise_dtypes=True)
            nc.gpsimd.memset(route[:, ROUNDS * E * 4:], 0.0)
            step(nc.gpsimd.memset(in_tile[:, :], 1.0))
            nc.gpsimd.memset(in_tile[:, E:E + 1], 0.0)
            step(nc.gpsimd.memset(cmask[:, :, :], 1.0))
            step(nc.gpsimd.affine_select(out=cmask[:, :, :], in_=cmask[:, :, :], compare_op=ALU.is_ge, fill=0.0,
                                         base=1 - CMP_BLOCK, pattern=[[P, NT], [-CMP_STRIDE, NC]], channel_multiplier=1))
            nc.gpsimd.tensor_scalar(cneg[:, :, :], cmask[:, :, :], -1.0, -NEG, ALU.add, ALU.mult)
            step(nc.gpsimd.memset(spread[:, :], 0.0))
            nc.gpsimd.affine_select(out=spread[:, :].rearrange("p (h c) -> p h c", h=HN),
                                    in_=spread[:, :].rearrange("p (h c) -> p h c", h=HN),
                                    compare_op=ALU.not_equal, fill=1.0, base=0,
                                    pattern=[[0, HN], [-1, NC]], channel_multiplier=1)
            step(nc.gpsimd.memset(own_head[:, :], 1.0))
            step(nc.gpsimd.affine_select(out=own_head[:, :], in_=own_head[:, :], compare_op=ALU.is_ge, fill=0.0,
                                         base=0, pattern=[[-NC, HN]], channel_multiplier=1))
            nc.gpsimd.affine_select(out=own_head[:, :], in_=own_head[:, :], compare_op=ALU.is_ge, fill=0.0,
                                    base=NC - 1, pattern=[[NC, HN]], channel_multiplier=-1)
            nc.gpsimd.memset(blk[0], 0.0)
            nc.gpsimd.memset(blk[1], 0.0)
            for h in range(HN):
                nc.gpsimd.memset(q_tok[:, :, h, DH:DE], SLOPES[h] / SCALE)
            nc.gpsimd.memset(fq_tok[:, :, :, DH:DE], 1.0 / SCALE)
            for g in range(G):
                nc.gpsimd.iota(ck65[:, g, DH:DE], pattern=[[0, 1]], base=CMP_BLOCK - 1, channel_multiplier=CMP_STRIDE,
                               allow_small_or_imprecise_dtypes=True)
            for g in range(G):
                nc.gpsimd.iota(ks_tok[:, :, g, DH:DE], pattern=[[P, NT], [0, 1]], base=0, channel_multiplier=1,
                               allow_small_or_imprecise_dtypes=True)
                last = nc.gpsimd.iota(kw_tok[:, :, g, DH:DE], pattern=[[P, NT], [0, 1]], base=0, channel_multiplier=1,
                                      allow_small_or_imprecise_dtypes=True)
            last.then_inc(consts_made, 1)
            turn = [0]

            def invert():
                r = INVERTED[turn[0]]
                turn[0] += 1
                pool.wait_ge(mean_made, turn[0])
                nc.gpsimd.tensor_tensor(r, r, minus_half[0:r.shape[0], 0:r.shape[1]], ALU.pow).then_inc(inv_made, 1)

            for t in range(NT):
                invert()
            for j in range(0, N_SPLIT, 2):
                b, k = j // KD, j % KD
                if b >= 1 and k == 0:
                    invert()
                if b == 5 and k == 0:
                    invert()
                keep_low(pool, nc.gpsimd, j, lo_made)
                if b >= 1 and k == 6:
                    invert()
            for j in range(N_SPLIT, N_PIECES):
                keep_low(pool, nc.gpsimd, j, lo_made)
            for t in range(NT):
                invert()

        @block.scalar
        def _(act):
            n = [0]

            def step(ins):
                n[0] += 1
                ins.then_inc(a_step, 1)
                act.wait_ge(a_step, n[0])
            for c0, w, name in ((B_GATE, 24, "b_nsa_gate"), (B_GATE + 24, 8, "b_forget"), (B_CK2, DH, "b_ck2"),
                                (B_CV2, DH, "b_cv2"), (B_ROUTER, E, "b_router")):
                act.dma_start(brow[:, c0:c0 + w], a[name]).then_inc(small_in, 16)
            act.dma_start(w_c2[:, 0, :, :], a["w_ck2"][0].rearrange("(c p) n -> p c n", p=P)).then_inc(small_in, 16)
            act.dma_start(w_c2[:, 1, :, :], a["w_cv2"][0].rearrange("(c p) n -> p c n", p=P)).then_inc(small_in, 16)
            act.dma_start(w_r[:, :, :], a["w_router"][0].rearrange("(k p) n -> p k n", p=P)).then_inc(small_in, 16)

            def square_out(t):
                return heads[:, 2048 + D * t:2048 + D * t + D]

            def square_rows(t):
                nc.scalar.activation(square_out(t), x[:, t, :],
                                     ACT.Square, accum_out=ss[:, t:t + 1]).then_inc(squared, 1)
            for t in range(NT):
                act.wait_ge(x_in[t], 16)
                square_rows(t)

            def keep_high(j):
                parts, names = split_piece(j)
                for name in names:
                    wait_block(act, name)
                for w, (k, n) in parts:
                    last = nc.scalar.activation(w_hi[:, k, n], w, ACT.Copy)
                last.then_inc(hi_made, 1)

            def keep_high_tile(t):
                for j in range(2):
                    act.wait_ge(hT_made, 2 * t + j + 1)
                    k, q = slice(4 * j, 4 * j + 4), slice(P * t, P * t + P)
                    nc.scalar.activation(hT_hi[:, k, q], hT[:, k, q], ACT.Copy).then_inc(hT_hi_made, 1)
            for k in range(4):
                keep_high(k)
            keep_high_tile(0)
            for k in range(4, KD):
                keep_high(k)
            keep_high_tile(1)

            def two(ap):
                return ap.unsqueeze(2).to_broadcast([P, G, 2, DH])
            for i in range(12):
                b, t, ps = i // 2, i % 2, PJ[i % 2]
                if t == 1 and b < 5:
                    for k in range(KD):
                        if k < KD - 1:
                            act.wait_ge(chunk_used, (KD - 1) * b + k + 1)
                        else:
                            act.wait_ge(proj_done, i + 1)
                        keep_high(KD * (b + 1) + k)
                act.wait_ge(proj_done, i + 1)
                dve_before = i if i < 10 else 10
                if i >= 2 and b < 5:
                    act.wait_ge(proj_read_v, dve_before - 1)
                if b == 0:
                    if t == 0:
                        act.wait_ge(xn_turned, 4)
                    kv = ps[:, :].rearrange("p (j g d) -> p j g d", j=4, g=G)
                    nc.scalar.activation(kc_dup[:, t], two(kv[:, 0]), ACT.Copy)
                    nc.scalar.activation(vc_dup[:, t], two(kv[:, 1]), ACT.Copy)
                    nc.scalar.activation(vs[:, t], kv[:, 3], ACT.Copy)
                    nc.scalar.activation(sq[i % 2][:, 0:P], ps[:, 256:384], ACT.Square).then_inc(proj_read_a, 1)
                elif b == 1:
                    nc.scalar.activation(vw[:, t], ps[:, 128:256].rearrange("p (g d) -> p g d", g=G), ACT.Copy)
                    nc.scalar.activation(gates[:, t], ps[:, 256:288], ACT.Copy).then_inc(gates_kept, 1)
                    nc.scalar.activation(sq[i % 2][:, 0:P], ps[:, 0:128], ACT.Square).then_inc(proj_read_a, 1)
                    if t == 1:
                        act.wait_ge(gates_kept, 2)
                        nc.scalar.activation(gate[:, :, :], gates[:, :, 0:24], ACT.Tanh, scale=0.5).then_inc(gates_tanh, 1)
                        nc.scalar.activation(fa[:, :, :], gates[:, :, 24:32], ACT.Abs).then_inc(f_abs, 1)
                        act.wait_ge(f_abs, 1)
                        nc.scalar.activation(fb[:, :, :], fa[:, :, :], ACT.Exp, scale=-1.0).then_inc(f_exp, 1)
                        act.wait_ge(f_exp, 1)
                        nc.scalar.activation(fa[:, :, :], fb[:, :, :], ACT.Ln, bias=1.0).then_inc(f_ln, 1)
                elif b == 5:
                    nc.scalar.activation(fv[:, t], ps[:, :].rearrange("p (h d) -> p h d", h=HF), ACT.Copy).then_inc(proj_read_a, 1)
                else:
                    nc.scalar.activation(sq[i % 2], ps[:, :], ACT.Square).then_inc(proj_read_a, 1)
                if i == 7:
                    act.wait_ge(hid_in, 1)
                    nc.scalar.activation(hid_b, hid_b, ACT.Tanh, scale=0.7978845608028654).then_inc(hid_tanh, 1)
            for u in range(0, len(UNITS), 2):
                src, dst, h0, gain = UNITS[u]
                act.wait_ge(turned, u + 1)
                nc.scalar.activation(dst[:, h0:h0 + 2, :], TB[0][0:DE, :].rearrange("p (h t) -> p h t", h=2), ACT.Copy,
                                     scale=gain[0:DE, :]).then_inc(kept_a, 1)
                if u in (6, 8, 10):
                    keep_high(MERGE + (u - 6) // 2)
                if u == 4:
                    act.wait_ge(cs_max, 1)
                    nc.scalar.activation(cp, cp, ACT.Exp).then_inc(cs_exp, 1)
            for m in range(24):
                act.wait_ge(s_max, m + 1)
                if m >= 2:
                    act.wait_ge(p_turned, m - 1)
                nc.scalar.activation(pr[m % 2][:, 0:P], sm[m % 2][:, 0:P], ACT.Exp, bias=nmx[:, m % 2, 0:1],
                                     accum_out=sums[:, m, 0:1])
                nc.scalar.activation(pr[m % 2][:, P:384], sm[m % 2][:, P:384], ACT.Exp, bias=nmx[:, m % 2, 1:2],
                                     accum_out=sums[:, m, 1:2]).then_inc(p_made, 1)
                if m in MERGE_AT:
                    c = MERGE_AT[m]
                    act.wait_ge(merge_done, c + 1)
                    nc.scalar.activation(mergeT[:, c, :], PJ[c % 2][:, 0:T], ACT.Tanh, scale=0.5,
                                         bias=scaled[:, c:c + 1]).then_inc(merge_made, 1)
                    keep_high(MERGE + c + 3)
            for mix in range(2):
                for j in range(2):
                    act.wait_ge(o_turned, 2 * mix + j + 1)
                    nc.scalar.activation(oT_hi[:, OT_PLACE[2 * mix + j]], (S, TB)[mix][j][:, :].rearrange("p (k t) -> p k t", k=2),
                                         ACT.Copy).then_inc(oT_hi_made, 1)
                if mix == 0:
                    act.wait_ge(o_done, 3)
                    act.dma_start(b_down, a["b_e_down"][0]).then_inc(bdown_in, 16)
            for c in range(KD):
                if c:
                    act.wait_ge(up_done, c)
                keep_high(UP + c + 3)
                act.wait_ge(y_made, c + 1)
                nc.scalar.activation(yT_hi[:, c, :], yT[:, c, :], ACT.Copy).then_inc(yT_hi_made, 1)
            for kk in range(3, KD):
                if kk == 3:
                    act.wait_ge(up_done, KD)
                    act.dma_start(e_rows[:, 0, :], a["b_e_gate"][0]).then_inc(ebias_in, 16)
                    act.dma_start(e_rows[:, 1, :], a["b_e_up"][0]).then_inc(ebias_in, 16)
                else:
                    act.wait_ge(out_used, kk - 3)
                keep_high(OUT + kk)
            for t in range(NT):
                act.wait_ge(summed, t + 1)
                square_rows(t)
            for t in range(NT):
                act.wait_ge(inv_made, N_INV - NT + t + 1)
                last = nc.scalar.activation(xn[:, t, :], x[:, t, :], ACT.Copy, scale=rr[:, t:t + 1])
            last.then_inc(xn_ready, 1)
            act.wait_ge(lg_moved, 1)
            nc.scalar.activation(lg[:, :, :], lg[:, :, :], ACT.Exp).then_inc(lg_exp, 1)

            def keep_y(done):
                act.wait_ge(mat_done["down"], done)
                nc.scalar.activation(e_y, banks[3][:, :], ACT.Copy).then_inc(y_kept, 1)

            def expert(it, first):
                if not first:
                    keep_y(it)
                act.wait_ge(g_made, it + 1)
                nc.scalar.activation(e_sig, e_g, ACT.Sigmoid, scale=SWISH).then_inc(sig_made, 1)
                act.wait_ge(hotw_turned, it + 1)
                nc.scalar.activation(hotT, bank45[:, 1, 0:T].rearrange("p (t q) -> p t q", t=NT), ACT.Copy).then_inc(hotT_made, 1)
            expert(0, True)
            act.wait_ge(route_made, 1)
            total = act.value_load(total_i[0:1, 0:1], min_val=E, max_val=ROUNDS * E)
            for u in range(1, STEPS):
                expert(u, False)
            with act.Fori(STEPS, total, STEPS) as base:
                for u in range(STEPS):
                    expert(base + u, False)
            keep_y(total)

        @block.vector
        def _(dve):
            n = [0]

            def step(ins):
                n[0] += 1
                ins.then_inc(v_step, 1)
                dve.wait_ge(v_step, n[0])

            n_inv = [0]

            def inv_rms(dst, src, width):
                nc.vector.tensor_scalar(dst, src, 1.0 / width, EPS, ALU.mult, ALU.add).then_inc(mean_made, 1)
                n_inv[0] += 1
                dve.wait_ge(inv_made, n_inv[0])

            def norm_row_tile(t, made):
                inv_rms(rr[:, t:t + 1], ss[:, t:t + 1], D)
                nc.vector.tensor_scalar(xn[:, t, :], x[:, t, :], rr[:, t:t + 1], None, ALU.mult).then_inc(made, 1)

            def keep_hT_tile(gain_col, bank_list, base, t):
                for j in range(2):
                    dve.wait_ge(xn_turned, base + 2 * t + j + 1)
                    nc.vector.tensor_tensor(hT[:, 4 * j:4 * j + 4, P * t:P * t + P],
                                            bank_list[2 * t + j][:, :].rearrange("p (k q) -> p k q", k=4),
                                            col(vcol[:, gain_col + 4 * j:gain_col + 4 * j + 4], P), ALU.mult).then_inc(hT_made, 1)

            for t in range(NT):
                dve.wait_ge(squared, t + 1)
                norm_row_tile(t, xn_made)
            dve.wait_ge(vec_turned, 1)
            step(nc.vector.tensor_copy(vcol[:, :], TB[0][:, 0:R_ALL]))
            nc.vector.tensor_scalar(scaled[:, 0:16], vcol[:, R_BM:R_BM + 16], 0.5, None, ALU.mult)
            nc.vector.tensor_scalar(scaled[:, 16:17], vcol[:, R_QN:R_QN + 1], SCALE, None, ALU.mult)
            nc.vector.tensor_scalar(scaled[:, 17:18], vcol[:, R_QF:R_QF + 1], SCALE, None, ALU.mult).then_inc(vec_kept, 1)
            for t in range(NT):
                keep_hT_tile(R_GA, [PJ[0], PJ[1], S[0], S[1]], 0, t)

            def keep_low_tile(t):
                q = slice(P * t, P * t + P)
                dve.wait_ge(hT_made, 2 * t + 2)
                dve.wait_ge(hT_hi_made, 2 * t + 2)
                nc.vector.tensor_tensor(hT_lo[:, :, q], hT[:, :, q], hT_hi[:, :, q], ALU.subtract).then_inc(hT_lo_made, 1)

            def keep_low_chunks(b):
                for k in range(1, KD, 2):
                    keep_low(dve, nc.vector, KD * b + k, lo_made_v)
            keep_low_tile(0)
            keep_low_chunks(0)
            keep_low_tile(1)

            def head_norm(i, c0, n_heads, dst):
                ps = PJ[i % 2]
                dve.wait_ge(proj_read_a, i + 1)
                step(nc.vector.tensor_reduce(ssq[:, 0:n_heads], sq[i % 2][:, 0:n_heads * DH].rearrange("p (h d) -> p h d", d=DH),
                                             AX.X, ALU.add))
                inv_rms(rrq[:, 0:n_heads], ssq[:, 0:n_heads], DH)
                nc.vector.tensor_tensor(dst, ps[:, c0:c0 + n_heads * DH].rearrange("p (h d) -> p h d", d=DH),
                                        col(rrq[:, 0:n_heads], DH), ALU.mult).then_inc(proj_read_v, 1)
            for t in range(NT):
                head_norm(t, 256, G, ks_tok[:, t, :, 0:DH])
                if t == 0:
                    keep_low_chunks(1)
            head_norm(2, 0, G, kw_tok[:, 0, :, 0:DH])
            keep_low_chunks(2)
            dve.wait_ge(consts_made, 2)
            for v in range(2):
                dve.wait_ge(kv_turned, v + 1)
                tb = TB[v].rearrange("p (g t) -> p g t", g=G)
                for par in range(2):
                    lo = 64 * par
                    for half in range(2):
                        s0 = CMP_STRIDE * half
                        tv = tb[lo:lo + 64, :, s0:s0 + 240].rearrange("p g (i m u) -> p g i m u", m=8, u=2)[:, :, :, :, par]
                        pcol = vcol[lo:lo + 64, (R_PK, R_PV)[v] + 8 * half:(R_PK, R_PV)[v] + 8 * half + 8]
                        pcol = pcol.unsqueeze(1).unsqueeze(1).to_broadcast([64, G, NC - 1, 8])
                        dst = blk[v][lo:lo + 64, 8 * half:8 * half + 8, :, 0:NC - 1].rearrange("p m g i -> p g i m")
                        for g in range(G):
                            last = nc.vector.tensor_tensor(dst[:, g], tv[:, g], pcol[:, g], ALU.add)
                last.then_inc(blk_made, 1)
            head_norm(3, 0, G, kw_tok[:, 1, :, 0:DH])
            dve.wait_ge(gates_kept, 2)
            dve.wait_ge(gates_tanh, 1)
            dve.wait_ge(f_abs, 1)
            step(nc.vector.tensor_scalar(gate[:, :, :], gate[:, :, :], 1.0, 0.5, ALU.add, ALU.mult))
            step(nc.vector.tensor_scalar(gates[:, :, 24:32], gates[:, :, 24:32], 0.0, None, ALU.min))
            dve.wait_ge(f_ln, 1)
            nc.vector.tensor_tensor(fb[:, :, :], fa[:, :, :], gates[:, :, 24:32], ALU.subtract).then_inc(f_neg, 1)
            for t in range(NT):
                head_norm(4 + t, 0, HN, q_tok[:, t, :, 0:DH])
                if t == 0:
                    keep_low_chunks(3)
            dve.wait_ge(hid_done, 1)
            nc.vector.tensor_copy(hid_a, S[0][:, 0:P]).then_inc(hid_rows, 1)
            head_norm(6, 0, HF, fk_tok[:, 0, :, 0:DH])
            dve.wait_ge(hid_turned, 1)
            for v in range(2):
                for c in range(2):
                    r = (R_BK1, R_BV1)[v] + c
                    last = nc.vector.tensor_scalar(hid[:, v, c, :], S[0][:, P + 64 * v + 32 * c:P + 64 * v + 32 * c + 32],
                                                   vcol[:, r:r + 1], None, ALU.add)
            step(last)
            hflat = late[:, 3072:3200]
            step(nc.vector.tensor_tensor(hid_a, hflat, hflat, ALU.mult))
            step(nc.vector.tensor_scalar(hid_b, hid_a, 0.044715, 1.0, ALU.mult, ALU.add))
            nc.vector.tensor_tensor(hid_b, hid_b, hflat, ALU.mult).then_inc(hid_in, 1)
            step(nc.vector.tensor_scalar(hid_a, hflat, 0.5, None, ALU.mult))
            keep_low_chunks(4)
            head_norm(7, 0, HF, fk_tok[:, 1, :, 0:DH])
            dve.wait_ge(hid_tanh, 1)
            nc.vector.scalar_tensor_tensor(out=hflat, in0=hid_b, scalar=1.0, in1=hid_a, op0=ALU.add, op1=ALU.mult).then_inc(hid_made, 1)
            dve.wait_ge(f_summed, 1)
            nc.vector.tensor_copy(b_router, OB[0][:, 32:64])
            nc.vector.tensor_copy(fk_tok[:, :, :, DH], OB[0][:, 0:16].rearrange("p (t h) -> p t h", t=NT)).then_inc(f_placed, 1)
            for t in range(NT):
                head_norm(8 + t, 0, HF, fq_tok[:, t, :, 0:DH])
                if t == 0:
                    dve.wait_ge(ck_done, 1)
                    step(nc.vector.tensor_copy(ck_sq, S[1][0:NC, 0:P]))
                    step(nc.vector.tensor_tensor(ck_sq, ck_sq, ck_sq, ALU.mult))
                    step(nc.vector.tensor_reduce(ck_ss[0:NC, :], ck_sq.rearrange("p (g d) -> p g d", g=G), AX.X, ALU.add))
                    inv_rms(ck_r[0:NC, :], ck_ss[0:NC, :], DH)
                    nc.vector.tensor_tensor(ck65[:, :, 0:DH], S[1][0:NC, 0:P].rearrange("p (g d) -> p g d", g=G),
                                            col(ck_r[0:NC, :], DH), ALU.mult)
                    nc.vector.tensor_copy(vc16, S[1][0:NC, P:2 * P]).then_inc(ck_kept, 1)
                    keep_low_chunks(5)
            dve.wait_ge(ck_turned, 1)
            nc.vector.tensor_scalar(kcT, OB[1][0:DE, 0:32].rearrange("p (g c) -> p g c", g=G),
                                    vcol[0:DE, R_KC:R_KC + 1], None, ALU.mult)
            for g in range(G):
                last = nc.vector.tensor_tensor(
                    v_block[:, 4 * g:4 * g + 4, :],
                    S[1][:, DH * g:DH * g + DH].unsqueeze(1).to_broadcast([P, 4, DH]),
                    col(own_head[:, 4 * g:4 * g + 4], DH), ALU.mult)
            last.then_inc(ck_ready, 1)

            def keep_unit(u):
                src, dst, h0, gain = UNITS[u]
                dve.wait_ge(turned, u + 1)
                nc.vector.tensor_scalar(dst[:, h0:h0 + 2, :], TB[1][0:DE, :].rearrange("p (h t) -> p h t", h=2),
                                        gain[0:DE, :], None, ALU.mult).then_inc(kept_v, 1)
            for u in (1, 3, 5):
                keep_unit(u)
            dve.wait_ge(cs_done, 1)
            c4 = cp.rearrange("p (t h c) -> p t h c", t=NT, h=HN)
            c3 = cp.rearrange("p (n c) -> p n c", c=NC)
            for t in range(NT):
                last = nc.vector.tensor_tensor(c4[:, t], S[0][:, P * t:P * t + P].rearrange("p (h c) -> p h c", h=HN),
                                               cneg[:, t, :].unsqueeze(1).to_broadcast([P, HN, NC]), ALU.add)
            step(last)
            step(nc.vector.tensor_reduce(csum, c3, AX.X, ALU.max))
            nc.vector.tensor_tensor(c3, c3, col(csum, NC), ALU.subtract).then_inc(cs_max, 1)
            keep_unit(7)
            dve.wait_ge(cs_exp, 1)
            for t in range(NT):
                last = nc.vector.tensor_tensor(c4[:, t], c4[:, t], cmask[:, t, :].unsqueeze(1).to_broadcast([P, HN, NC]), ALU.mult)
            step(last)
            step(nc.vector.tensor_reduce(csum, c3, AX.X, ALU.add))
            step(nc.vector.tensor_scalar(csum, csum, 1e-30, None, ALU.max))
            keep_unit(9)
            step(nc.vector.reciprocal(csum, csum))
            step(nc.vector.tensor_tensor(csum.rearrange("p (t h) -> p t h", t=NT), csum.rearrange("p (t h) -> p t h", t=NT),
                                         gate[:, :, 0:HN], ALU.mult))
            nc.vector.tensor_tensor(c3, c3, col(csum, NC), ALU.mult).then_inc(cp_made, 1)
            for u in (11, 13):
                keep_unit(u)
            dve.wait_ge(cp_turned, 1)
            nc.vector.tensor_copy(cpT, S[1][:, 0:T].rearrange("p (t q) -> p t q", t=NT)).then_inc(cpT_made, 1)
            dve.wait_ge(co_done, 1)
            nc.vector.tensor_copy(o_nsa[:, 0, :], OB[0])
            nc.vector.tensor_copy(o_nsa[:, 1, :], OB[1]).then_inc(co_kept, 1)

            def row_max(m):
                dve.wait_ge(s_done, m + 1)
                if m >= 2:
                    dve.wait_ge(p_made, m - 1)
                b = m % 2
                nc.vector.tensor_tensor_reduce(sm[b][:, 0:P], S[b][:, 0:P], causal[:, P:T], 1.0, NEG * 2,
                                               ALU.add, ALU.max, mx[:, b, 0:1])
                step(nc.vector.tensor_tensor_reduce(sm[b][:, P:384], S[b][:, P:384], causal[:, :], 1.0, NEG * 2,
                                                    ALU.add, ALU.max, mx[:, b, 1:2]))
                nc.vector.tensor_scalar(nmx[:, b, :], mx[:, b, :], -1.0, None, ALU.mult).then_inc(s_max, 1)

            def keep_pT(m):
                dve.wait_ge(p_turned, m + 1)
                nc.vector.tensor_copy(prT[m % 2], TB[m % 2][:, 0:384]).then_inc(pT_made, 1)

            def keep_o(br):
                dve.wait_ge(o_done, br + 1)
                dst = o_fox if br == 2 else o_nsa
                step(nc.vector.reciprocal(rg[:, :, :].rearrange("p t h -> p h t"), sums[:, 8 * br:8 * br + 8, :]))
                if br < 2:
                    g0 = (16, 8)[br]
                    step(nc.vector.tensor_tensor(rg[:, :, :], rg[:, :, :], gate[:, :, g0:g0 + 8], ALU.mult))
                for t in range(NT):
                    ob = OB[t].rearrange("p (h d) -> p h d", d=DH)
                    if br == 2:
                        last = nc.vector.tensor_tensor(dst[:, t, :].rearrange("p (h d) -> p h d", d=DH), ob, col(rg[:, t, :], DH), ALU.mult)
                    else:
                        step(nc.vector.tensor_tensor(tmp_br.rearrange("p (h d) -> p h d", d=DH), ob, col(rg[:, t, :], DH), ALU.mult))
                        last = nc.vector.tensor_tensor(dst[:, t, :], dst[:, t, :], tmp_br, ALU.add)
                        if t == 0:
                            step(last)
                last.then_inc(o_kept, 1)

            def keep_low_o(mix):
                for j in range(2):
                    dve.wait_ge(o_turned, 2 * mix + j + 1)
                    dve.wait_ge(oT_hi_made, 2 * mix + j + 1)
                    i = OT_PLACE[2 * mix + j]
                    nc.vector.tensor_tensor(oT_lo[:, i], (S, TB)[mix][j][:, :].rearrange("p (k t) -> p k t", k=2),
                                            oT_hi[:, i], ALU.subtract).then_inc(oT_lo_made, 1)
            for m in range(26):
                if m < 24:
                    row_max(m)
                if 1 <= m <= 24:
                    keep_pT(m - 1)
                if m == 25:
                    keep_low_o(0)
                if m in (9, 17, 25):
                    keep_o((m - 9) // 8)
            keep_low_o(1)
            def keep_low_y(c):
                dve.wait_ge(yT_hi_made, c + 1)
                nc.vector.tensor_tensor(yT_lo[:, c, :], yT[:, c, :], yT_hi[:, c, :], ALU.subtract).then_inc(yT_lo_made, 1)
            dve.wait_ge(merge_made, 16)
            for c in range(KD):
                dve.wait_ge(up_done, c + 1)
                ps = PJ[c % 2]
                step(nc.vector.scalar_tensor_tensor(out=yT[:, c, :], in0=mergeT[:, c, :], scalar=1.0, in1=ps[:, 0:T],
                                                    op0=ALU.add, op1=ALU.mult))
                step(nc.vector.scalar_tensor_tensor(out=tmp_up, in0=mergeT[:, KD + c, :], scalar=1.0, in1=ps[:, T:2 * T],
                                                    op0=ALU.add, op1=ALU.mult))
                nc.vector.tensor_tensor(yT[:, c, :], yT[:, c, :], tmp_up, ALU.add).then_inc(y_made, 1)
                dve.wait_ge(y_made, c + 1)
                if c:
                    keep_low_y(c - 1)
            keep_low_y(KD - 1)
            for t in range(NT):
                dve.wait_ge(out_done, 1 + t)
                for h in range(2):
                    last = nc.vector.scalar_tensor_tensor(out=x[:, t, 512 * h:512 * h + 512], in0=(S, TB)[t][h][:, :], scalar=0.5,
                                                          in1=x[:, t, 512 * h:512 * h + 512], op0=ALU.mult, op1=ALU.add)
                last.then_inc(summed, 1)
                keep_hT_tile(R_GM, [PJ[0], PJ[1], OB[0], OB[1]], 4, t)
            for t in range(NT):
                dve.wait_ge(squared, NT + t + 1)
                inv_rms(rr[:, t:t + 1], ss[:, t:t + 1], D)

            dve.wait_ge(lg_done, 2)
            for t in range(NT):
                last = nc.vector.scalar_tensor_tensor(out=logits[:, t, :], in0=PJ[0][:, E * t:E * t + E], scalar=rr[:, t:t + 1],
                                                      in1=b_router, op0=ALU.mult, op1=ALU.add)
            step(last)
            for t in range(NT):
                last = nc.vector.max(top8[:, t, :], logits[:, t, :])
            step(last)
            fourth = top8[:, :, TOPK - 1:TOPK].to_broadcast([P, NT, E])
            nc.vector.tensor_tensor(equal, logits, fourth, ALU.is_equal)
            step(nc.vector.tensor_tensor(above[:, :, :], logits, fourth, ALU.is_gt))
            nc.vector.tensor_tensor(lg[:, :, :], logits, top8[:, :, 0:1].to_broadcast([P, NT, E]), ALU.subtract).then_inc(lg_moved, 1)
            step(nc.vector.tensor_reduce(tot[:, 0:2], above[:, :, :], AX.X, ALU.add))
            nc.vector.tensor_scalar(tot[:, 2:4], tot[:, 0:2], -1.0, float(TOPK), ALU.mult, ALU.add)
            step(nc.vector.tensor_tensor_scan(work[:, 320:384], in_tile[:, :], work[:, 256:320], 0.0, ALU.mult, ALU.add))
            step(nc.vector.tensor_tensor(count, count, col(tot[:, 2:4], E), ALU.is_le))
            step(nc.vector.tensor_tensor(count, count, equal, ALU.mult))
            nc.vector.tensor_tensor(chosen, above[:, :, :], count, ALU.add).then_inc(sel_made, 1)
            dve.wait_ge(sel_made, 1)
            dve.wait_ge(lg_exp, 1)
            step(nc.vector.tensor_tensor(comb, lg[:, :, :], chosen, ALU.mult))
            step(nc.vector.tensor_reduce(tot[:, 4:6], comb, AX.X, ALU.add))
            step(nc.vector.reciprocal(tot[:, 6:8], tot[:, 4:6]))
            nc.vector.tensor_tensor(comb, comb, col(tot[:, 6:8], E), ALU.mult).then_inc(comb_made, 1)
            dve.wait_ge(comb_made, 1)
            dve.wait_ge(pos_done, 1)
            for t in range(NT):
                last = nc.vector.scalar_tensor_tensor(out=above[:, t, :], in0=TB[1][:, E * t:E * t + E], scalar=1.0,
                                                      in1=chosen[:, t, :], op0=ALU.add, op1=ALU.mult)
            step(last)
            steps = ROUNDS * E
            rt = route[:, 0:steps * 4].rearrange("p (r e j) -> p r e j", r=ROUNDS, e=E)
            for t in range(NT):
                last = nc.vector.tensor_tensor(rt[:, :, :, t], above[:, t, :].unsqueeze(1).to_broadcast([P, ROUNDS, E]),
                                               col(round_off[:, :], E), ALU.add)
            step(last)
            for t in range(NT):
                last = nc.vector.tensor_scalar(hot[:, t, :], slot_no[:, :], rv0[:, t:t + 1], None, ALU.is_equal)
            last.then_inc(hot_made, 1)
            for t in range(NT):
                last = nc.vector.tensor_copy(rt[:, :, :, 2 + t], comb[:, t, :].unsqueeze(1).to_broadcast([P, ROUNDS, E]))
            step(last)
            step(nc.vector.tensor_reduce(tot[:, 0:1], TB[1][:, 2 * E:3 * E], AX.X, ALU.max))
            step(nc.vector.tensor_scalar(tot[:, 1:2], tot[:, 0:1], float(C), None, ALU.is_gt))
            for r in range(2, ROUNDS):
                step(nc.vector.scalar_tensor_tensor(out=tot[:, 1:2], in0=tot[:, 0:1], scalar=float(C * r), in1=tot[:, 1:2],
                                                    op0=ALU.is_gt, op1=ALU.add))
            step(nc.vector.tensor_scalar(tot[:, 2:3], tot[:, 1:2], float(E), float(E), ALU.mult, ALU.add))
            step(nc.vector.tensor_scalar(tot[:, 3:4], tot[:, 2:3], -1.0, None, ALU.add))
            nc.vector.tensor_copy(total_i[:, :], tot[0:1, 2:4]).then_inc(route_made, 1)
            step(nc.vector.tensor_copy(e_sel, ident[0:E, 0:1].to_broadcast([E, C])))
            def expert(it, first):
                k = [0]

                def chain(ins):
                    k[0] += 1
                    ins.then_inc(v_loop_step, 1)
                    dve.wait_ge(v_loop_step, it * CHAIN + k[0])
                e = it if isinstance(it, int) else it & (E - 1)
                rv = route[:, :].rearrange("p (s j) -> p s j", j=4)
                rcols = rv[:, it:it + 2, :] if isinstance(it, int) else rv[:, bass.ds(it, 2), :]
                chain(nc.vector.tensor_copy(now.rearrange("p (s j) -> p s j", j=4), rcols))
                dve.wait_ge(gathered, it + 1)
                for t in range(NT):
                    last = nc.vector.tensor_scalar(hot[:, t, :], slot_no[:, :], now[:, 4 + t:5 + t], None, ALU.is_equal)
                last.then_inc(hot_made, 1)
                if not first:
                    dve.wait_ge(hotw_turned, it)
                for t in range(NT):
                    last = nc.vector.tensor_scalar(hotw[:, t, :, :], slot_no[:, :].unsqueeze(1).to_broadcast([P, 2, C]),
                                                   now[:, t:t + 1], now[:, 2 + t:3 + t], ALU.is_equal, ALU.mult)
                last.then_inc(hotw_made, 1)
                if not first:
                    add_rows(it - 1)
                dve.wait_ge(mat_done["gate"], it + 1)
                nc.vector.tensor_scalar(e_g, banks[1][:, :], LIMIT, None, ALU.min).then_inc(g_made, 1)
                dve.wait_ge(mat_done["up"], it + 1)
                nc.vector.tensor_scalar(e_u, banks[2][:, :], LIMIT, -LIMIT, ALU.min, ALU.max).then_inc(up_read, 1)
                dve.wait_ge(up_read, it + 1)
                dve.wait_ge(g_made, it + 1)
                chain(nc.vector.scalar_tensor_tensor(out=e_u, in0=e_u, scalar=1.0, in1=e_g, op0=ALU.add, op1=ALU.mult))
                dve.wait_ge(sig_made, it + 1)
                nc.vector.tensor_tensor(e_h, e_u, e_sig, ALU.mult).then_inc(eh_made, 1)
                next_sel(it, chain)
                dve.wait_ge(eh_turned, it + 1)
                nc.vector.tensor_copy(e_hT, bank45[:, 0, :].rearrange("p (k h s) -> p k h s", h=2, s=C)).then_inc(ehT_made, 1)
                keep_x(it + 1)
                if isinstance(it, int) and it == 1:
                    add_biases()
                assert k[0] == CHAIN

            def next_sel(it, chain):
                e1 = (it + 1) & (E - 1)
                col_e = ident[0:E, e1:e1 + 1] if isinstance(e1, int) else ident[0:E, bass.ds(e1, 1)]
                chain(nc.vector.tensor_copy(e_sel, col_e.to_broadcast([E, C])))

            def keep_x(i):
                dve.wait_ge(gathered, i + 1)
                nc.vector.tensor_tensor(e_x, banks[0][:, :].rearrange("p (k s) -> p k s", s=C), col(vcol[:, R_GM:R_GM + KD], C), ALU.mult).then_inc(ex_made, 1)

            def add_biases():
                for t in range(NT):
                    dve.wait_ge(bd_done, t + 1)
                    for h in range(2):
                        last = nc.vector.tensor_tensor(x[:, t, 512 * h:512 * h + 512], x[:, t, 512 * h:512 * h + 512],
                                                       bank67[:, h, :], ALU.add)
                    last.then_inc(bd_added, 1)

            def add_rows(i):
                for j in range(4):
                    t, h = j // 2, j % 2
                    dve.wait_ge(spread_done, i * 4 + j + 1)
                    ins = nc.vector.tensor_tensor(x[:, t, 512 * h:512 * h + 512], x[:, t, 512 * h:512 * h + 512],
                                                  bank67[:, j % 2, :], ALU.add)
                    if j != 2:
                        ins.then_inc(rows_added if j == 3 else added, 1)
            dve.wait_ge(route_made, 1)
            total = dve.value_load(total_i[0:1, 0:1], min_val=E, max_val=ROUNDS * E)
            keep_x(0)
            dve.wait_ge(comb_turned, 1)
            nc.vector.tensor_copy(combT, bank45[0:E, 1, T:2 * T].rearrange("p (t q) -> p t q", t=NT)).then_inc(combT_made, 1)
            expert(0, True)
            for u in range(1, STEPS):
                expert(u, False)
            with dve.Fori(STEPS, total, STEPS) as base:
                for u in range(STEPS):
                    expert(base + u, False)
            add_rows(dve.value_load(total_i[0:1, 1:2], min_val=E - 1, max_val=ROUNDS * E - 1))

        @block.tensor
        def _(pe):
            mm = nc.tensor.matmul

            def turn_rows(src, t, bank_list):
                for j in range(2):
                    for k in range(4):
                        c = P * (4 * j + k)
                        last = nc.tensor.transpose(bank_list[2 * t + j][:, P * k:P * k + P], src[:, t, c:c + P], ident[:, :])
                    last.then_inc(xn_turned, 1)
            pe.wait_ge(consts_made, 1)
            pe.wait_ge(vec_in, 16 * 13)
            nc.tensor.transpose(TB[0][:, 0:R_ALL], vrow[:, :], ident[0:R_ALL, 0:R_ALL]).then_inc(vec_turned, 1)
            for t in range(NT):
                pe.wait_ge(xn_made, t + 1)
                turn_rows(xn, t, [PJ[0], PJ[1], S[0], S[1]])
            pe.wait_ge(consts_made, 2)
            def project(i, name, n):
                ps, t = PJ[i % 2], i % 2
                if i >= 2:
                    pe.wait_ge(proj_read_a, i - 1)
                    pe.wait_ge(proj_read_v, min(i - 1, 10))
                else:
                    pe.wait_ge(hT_lo_made, i + 1)
                b, q = i // 2, slice(P * t, P * t + P)
                if t == 0:
                    for k in range(KD):
                        pe.wait_ge(hi_made, KD * b + k + 1)
                        for h in (hT_hi, hT_lo):
                            mm(ps[:, 0:n], h[:, k, q], w_hi[:, k, 0:n], start=(k == 0 and h is hT_hi), stop=False)
                    for k in range(KD):
                        pe.wait_ge((lo_made, lo_made_v)[k % 2], KD // 2 * b + k // 2 + 1)
                        last = mm(ps[:, 0:n], hT_hi[:, k, q], w_lo[:, k, 0:n], start=False, stop=(k == KD - 1))
                else:
                    for k in range(KD):
                        mm(ps[:, 0:n], hT_hi[:, k, q], w_hi[:, k, 0:n], start=(k == 0), stop=False)
                        mm(ps[:, 0:n], hT_lo[:, k, q], w_hi[:, k, 0:n], start=False, stop=False)
                        last = mm(ps[:, 0:n], hT_hi[:, k, q], w_lo[:, k, 0:n], start=False, stop=(k == KD - 1))
                        if k < KD - 1:
                            last.then_inc(chunk_used, 1)
                if name == "kw":
                    pe.wait_ge(small_in, 16 * 8)
                    last = mm(ps[:, 256:288], ones[0:1, :], brow[:, 0:32], start=False, stop=True, skip_group_check=True)
                last.then_inc(proj_done, 1)

            project(0, "kv", 512)
            project(1, "kv", 512)
            project(2, "kw", 288)
            pe.wait_ge(vec_kept, 1)
            pe.wait_ge(proj_read_a, 2)
            for v in range(2):
                for g in range(G):
                    for t in range(NT):
                        last = nc.tensor.transpose(TB[v][:, 256 * g + P * t:256 * g + P * t + P],
                                                   (kc_dup, vc_dup)[v][:, t, g].rearrange("p u d -> p (u d)"), ident[:, :])
                last.then_inc(kv_turned, 1)
            project(3, "kw", 288)
            project(4, "q", 512)
            pe.wait_ge(blk_made, 2)
            wait_block(pe, "ck1")
            wait_block(pe, "cv1")
            for m in range(16):
                for v, name in enumerate(("ck1", "cv1")):
                    for c in range(2):
                        lo = 64 * v + 32 * c
                        last = mm(S[0][lo:lo + 32, 0:P], blk[v][:, m, :, :].rearrange("p g i -> p (g i)"),
                                  view[name][:, m, P * c:P * c + P], start=(m == 0), stop=(m == 15))
            last.then_inc(hid_done, 1)
            project(5, "q", 512)
            project(6, "fk", 512)
            pe.wait_ge(hid_rows, 1)
            nc.tensor.transpose(S[0][:, P:2 * P], hid_a, ident[:, :]).then_inc(hid_turned, 1)
            project(7, "fk", 512)
            pe.wait_ge(f_neg, 1)
            mm(OB[0][:, 32:64], ones[0:1, :], brow[:, B_ROUTER:B_ROUTER + E], start=True, stop=True)
            mm(OB[0][:, 0:8], upto[:, :], fb[:, 0, :], start=True, stop=True)
            mm(OB[0][:, 8:16], ones[:, :], fb[:, 0, :], start=True, stop=False)
            mm(OB[0][:, 8:16], upto[:, :], fb[:, 1, :], start=False, stop=True).then_inc(f_summed, 1)
            project(8, "fq", 512)
            pe.wait_ge(hid_made, 1)
            for v in range(2):
                for g in range(G):
                    c0 = P * v + DH * g
                    for c in range(2):
                        mm(S[1][0:NC, c0:c0 + DH], hid[:, v, c, NC * g:NC * g + NC], w_c2[:, v, c, :], start=(c == 0), stop=False)
                    b0 = (B_CK2, B_CV2)[v]
                    last = mm(S[1][0:NC, c0:c0 + DH], ones[0:1, 0:NC], brow[:, b0:b0 + DH], start=False, stop=True)
            last.then_inc(ck_done, 1)
            project(9, "fq", 512)
            project(10, "fv", 512)
            pe.wait_ge(ck_kept, 1)
            for g in range(G):
                nc.tensor.transpose(OB[1][0:DE, NC * g:NC * g + NC], ck65[:, g, :], ident[0:NC, 0:NC])
            mm(S[1][:, 0:P], spread[:, :], vc16, start=True, stop=True).then_inc(ck_turned, 1)
            project(11, "fv", 512)

            def turn_heads(u):
                src, dst, h0, gain = UNITS[u]
                if u >= 2:
                    pe.wait_ge((kept_a, kept_v)[u % 2], u // 2)
                for h in range(2):
                    for t in range(NT):
                        last = nc.tensor.transpose(TB[u % 2][0:DE, 256 * h + P * t:256 * h + P * t + P],
                                                   src[:, t, h0 + h, :], ident[:, :])
                last.then_inc(turned, 1)
            pe.wait_ge(blk_made, 2)
            pe.wait_ge(proj_read_v, 10)
            pe.wait_ge(f_placed, 1)
            for u in range(6):
                turn_heads(u)
            pe.wait_ge(ck_ready, 1)
            pe.wait_ge(kept_a, 2)
            pe.wait_ge(kept_v, 2)
            for t in range(NT):
                for h in range(HN):
                    last = mm(S[0][:, P * t + NC * h:P * t + NC * h + NC], qT[:, h, P * t:P * t + P], kcT[:, h // 4, :],
                              start=True, stop=True)
            last.then_inc(cs_done, 1)
            for u in range(6, len(UNITS)):
                turn_heads(u)
            pe.wait_ge(cp_made, 1)
            for t in range(NT):
                last = nc.tensor.transpose(S[1][:, P * t:P * t + P], cp[:, P * t:P * t + P], ident[:, :])
            last.then_inc(cp_turned, 1)
            pe.wait_ge(cpT_made, 1)
            for t in range(NT):
                last = mm(OB[t], cpT[:, t, :], v_block.rearrange("p h d -> p (h d)"), start=True, stop=True)
            last.then_inc(co_done, 1)

            MAPS = [(qT, kwT, vw, h, h // 4) for h in range(HN)] + [(qT, ksT, vs, h, h // 4) for h in range(HN)] \
                + [(fqT, fkT, fv, h, h) for h in range(HF)]

            def scores(m):
                q, k, _, h, g = MAPS[m]
                if m >= 2:
                    pe.wait_ge(s_max, m - 1)
                mm(S[m % 2][:, 0:P], q[:, h, 0:P], k[:, g, 0:P], start=True, stop=True)
                mm(S[m % 2][:, P:384], q[:, h, P:T], k[:, g, :], start=True, stop=True).then_inc(s_done, 1)

            def turn_p(m):
                pe.wait_ge(p_made, m + 1)
                if m >= 2:
                    pe.wait_ge(pT_made, m - 1)
                for j in range(3):
                    last = nc.tensor.transpose(TB[m % 2][:, P * j:P * j + P], pr[m % 2][:, P * j:P * j + P], ident[:, :])
                last.then_inc(p_turned, 1)

            def values(m):
                _, _, v, h, g = MAPS[m]
                pe.wait_ge(pT_made, m + 1)
                if h == 0:
                    if m == 0:
                        pe.wait_ge(co_kept, 1)
                    else:
                        pe.wait_ge(o_kept, m // 8)
                pt, c = prT[m % 2], DH * h
                mm(OB[0][:, c:c + DH], pt[:, 0:P], v[:, 0, g, :], start=True, stop=True)
                mm(OB[1][:, c:c + DH], pt[:, P:2 * P], v[:, 0, g, :], start=True, stop=False)
                last = mm(OB[1][:, c:c + DH], pt[:, 2 * P:384], v[:, 1, g, :], start=False, stop=True)
                if h == 7:
                    last.then_inc(o_done, 1)

            def merge(c):
                if c >= 2:
                    pe.wait_ge(merge_made, c - 1)
                pe.wait_ge(*low_done(MERGE + c + 1))
                w = quarter(MERGE + c)
                for k in range(KD):
                    mm(PJ[c % 2][:, 0:T], w_hi[:, k, w], hT_hi[:, k, :], start=(k == 0), stop=False)
                    mm(PJ[c % 2][:, 0:T], w_hi[:, k, w], hT_lo[:, k, :], start=False, stop=False)
                    last = mm(PJ[c % 2][:, 0:T], w_lo[:, k, w], hT_hi[:, k, :], start=False, stop=(k == KD - 1))
                last.then_inc(merge_done, 1)
            pe.wait_ge(kept_a, 7)
            pe.wait_ge(kept_v, 7)
            pe.wait_ge(proj_read_a, 12)

            def turn_outputs(mix):
                pe.wait_ge(o_kept, (2, 3)[mix])
                for j in range(2):
                    for k in range(2):
                        for t in range(NT):
                            c = P * (2 * j + k)
                            last = nc.tensor.transpose((S, TB)[mix][j][:, 256 * k + P * t:256 * k + P * t + P],
                                                       (o_nsa, o_fox)[mix][:, t, c:c + P], ident[:, :])
                    last.then_inc(o_turned, 1)

            def lift(c, mix):
                if mix == 0:
                    if c >= 2:
                        pe.wait_ge(y_made, c - 1)
                    pe.wait_ge(*low_done(UP + c + 1))
                if c == 0:
                    pe.wait_ge(oT_lo_made, 2 * mix + 2)
                w = quarter(UP + c)
                ps = PJ[c % 2][:, T * mix:T * mix + T]
                for k in range(4):
                    wk, o = 4 * mix + k, (OT_PLACE[2 * mix + k // 2], k % 2)
                    mm(ps, w_hi[:, wk, w], oT_hi[:, o[0], o[1]], start=(k == 0), stop=False)
                    mm(ps, w_hi[:, wk, w], oT_lo[:, o[0], o[1]], start=False, stop=False)
                    last = mm(ps, w_lo[:, wk, w], oT_hi[:, o[0], o[1]], start=False, stop=(k == 3))
                return last
            for m in range(26):
                if m < 24:
                    scores(m)
                if m == 24:
                    pe.wait_ge(s_max, 24)
                    turn_outputs(0)
                if m in MERGE_AT:
                    merge(MERGE_AT[m])
                if 1 <= m <= 24:
                    turn_p(m - 1)
                if m >= 2:
                    values(m - 2)
            pe.wait_ge(merge_made, 16)
            for c in range(2):
                lift(c, 0)
            pe.wait_ge(pT_made, 24)
            turn_outputs(1)
            for c in range(KD):
                if c >= 2:
                    lift(c, 0)
                lift(c, 1).then_inc(up_done, 1)
            turned_banks = [PJ[0], PJ[1], OB[0], OB[1]]

            def out_piece(kk, t):
                q, w = slice(P * t, P * t + P), quarter(OUT + kk)
                for h in range(2):
                    ps = (S, TB)[t][h][:, :].rearrange("p (a b) -> p a b", b=P)
                    hs = slice(4 * h, 4 * h + 4)
                    mm(ps, yT_hi[:, kk, q], w_hi[:, hs, w], start=(kk == 0), stop=False)
                    mm(ps, yT_lo[:, kk, q], w_hi[:, hs, w], start=False, stop=False)
                    last = mm(ps, yT_hi[:, kk, q], w_lo[:, hs, w], start=False, stop=(kk == KD - 1))
                return last
            for kk in range(4):
                pe.wait_ge(yT_lo_made, kk + 1)
                pe.wait_ge(*low_done(OUT + kk + 1))
                out_piece(kk, 0)
                out_piece(kk, 1).then_inc(out_used, 1)
            pe.wait_ge(yT_lo_made, KD)
            for t in range(NT):
                for kk in range(4, KD):
                    if t == 0:
                        pe.wait_ge(*low_done(OUT + kk + 1))
                    elif kk == KD - 1:
                        pe.wait_ge(summed, 1)
                        turn_rows(x, 0, turned_banks)
                    last = out_piece(kk, t)
                last.then_inc(out_done, 1)

            def router(t):
                for k in range(KD):
                    last = mm(PJ[0][:, E * t:E * t + E], hT[:, k, P * t:P * t + P], w_r[:, k, :], start=(k == 0), stop=(k == KD - 1))
                last.then_inc(lg_done, 1)
            pe.wait_ge(hT_made, 6)
            router(0)
            pe.wait_ge(summed, 2)
            turn_rows(x, 1, turned_banks)
            pe.wait_ge(hT_made, 8)
            router(1)
            def keep_warm(n):
                for _ in range(n):
                    mm(S[0][:, 0:P], ident[:, :], ones[:, :], start=True, stop=True)
            keep_warm(14)
            pe.wait_ge(sel_made, 1)
            mm(TB[1][:, 0:E], before[:, :], chosen[:, 0, :], start=True, stop=True)
            mm(TB[1][:, E:2 * E], ones[:, :], chosen[:, 0, :], start=True, stop=False)
            mm(TB[1][:, E:2 * E], before[:, :], chosen[:, 1, :], start=False, stop=True)
            mm(TB[1][:, 2 * E:3 * E], ones[:, :], chosen[:, 0, :], start=True, stop=False)
            mm(TB[1][:, 2 * E:3 * E], ones[:, :], chosen[:, 1, :], start=False, stop=True).then_inc(pos_done, 1)

            def gather(i):
                pe.wait_ge(hot_made, i + 1)
                for k in range(KD):
                    for t in range(NT):
                        last = mm(banks[0][:, C * k:C * k + C], xn[:, t, P * k:P * k + P], hot[:, t, :], start=(t == 0), stop=(t == NT - 1))
                last.then_inc(gathered, 1)

            def product(m, bank, lhs, base, u, halves=(0, 1)):
                biased = m != "down"
                for h in halves:
                    if h == 0 and biased:
                        for half in range(2):
                            mm(bank[C * half:C * half + C, :], e_sel, e_rows[:, (m == "up") * 1, 512 * half:512 * half + 512],
                               start=True, stop=False)
                    s, nth = ex_slot(u, m, h)
                    pe.wait_ge(ring_in[s], n_in[s] + 16 * nth + base * (16 * fills // STEPS))
                    w = ring[:, s, :].rearrange("p (k n) -> p k n", k=4)
                    for k in range(4):
                        kk = 4 * h + k
                        for half in range(2):
                            last = mm(bank[C * half:C * half + C, :], lhs(kk), w[:, k, 512 * half:512 * half + 512],
                                      start=(kk == 0 and not biased), stop=(kk == KD - 1))
                    last.then_inc((half_done, mat_done)[h][m], 1)

            def scatter(i):
                pe.wait_ge(y_kept, i + 1)
                pe.wait_ge(hotT_made, i + 1)
                for j in range(4):
                    t, h = j // 2, j % 2
                    if j >= 2:
                        pe.wait_ge(added, i * 2 + j - 1)
                    mm(bank67[:, j % 2, :], hotT[C * h:C * h + C, t, :], e_y[C * h:C * h + C, :], start=True, stop=True).then_inc(spread_done, 1)

            def x_of(kk):
                return e_x[:, kk, :]

            def h_of(kk):
                return e_hT[:, kk % 4, kk // 4, :]

            def expert(base, u, first=False):
                it = base + u
                pe.wait_ge(ex_made, it + 1)
                product("gate", banks[1], x_of, base, u, (0,))
                if not first:
                    if isinstance(it, int) and it == 2:
                        pe.wait_ge(bd_added, NT)
                    scatter(it - 1)
                product("gate", banks[1], x_of, base, u, (1,))
                product("up", banks[2], x_of, base, u)
                gather(it + 1)
                pe.wait_ge(hotw_made, it + 1)
                for t in range(NT):
                    last = nc.tensor.transpose(bank45[:, 1, P * t:P * t + P], hotw[:, t, :, :].rearrange("p u s -> p (u s)"), ident[:, :])
                last.then_inc(hotw_turned, 1)
                pe.wait_ge(eh_made, it + 1)
                for k in range(4):
                    last = nc.tensor.transpose(bank45[:, 0, P * k:P * k + P], e_h[:, P * k:P * k + P], ident[:, :])
                last.then_inc(eh_turned, 1)
                if isinstance(it, int) and it == 1:
                    bias_rows()
                pe.wait_ge(ehT_made, it + 1)
                product("down", banks[3], h_of, base, u)

            def bias_rows():
                pe.wait_ge(combT_made, 1)
                pe.wait_ge(bdown_in, 16)
                pe.wait_ge(rows_added, 1)
                for t in range(NT):
                    if t:
                        pe.wait_ge(bd_added, t)
                    for h in range(2):
                        last = mm(bank67[:, h, :], combT[:, t, :], b_down[:, 512 * h:512 * h + 512], start=True, stop=True)
                    last.then_inc(bd_done, 1)
            pe.wait_ge(xn_ready, 1)
            keep_warm(10)
            gather(0)
            pe.wait_ge(comb_made, 1)
            pe.wait_ge(route_made, 1)
            for t in range(NT):
                last = nc.tensor.transpose(bank45[0:E, 1, T + P * t:T + P * t + P], comb[:, t, :], ident[:, :])
            last.then_inc(comb_turned, 1)
            pe.wait_ge(ebias_in, 32)
            keep_warm(4)
            expert(0, 0, True)
            total = pe.value_load(total_i[0:1, 0:1], min_val=E, max_val=ROUNDS * E)
            last_step = pe.value_load(total_i[0:1, 1:2], min_val=E - 1, max_val=ROUNDS * E - 1)
            for u in range(1, STEPS):
                expert(0, u)
            with pe.Fori(STEPS, total, STEPS) as base:
                for u in range(STEPS):
                    expert(base, u)
            scatter(last_step)


_INS = ['x', 'g_attn', 'w_in', 'qn_nsa', 'kn_cmp', 'kn_sel', 'kn_win', 'pos_cmp_k', 'w_ck1', 'b_ck1', 'w_ck2', 'b_ck2',
        'pos_cmp_v', 'w_cv1', 'b_cv1', 'w_cv2', 'b_cv2', 'b_nsa_gate', 'qn_fox', 'kn_fox', 'b_forget', 'w_up_nsa',
        'w_up_fox', 'b_merge', 'w_out', 'g_mlp', 'w_router', 'b_router', 'w_e_gate', 'b_e_gate', 'w_e_up', 'b_e_up',
        'w_e_down', 'b_e_down']


def kernel(**inputs):
    import numpy as _np
    import concourse.bacc as _bacc
    from concourse import mybir as _mybir
    from concourse.bass_utils import run_bass_kernel_spmd as _run

    nc = _bacc.Bacc("TRN2", target_bir_lowering=False, num_devices=1)
    arrays, args = {}, {}
    for name in _INS:
        v = _np.ascontiguousarray(inputs[name])
        arrays[f"in_{name}_dram"] = v
        args[name] = nc.dram_tensor(f"in_{name}_dram", v.shape, _mybir.dt.from_np(v.dtype), kind="ExternalInput").ap()
    out = nc.dram_tensor("out_0_dram", inputs["x"].shape, _mybir.dt.float32, kind="ExternalOutput").ap()
    build(nc, args, out)
    r = _run(nc, [arrays], core_ids=[0])
    return r.results[0]["out_0_dram"]
```
